# Optimizing a Trainium2 kernel written in Bass

```python
import math
import jax, jax.numpy as jnp
from jax import lax
import numpy as np

D_MODEL = 2048
BATCH = 1
SEQ = 512
DEPTH = 1
DEC_BATCH = 8
DEC_SEQ = 4
PAST_LEN = 1024
PAGE_SIZE = 128

ATT_HEADS = 16
HEAD_DIM = D_MODEL // ATT_HEADS
KV_HEADS = 4
ATT_W = ATT_HEADS * HEAD_DIM
KV_W = KV_HEADS * HEAD_DIM
IDX_HEADS = 16
IDX_DIM = 64
IDX_SCALE = IDX_HEADS ** -0.5 * IDX_DIM ** -0.5
TOPK_MAX = 256
Q_BLOCK = 128
ROPE_THETA = 10000.0
D_INNER = 2 * D_MODEL
SSD_HEAD_DIM = 64
SSD_HEADS = D_INNER // SSD_HEAD_DIM
SSD_GROUPS = 8
D_STATE = 128
CONV_W = 4
CHUNK = 128
CONV_DIM = D_INNER + 2 * SSD_GROUPS * D_STATE
EPS = 1e-6

IN_SPLITS = (ATT_W, KV_W, KV_W, ATT_W, IDX_HEADS * IDX_DIM, IDX_DIM, IDX_HEADS, D_INNER, CONV_DIM, SSD_HEADS, D_MODEL, D_MODEL)
IN_W = sum(IN_SPLITS)
SPLIT_POINTS = tuple(int(s) for s in np.cumsum(IN_SPLITS)[:-1])
BRANCH_W = ATT_W + D_INNER

kernel_name = "dsa_ssd_parallel_gated_decoder_step"

def rmsnorm(x, g):
    xf = x.astype(jnp.float32)
    y = xf * lax.rsqrt(jnp.mean(xf * xf, axis=-1, keepdims=True) + EPS)
    return (y * g.astype(jnp.float32)).astype(x.dtype)

def layernorm(x, w, b):
    xf = x.astype(jnp.float32)
    mu = jnp.mean(xf, axis=-1, keepdims=True)
    xc = xf - mu
    y = xc * lax.rsqrt(jnp.mean(xc * xc, axis=-1, keepdims=True) + EPS)
    return (y * w.astype(jnp.float32) + b.astype(jnp.float32)).astype(x.dtype)

def group_rmsnorm(y, g):
    b, l, w = y.shape
    yg = y.reshape(b, l, SSD_GROUPS, w // SSD_GROUPS).astype(jnp.float32)
    yg = yg * lax.rsqrt(jnp.mean(yg * yg, axis=-1, keepdims=True) + EPS)
    return (yg.reshape(b, l, w) * g.astype(jnp.float32)).astype(y.dtype)

def rope(x, pos):
    d = x.shape[-1]
    inv = ROPE_THETA ** (-jnp.arange(0, d, 2, dtype=jnp.float32) / d)
    ang = pos.astype(jnp.float32)[:, None] * inv[None, :]
    cos = jnp.cos(ang)[:, None, :]
    sin = jnp.sin(ang)[:, None, :]
    x1, x2 = jnp.split(x.astype(jnp.float32), 2, axis=-1)
    return jnp.concatenate([x1 * cos - x2 * sin, x2 * cos + x1 * sin], axis=-1).astype(x.dtype)

def causal_conv(x, prefix, w, b):
    n = x.shape[1]
    xp = jnp.concatenate([prefix.astype(x.dtype), x], axis=1)
    acc = b
    for tap in range(CONV_W):
        acc = acc + xp[:, tap:tap + n] * w[tap]
    return jax.nn.silu(acc), xp[:, n:]

def gather_pages(pool, page_table):
    g = pool[page_table]
    return g.reshape(g.shape[0], g.shape[1] * g.shape[2], *g.shape[3:])

def dsa_attend(q, qi, wi, q_pos, k_all, v_all, ki_all, k_pos, top_k):
    b, t = q.shape[0], q.shape[1]
    causal = k_pos[None, :] <= q_pos[:, None]
    dots = jax.nn.relu(jnp.einsum("bthd,bsd->bths", qi, ki_all))
    score = jnp.einsum("bths,bth->bts", dots, wi).astype(jnp.float32)
    score = jnp.where(causal[None], score, -jnp.inf)
    top_vals, idx = lax.top_k(score, top_k)
    valid = jnp.isfinite(top_vals)
    k_sel = jax.vmap(lambda kk, ii: kk[ii])(k_all, idx)
    v_sel = jax.vmap(lambda vv, ii: vv[ii])(v_all, idx)
    qg = q.reshape(b, t, KV_HEADS, ATT_HEADS // KV_HEADS, HEAD_DIM)
    s = jnp.einsum("btgrd,btkgd->btgrk", qg, k_sel).astype(jnp.float32) * (HEAD_DIM ** -0.5)
    s = jnp.where(valid[:, :, None, None, :], s, -jnp.inf)
    p = jax.nn.softmax(s, axis=-1).astype(v_sel.dtype)
    o = jnp.einsum("btgrk,btkgd->btgrd", p, v_sel)
    return o.reshape(b, t, ATT_W)

def ssd_scan(x, dt, a, bm, cm, s0):
    b, l, h, p = x.shape
    g, n = bm.shape[2], bm.shape[3]
    r = h // g
    q = min(CHUNK, l)
    pad = (-l) % q
    if pad:
        padf = lambda t: jnp.pad(t, [(0, 0), (0, pad)] + [(0, 0)] * (t.ndim - 2))
        x, dt, bm, cm = padf(x), padf(dt), padf(bm), padf(cm)
    c = (l + pad) // q
    x = x.reshape(b, c, q, g, r, p)
    dt = dt.reshape(b, c, q, g, r)
    bc = bm.reshape(b, c, q, g, n)
    cc = cm.reshape(b, c, q, g, n)
    a_cs = jnp.cumsum(dt * a.reshape(g, r), axis=2)
    seg = a_cs[:, :, :, None] - a_cs[:, :, None, :]
    mask = jnp.tril(jnp.ones((q, q), dtype=bool))[None, None, :, :, None, None]
    lmat = jnp.where(mask, jnp.exp(jnp.where(mask, seg, 0.0)), 0.0)
    xdt = x * dt[..., None]
    cb = jnp.einsum("bcign,bcjgn->bcijg", cc, bc)
    y_diag = jnp.einsum("bcijg,bcijgr,bcjgrp->bcigrp", cb, lmat, xdt)
    decay_to_end = jnp.exp(a_cs[:, :, -1:] - a_cs)
    chunk_states = jnp.einsum("bcjgn,bcjgr,bcjgrp->bcgrpn", bc, decay_to_end, xdt)
    chunk_decay = jnp.exp(a_cs[:, :, -1])

    def step(s, inp):
        dec, st = inp
        return s * dec[..., None, None] + st, s

    s_final, s_prev = lax.scan(step, s0.reshape(b, g, r, p, n),
                               (jnp.moveaxis(chunk_decay, 1, 0), jnp.moveaxis(chunk_states, 1, 0)))
    s_prev = jnp.moveaxis(s_prev, 0, 1)
    y_off = jnp.einsum("bcign,bcigr,bcgrpn->bcigrp", cc, jnp.exp(a_cs), s_prev)
    y = (y_diag + y_off).reshape(b, c * q, h, p)[:, :l]
    return y, s_final.reshape(b, h, p, n)

def mixer(xn, past_k, past_v, past_idx_k, ssm0, conv_prefix,
          w_in, conv_w, conv_b, dt_bias, a_log, d_skip, ssd_norm_g, idx_ln_w, idx_ln_b, w_branch, w_out):
    f32 = jnp.float32
    bsz, n_new, _ = xn.shape
    n_past = past_k.shape[1]
    pos = n_past + jnp.arange(n_new, dtype=jnp.int32)
    key_pos = jnp.arange(n_past + n_new, dtype=jnp.int32)
    proj = jnp.einsum("bld,de->ble", xn, w_in)
    (q, k, v, z_att, qi, ki, wi, z_ssd, xbc, dt, g_att, g_ssd) = jnp.split(proj, SPLIT_POINTS, axis=-1)

    q = rope(q.reshape(bsz, n_new, ATT_HEADS, HEAD_DIM), pos)
    k = rope(k.reshape(bsz, n_new, KV_HEADS, HEAD_DIM), pos)
    v = v.reshape(bsz, n_new, KV_HEADS, HEAD_DIM)
    qi = rope(qi.reshape(bsz, n_new, IDX_HEADS, IDX_DIM), pos)
    ki = rope(layernorm(ki, idx_ln_w, idx_ln_b)[:, :, None, :], pos)[:, :, 0, :]
    wi = wi * IDX_SCALE
    k_all = jnp.concatenate([past_k.astype(k.dtype), k], axis=1)
    v_all = jnp.concatenate([past_v.astype(v.dtype), v], axis=1)
    ki_all = jnp.concatenate([past_idx_k.astype(ki.dtype), ki], axis=1)
    top_k = max(1, min(TOPK_MAX, (n_past + n_new) // 4))
    qb = min(Q_BLOCK, n_new)
    nb = n_new // qb
    to_blocks = lambda t: jnp.moveaxis(t.reshape(bsz, nb, qb, *t.shape[2:]), 1, 0)

    def attend_block(args):
        qq, qqi, wwi, pp = args
        return dsa_attend(qq, qqi, wwi, pp, k_all, v_all, ki_all, key_pos, top_k)

    o = lax.map(attend_block, (to_blocks(q), to_blocks(qi), to_blocks(wi), pos.reshape(nb, qb)))
    o = jnp.moveaxis(o, 0, 1).reshape(bsz, n_new, ATT_W)
    y_att = o * jax.nn.silu(z_att)

    xbc_act, conv_new = causal_conv(xbc, conv_prefix, conv_w, conv_b)
    xs, bm, cm = jnp.split(xbc_act, [D_INNER, D_INNER + SSD_GROUPS * D_STATE], axis=-1)
    dt = jax.nn.softplus(dt.astype(f32) + dt_bias.astype(f32))
    a = -jnp.exp(a_log.astype(f32))
    xs_h = xs.reshape(bsz, n_new, SSD_HEADS, SSD_HEAD_DIM).astype(f32)
    y_ssd, ssm_new = ssd_scan(xs_h, dt, a,
                              bm.reshape(bsz, n_new, SSD_GROUPS, D_STATE).astype(f32),
                              cm.reshape(bsz, n_new, SSD_GROUPS, D_STATE).astype(f32),
                              ssm0.astype(f32))
    y_ssd = y_ssd + d_skip.astype(f32)[:, None] * xs_h
    y_ssd = y_ssd.reshape(bsz, n_new, D_INNER).astype(xn.dtype) * jax.nn.silu(z_ssd)
    y_ssd = group_rmsnorm(y_ssd, ssd_norm_g)

    ya = jnp.einsum("blw,wd->bld", y_att, w_branch[:ATT_W])
    yb = jnp.einsum("blw,wd->bld", y_ssd, w_branch[ATT_W:])
    merged = jax.nn.sigmoid(g_att) * ya + jax.nn.sigmoid(g_ssd) * yb
    out = jnp.einsum("bld,de->ble", merged, w_out)
    return out, k, v, ki, ssm_new.astype(xn.dtype), conv_new

def setup_inputs(seed: int = 0) -> dict:
    key = jax.random.key(seed)
    ks = jax.random.split(key, 24)
    f32 = jnp.float32
    n_pages = PAST_LEN // PAGE_SIZE
    n_phys = (DEC_BATCH * n_pages * 5) // 4
    nrm = lambda k, shape, s: s * jax.random.normal(k, shape, f32)
    x_prompt = nrm(ks[0], (BATCH, SEQ, D_MODEL), 1.0)
    x_sample = nrm(ks[1], (DEC_BATCH, DEC_SEQ, D_MODEL), 1.0)
    cache_k = nrm(ks[2], (DEPTH, n_phys, PAGE_SIZE, KV_HEADS, HEAD_DIM), 1.0)
    cache_v = nrm(ks[3], (DEPTH, n_phys, PAGE_SIZE, KV_HEADS, HEAD_DIM), 1.0)
    cache_idx_k = nrm(ks[4], (DEPTH, n_phys, PAGE_SIZE, IDX_DIM), 1.0)
    state_ssm = nrm(ks[5], (DEPTH, DEC_BATCH, SSD_HEADS, SSD_HEAD_DIM, D_STATE), 0.1)
    state_conv = nrm(ks[6], (DEPTH, DEC_BATCH, CONV_W - 1, CONV_DIM), 1.0)
    page_table = jax.random.permutation(ks[7], n_phys)[: DEC_BATCH * n_pages].reshape(DEC_BATCH, n_pages).astype(jnp.int32)
    norm_g = 1.0 + nrm(ks[8], (DEPTH, D_MODEL), 0.02)
    w_in = nrm(ks[9], (DEPTH, D_MODEL, IN_W), D_MODEL ** -0.5)
    conv_w = nrm(ks[10], (DEPTH, CONV_W, CONV_DIM), CONV_W ** -0.5)
    conv_b = nrm(ks[11], (DEPTH, CONV_DIM), 0.01)
    dt0 = jnp.exp(jax.random.uniform(ks[12], (DEPTH, SSD_HEADS), f32, math.log(1e-3), math.log(1e-1)))
    dt_bias = dt0 + jnp.log(-jnp.expm1(-dt0))
    a_log = jnp.log(jax.random.uniform(ks[13], (DEPTH, SSD_HEADS), f32, 1.0, 16.0))
    d_skip = 1.0 + nrm(ks[14], (DEPTH, SSD_HEADS), 0.1)
    ssd_norm_g = 1.0 + nrm(ks[15], (DEPTH, D_INNER), 0.02)
    idx_ln_w = 1.0 + nrm(ks[16], (DEPTH, IDX_DIM), 0.02)
    idx_ln_b = nrm(ks[17], (DEPTH, IDX_DIM), 0.01)
    w_branch = jnp.concatenate([nrm(ks[18], (DEPTH, ATT_W, D_MODEL), ATT_W ** -0.5),
                                nrm(ks[19], (DEPTH, D_INNER, D_MODEL), D_INNER ** -0.5)], axis=1)
    w_out = nrm(ks[20], (DEPTH, D_MODEL, D_MODEL), D_MODEL ** -0.5)
    final_norm_g = 1.0 + nrm(ks[21], (D_MODEL,), 0.02)
    return {"x_prompt": x_prompt, "x_sample": x_sample, "cache_k": cache_k, "cache_v": cache_v,
            "cache_idx_k": cache_idx_k, "state_ssm": state_ssm, "state_conv": state_conv,
            "page_table": page_table, "norm_g": norm_g, "w_in": w_in, "conv_w": conv_w, "conv_b": conv_b,
            "dt_bias": dt_bias, "a_log": a_log, "d_skip": d_skip, "ssd_norm_g": ssd_norm_g,
            "idx_ln_w": idx_ln_w, "idx_ln_b": idx_ln_b, "w_branch": w_branch, "w_out": w_out,
            "final_norm_g": final_norm_g}

def reference(x_prompt, x_sample, cache_k, cache_v, cache_idx_k, state_ssm, state_conv, page_table,
              norm_g, w_in, conv_w, conv_b, dt_bias, a_log, d_skip, ssd_norm_g, idx_ln_w, idx_ln_b,
              w_branch, w_out, final_norm_g):
    hp, hs = x_prompt, x_sample
    bp = hp.shape[0]
    outs_p, outs_s = [], []
    for l in range(DEPTH):
        weights = (w_in[l], conv_w[l], conv_b[l], dt_bias[l], a_log[l], d_skip[l], ssd_norm_g[l],
                   idx_ln_w[l], idx_ln_b[l], w_branch[l], w_out[l])
        dp, *st_p = mixer(rmsnorm(hp, norm_g[l]),
                          jnp.zeros((bp, 0, KV_HEADS, HEAD_DIM), hp.dtype),
                          jnp.zeros((bp, 0, KV_HEADS, HEAD_DIM), hp.dtype),
                          jnp.zeros((bp, 0, IDX_DIM), hp.dtype),
                          jnp.zeros((bp, SSD_HEADS, SSD_HEAD_DIM, D_STATE), hp.dtype),
                          jnp.zeros((bp, CONV_W - 1, CONV_DIM), hp.dtype),
                          *weights)
        hp = hp + dp
        ds, *st_s = mixer(rmsnorm(hs, norm_g[l]),
                          gather_pages(cache_k[l], page_table),
                          gather_pages(cache_v[l], page_table),
                          gather_pages(cache_idx_k[l], page_table),
                          state_ssm[l], state_conv[l],
                          *weights)
        hs = hs + ds
        outs_p.append(st_p)
        outs_s.append(st_s)
    stack = lambda lst, i: jnp.stack([o[i] for o in lst], axis=0)
    y_prompt = rmsnorm(hp, final_norm_g)
    y_sample = rmsnorm(hs, final_norm_g)
    k_prompt, v_prompt, idx_k_prompt = stack(outs_p, 0), stack(outs_p, 1), stack(outs_p, 2)
    ssm_prompt, conv_prompt = stack(outs_p, 3), stack(outs_p, 4)
    k_sample, v_sample, idx_k_sample = stack(outs_s, 0), stack(outs_s, 1), stack(outs_s, 2)
    ssm_sample, conv_sample = stack(outs_s, 3), stack(outs_s, 4)
    return (y_prompt, y_sample, k_prompt, v_prompt, idx_k_prompt, ssm_prompt, conv_prompt,
            k_sample, v_sample, idx_k_sample, ssm_sample, conv_sample)


_drawn_inputs = setup_inputs


def setup_inputs(seed=0):
    import zlib

    import numpy as np

    out = dict(_drawn_inputs(seed))
    spreads = {}
    factors = {'conv_b': 3.52,
     'ssd_norm_g': 17.486,
     'idx_ln_b': 5.713,
     'final_norm_g': 7.648,
     'cache_k': 7.311,
     'cache_v': 5.728,
     'cache_idx_k': 6.532}
    for name, (base, spread) in spreads.items():
        noise = np.random.default_rng([zlib.crc32(name.encode()), seed]).standard_normal(out[name].shape)
        drawn = base * np.exp(spread * noise) if base else spread * noise
        out[name] = __import__('jax').numpy.asarray(drawn.astype(out[name].dtype))
    for name, factor in factors.items():
        out[name] = (out[name] * factor).astype(out[name].dtype)
    return out
```

```python
from contextlib import ExitStack

import numpy as np
import concourse.bass as bass
import concourse.mybir as mybir

ALU = mybir.AluOpType
ACT = mybir.ActivationFunctionType
AX = mybir.AxisListType
F32 = mybir.dt.float32
BF16 = mybir.dt.bfloat16
I32 = mybir.dt.int32

P = 128
D_MODEL = 2048
KC = D_MODEL // P
SEQ = 512
DB, DS = 8, 4
NS = DB * DS
NT = SEQ + NS
HALF = NT // 2
TT = 5
ROWS = [P, P, P, P, NS]
PAGES, PAGE = 8, 128
PAST = PAGES * PAGE
NPHYS = DB * PAGES * 5 // 4
SKEYS = PAST + NS
HD = 128
QH, KVH = 16, 4
REP = QH // KVH
IH, ID = 16, 64
IDX_SCALE = IH ** -0.5 * ID ** -0.5
ATT_SCALE = HD ** -0.5
TOPK_P = SEQ // 4
TOPK_S = 256
THETA = 10000.0
D_INNER = 4096
SH, SP_ = 64, 64
SG = 8
GH = SH // SG
NST = 128
CW = 4
CONV_DIM = D_INNER + 2 * SG * NST
EPS = 1e-6
SLAB = 256
FT = SLAB // P

O_Q = 0
O_K = 2048
O_V = O_K + 512
O_ZATT = O_V + 512
O_QI = O_ZATT + 2048
O_KI = O_QI + IH * ID
O_WI = O_KI + ID
O_Z = O_WI + IH
O_X = O_Z + D_INNER
O_B = O_X + D_INNER
O_C = O_B + SG * NST
O_DT = O_C + SG * NST
O_GA = O_DT + SH
O_GS = O_GA + D_MODEL

RAW_S = SEQ + CW - 1
RAW = RAW_S + DB * (CW - 1 + DS)
ACC = RAW - (CW - 1)

NEG = -1e30
PICKED = -3e38


def constant_arrays():
    c = {}
    c["ident"] = np.eye(P, dtype=np.float32)
    pos = np.zeros(TT * P, np.int64)
    pos[:SEQ] = np.arange(SEQ)
    pos[SEQ:SEQ + NS] = PAST + np.arange(NS) % DS
    rope = np.zeros((TT, P, 2 * (HD // 2) + 2 * (ID // 2)), np.float32)
    for d, at in ((HD, 0), (ID, HD)):
        inv = np.float32(THETA) ** (-np.arange(0, d, 2, dtype=np.float32) / np.float32(d))
        ang = pos.astype(np.float32)[:, None] * inv[None].astype(np.float32)
        rope[:, :, at:at + d // 2] = np.cos(ang).reshape(TT, P, -1)
        rope[:, :, at + d // 2:at + d] = np.sin(ang).reshape(TT, P, -1)
    c["rope"] = rope
    i = np.arange(P)
    c["causal_q"] = np.where(i[None, :] <= i[:, None], 0, NEG).astype(np.float32)
    c["causal_k"] = (i[:, None] <= i[None, :]).astype(np.float32)
    s = np.arange(NS)
    same = s[:, None] // DS == s[None, :] // DS
    c["dec_k"] = (same & (s[:, None] <= s[None, :])).astype(np.float32)
    dec_q = np.zeros((NS, SKEYS), np.float32)
    dec_q[:, PAST:] = np.where(same & (s[None, :] <= s[:, None]), 0, NEG)
    c["dec_q"] = dec_q
    selrow = np.zeros((NS, DB, P), np.float32)
    for b in range(DB):
        for g in range(KVH):
            for r in range(REP):
                for t in range(DS):
                    selrow[DS * b + t, b, 32 * g + DS * r + t] = 1
    c["selrow"] = selrow
    headmask = np.zeros((IH * DS, DB, NS), np.float32)
    for b in range(DB):
        for h in range(IH):
            for t in range(DS):
                headmask[DS * h + t, b, DS * b + t] = 1
    c["headmask"] = headmask
    c["in_batch"] = (s[:, None] // DS == np.arange(DB)[None]).astype(np.float32)
    c["batch_cols"] = np.broadcast_to((np.arange(DB)[:, None] == s[None] // DS), (P, DB, NS)).astype(np.float32)
    return c


class Steps:

    def __init__(self, eng, semaphore):
        self.eng, self.sem, self.count, self.frame = eng, semaphore, 0, None

    def add(self, instruction):
        instruction.then_inc(self.sem, 1)
        self.count += 1

    def wait(self):
        base, inside = self.frame if self.frame else (0, 0)
        self.eng.wait_ge(self.sem, base + self.count)

    def loop(self, start, trips, per):
        return _Loop(self, start, trips, per)


class _Loop:
    def __init__(self, steps, start, trips, per):
        self.s, self.start, self.trips, self.per = steps, start, trips, per

    def __enter__(self):
        self.fori = self.s.eng.Fori(self.start, self.start + self.trips)
        i = self.fori.__enter__()
        self.before = self.s.count
        self.s.frame = ((i - self.start) * self.per + self.before if self.per else self.before, 0)
        self.s.count = 0
        return i

    def __exit__(self, *exc):
        if exc[0] is None:
            assert self.s.count == self.per, f"the body adds {self.s.count}, the loop was told {self.per}"
        self.s.count = self.before + self.trips * self.per
        self.s.frame = None
        return self.fori.__exit__(*exc)


def build(nc, a, out, c):
    with ExitStack() as ctx:
        sems = {}

        def sem(name):
            if name not in sems:
                sems[name] = ctx.enter_context(nc.semaphore(name))
            return sems[name]

        def sb(name, shape, dt=F32):
            return ctx.enter_context(nc.sbuf_tensor(name, shape, dt))

        ps = ctx.enter_context(nc.psum_tensor("ps", [P, 8, 512], F32))

        def dram(name, shape):
            return nc.dram_tensor(name, shape, F32, kind="Internal").ap()

        yatt_dram = dram("yatt_dram", (P, QH * NT))
        yssd_dram = dram("yssd_dram", (P, 2 * KC * NT))
        merged_dram = dram("merged_dram", (P, KC * NT))
        acsT_dram = dram("acsT_dram", (SH, NT))
        acs_dram = dram("acs_dram", (TT, P, SH))
        wi_dram = dram("wi_dram", (NS, IH))

        xnT = sb("xnT", [P, KC, NT])
        W = sb("W", [P, 3, KC, SLAB])
        ident = sb("ident", [P, P])
        ident_bf = sb("ident_bf", [P, P], BF16)
        ones = sb("ones", [P, P])
        causal_q = sb("causal_q", [P, P])
        causal_k = sb("causal_k", [P, P])
        dec_k = sb("dec_k", [NS, NS])
        gT = sb("gT", [P, KC])
        gnT = sb("gnT", [P, 2 * KC])
        cwT = sb("cwT", [P, CONV_DIM // P, DB * (CW - 1) + CW + 1])
        dskip = sb("dskip", [P, SH])
        in_batch = sb("in_batch", [NS, DB])
        batch_cols = sb("batch_cols", [P, DB, NS])
        dt_tok = sb("dt_tok", [P, TT, SH])
        acs_tok = sb("acs_tok", [P, TT, SH])
        grow_tok = sb("grow_tok", [P, TT, SH])
        dec_tok = sb("dec_tok", [P, TT, SH])
        cdec = sb("cdec", [P, 4, SH])
        decS = sb("decS", [P, SH // 2, DB])
        small = sb("small", [P, 64])
        sumsq, rstd = small[:, 0:8], small[:, 8:16]
        lnst, lnagg, lnr = small[:, 16:22], small[:, 22:24], small[:, 24:25]
        c_small = sb("c_small", [P, 32])
        wi4 = c_small[:, 28:32]
        pt_sb = sb("pt_sb", [1, DB * PAGES], I32)
        ARENA = 27880
        R = sb("R", [P, ARENA])

        def carve(at, *shape, rows=P, dt=F32):
            n = int(np.prod(shape))
            words = n if dt == F32 else n // 2
            assert at + words <= ARENA, (at, words)
            v = R[0:rows, at:at + words]
            if dt != F32:
                v = v.bitcast(dt)
            if len(shape) == 2:
                v = v.rearrange("p (a b) -> p a b", a=shape[0])
            if len(shape) == 3:
                v = v.rearrange("p (a b c) -> p a b c", a=shape[0], b=shape[1])
            return v, at + words

        qkT, at = carve(0, QH + KVH, NT)
        vtok, at = carve(at, TT, KVH * HD)
        att_free = at
        qiT, at = carve(at, IH, NT)
        kiT, at = carve(at, NT, rows=ID)
        wi_tok, at = carve(at, TT, IH)
        b_free = at
        rope, at = carve(b_free, TT, HD + ID)
        tcos, at = carve(at, SLAB)
        tsin, at = carve(at, SLAB)
        rot, at = carve(at, 2, SLAB)
        lnw, at = carve(at, ID)
        lnb, at = carve(at, ID)
        kin, at = carve(at, 2, ID)
        dtT, at = carve(at, NT, rows=SH)
        dtE, at = carve(at, NT, rows=SH)
        dtU, at = carve(at, NT, rows=SH)
        dtL, at = carve(at, NT, rows=SH)
        xt, at = carve(0, 2, D_MODEL)
        xsq, at = carve(at, D_MODEL)
        convrows, at = carve(at, CONV_DIM, rows=DB * (CW - 1) + CW + 1)
        grow_rows, at = carve(at, P, rows=KC)
        gnrow_rows, at = carve(at, P, rows=2 * KC)
        dtR = R[0:SH, b_free + TT * (HD + ID):b_free + TT * (HD + ID) + NT]

        def bank(n, rows=P, cols=512, r0=0):
            return ps[r0:r0 + rows, n, 0:cols]

        def tok(t):
            return slice(P * t, P * t + ROWS[t])

        def bc(ap, shape, *axes):
            for x in axes:
                ap = ap.unsqueeze(x)
            return ap.to_broadcast(shape)

        Wflat = W[:, :, :, :].rearrange("p a b c -> p (a b c)")

        def wcarve(at, *shape, rows=P):
            n = int(np.prod(shape))
            assert at + n <= 3 * KC * SLAB
            v = Wflat[0:rows, at:at + n]
            if len(shape) == 2:
                v = v.rearrange("p (a b) -> p a b", a=shape[0])
            if len(shape) == 3:
                v = v.rearrange("p (a b c) -> p a b c", a=shape[0], b=shape[1])
            return v, at + n

        kidx, at = wcarve(0, 2, PAGES * ID)
        kisT, at = wcarve(at, 2, PAST, rows=ID)
        srelu, at = wcarve(at, 2, SKEYS, rows=IH * DS)
        prelu, at = wcarve(at, 4, SEQ)
        qist, at = wcarve(at, 4, P, rows=ID)
        qis, at = wcarve(at, 2 * IH * DS, rows=ID)
        hw, at = wcarve(at, 2, NS, rows=IH * DS)
        headmask, at = wcarve(at, DB, NS, rows=IH * DS)
        wcol, at = wcarve(at, DB, rows=IH * DS)
        dec_q, at = wcarve(at, SKEYS, rows=NS)
        psc, at = carve(b_free, 3, SEQ)
        ssc, at = carve(at, SKEYS, rows=NS)
        pmask, at = carve(at, 4, SEQ, dt=BF16)
        smask, at = carve(at, SKEYS, rows=NS, dt=BF16)
        top8, at = carve(at, 8)
        at_masks = at
        qst, at = carve(att_free, REP, P)
        pexp, at = carve(at, REP, SEQ)
        pT, at = carve(at, 2, SEQ)
        on, at = carve(at, REP, P)
        assert at <= b_free
        Kb, at = wcarve(0, 2 * PAGES, KVH * HD)
        V0, at = wcarve(at, PAGES, KVH * HD)
        V1, at = carve(att_free, PAGES, KVH * HD)
        Vb = [V0, V1]
        kTb, at = carve(at, 2, PAST)
        sexp, at = carve(at, SKEYS)
        sT, at = carve(at, PAGES + 1, P)
        qsb, at = carve(at, KVH, 32)
        assert at <= b_free
        selrow, at = carve(at_masks, DB, P, rows=NS, dt=BF16)
        selst, at = carve(at, P, rows=NS, dt=BF16)
        selrow_f = psc.rearrange("p a b -> p (a b)")[0:NS, 0:DB * P].rearrange("p (a b) -> p a b", a=DB)
        zt, at = carve(att_free, 2, NT)

        NJ = GH // 2 + 2
        raw, at = carve(0, NJ, RAW)
        zraw, at = carve(at, 4, NT)
        acc, at = carve(at, 2, RAW)
        xact, at = carve(at, NJ, NT)
        zs, at = carve(at, 4, NT)
        acsbc, at = carve(at, GH, NT)
        xdt, at = carve(at, GH, SP_)
        xD, at = carve(at, GH, SP_)
        xdtd, at = carve(at, GH, SP_)
        E, at = carve(at, GH, P)
        Btok, at = carve(at, P)
        Bblk, at = carve(at, DB, NST, rows=NS)
        ytok, at = carve(at, GH * SP_)
        yT, at = carve(at, 4, NT)
        S, at = carve(at, GH * SP_)
        st, at = carve(at, DB // 2, 4, NST)
        ST, at = carve(at, 2, GH * SP_)
        Cm, at = carve(at, DB, NS)
        cn, at = carve(at, NJ, CW - 1 + DB * (CW - 1))
        cno, at = carve(at, NJ * P, rows=CW - 1 + DB * (CW - 1))
        cw_g, at = carve(at, NJ, DB * (CW - 1) + CW + 1)
        gn_g = small[:, 28:32]
        cbm = causal_q
        NC = CW - 1 + DB * (CW - 1)
        sq = xact
        rn_row = acsbc[:, 0, :]
        rn = rn_row.rearrange("p (a b) -> p a b", a=2)
        fsb = acc.rearrange("p a b -> p (a b)")[:, 0:4 * NST]

        yattF, at = carve(0, QH, NT)
        yssdF, at = carve(at, 2 * KC, NT)
        gateA, at = carve(at, 2, NT)
        gateS = cwT.rearrange("p a b -> p (a b)")[:, 0:2 * NT].rearrange("p (a b) -> p a b", a=2)
        mergedT, at = carve(0, KC, NT)
        h_out, at = carve(at, TT, D_MODEL)
        fg_bc, at = carve(at, D_MODEL)
        gsq, at = carve(at, D_MODEL)

        def decode_acc(j):
            return acc[:, j % 2, RAW_S:RAW].rearrange("p (b k) -> p b k", b=DB)[:, :, 0:DS]

        c_dtb, c_alog, c_aneg, nmx, mx, rsum, rinv = (c_small[:, k:k + 1] for k in (0, 1, 2, 3, 7, 11, 15))
        expS = c_small[0:SH, 20:20 + DB]
        nmx4, mx4, rsum4, rinv4 = (c_small[:, k:k + 4] for k in (3, 7, 11, 15))

        ROOTS_B, ROOTS_E, ROOTS_G = TT, 2 * TT, 2 * TT + SG

        STAGE_ENDS = {"A": 5, "B": 10, "C1": 15, "C2": 20, "C3a": 25, "C3": 30, "D": 34, "D2": 38, "E": 42, "F": 46}

        def stage_end(eng, name):
            eng.drain().then_inc(sem("stage_ended"), 1)
            eng.wait_ge(sem("stage_ended"), STAGE_ENDS[name])

        def apart(eng):
            eng.sem_inc(sem("waited"), 1)

        FIRST_USE = {"B": (0, 0, 0), "D": (8, 8, 1), "E": (12, 12, 1), "F": (28, 28, 9), "G": (44, 44, 17)}
        w_in_rows = a["w_in"][0].rearrange("(kc p) n -> p kc n", p=P)
        w_br_rows = a["w_branch"][0].rearrange("(kc p) n -> p kc n", p=P)
        w_out_rows = a["w_out"][0].rearrange("(kc p) n -> p kc n", p=P)

        def load_slab(eng, slot, src, after=None):
            if after:
                eng.wait_ge(sem(after[0]), after[1])
            eng.dma_start(W[:, slot, :, :], src).then_inc(sem(f"slab{slot}_loaded"), 16)

        def await_slab(eng, slot, use):
            eng.wait_ge(sem(f"slab{slot}_loaded"), (use + (2 if slot == 2 else 1)) * 16)

        NSTATE = DB * (CW - 1)
        N_CONST = 17
        block = ctx.enter_context(nc.Block())

        @block.sync
        def _(eng):
            for t in range(2):
                eng.dma_start(xt[:, t, :], a["x_prompt"][0, tok(t), :]).then_inc(sem(f"x_in{t}"), 16)
            row = lambda ap: ap.rearrange("(a n) -> a n", a=1)
            col = lambda ap: ap.rearrange("(n a) -> n a", a=1)
            for dst, src in ((ident[:, :], c["ident"]), (grow_rows, a["norm_g"][0].rearrange("(a b) -> a b", b=P)),
                             (gnrow_rows, a["ssd_norm_g"][0].rearrange("(a b) -> a b", b=P)),
                             (convrows[0:NSTATE, :], a["state_conv"][0].rearrange("b k n -> (b k) n")),
                             (convrows[NSTATE:NSTATE + CW, :], a["conv_w"][0]),
                             (convrows[NSTATE + CW:NSTATE + CW + 1, :], a["conv_b"]),
                             (causal_q[:, :], c["causal_q"]), (causal_k[:, :], c["causal_k"]),
                             (dec_k[:, :], c["dec_k"]), (in_batch[:, :], c["in_batch"]),
                             (batch_cols[:, :, :], c["batch_cols"]),
                             (pt_sb[:, :], row(a["page_table"].rearrange("b n -> (b n)"))),
                             (dskip[:, :], a["d_skip"][0].partition_broadcast(P)),
                             (rope[:, :, :], c["rope"].rearrange("t p n -> p t n")),
                             (lnw, a["idx_ln_w"][0].partition_broadcast(P)),
                             (lnb, a["idx_ln_b"][0].partition_broadcast(P)),
                             (c_dtb[0:SH, :], col(a["dt_bias"][0]))):
                eng.dma_start(dst, src).then_inc(sem("consts_in"), 16)
            eng.dma_start(c_alog[0:SH, :], col(a["a_log"][0])).then_inc(sem("alog_in"), 16)
            eng.dma_start(W[:, 2, :, 0:ID + IH], w_in_rows[:, :, O_KI:O_KI + ID + IH]).then_inc(sem("slab2_loaded"), 16)
            eng.dma_start(W[:, 2, :, ID + IH:ID + IH + SH], w_in_rows[:, :, O_DT:O_DT + SH]).then_inc(sem("slab2_loaded"), 16)
            for s in range(2):
                load_slab(eng, s, w_in_rows[:, :, s * SLAB:(s + 1) * SLAB])
            for t in range(2, TT):
                eng.wait_ge(sem("xT_turned"), t - 1)
                src = a["x_prompt"][0, tok(t), :] if t < 4 else a["x_sample"].rearrange("b t d -> (b t) d")
                eng.dma_start(xt[0:ROWS[t], t % 2, :], src).then_inc(sem(f"x_in{t % 2}"), 16)
            stage_end(eng, "A")
            with eng.Fori(1, 6) as i:
                for s in range(2):
                    load_slab(eng, s, w_in_rows[:, :, bass.ds(i * (2 * SLAB) + s * SLAB, SLAB)],
                              ("tok_ready", i * 10 + (5 * s - 5)))
            with eng.Fori(6, 8) as i:
                for s in range(2):
                    load_slab(eng, s, w_in_rows[:, :, bass.ds((i - 6) * (2 * SLAB) + (O_QI + s * SLAB), SLAB)],
                              ("tok_ready", i * 10 + (5 * s - 5)))
            for k in ("B", "C1", "C2", "C3a", "C3"):
                stage_end(eng, k)
            for s in range(2):
                load_slab(eng, s, w_in_rows[:, :, O_ZATT + s * SLAB:O_ZATT + (s + 1) * SLAB])
            with eng.Fori(1, 4) as i:
                for s in range(2):
                    load_slab(eng, s, w_in_rows[:, :, bass.ds(i * (2 * SLAB) + (O_ZATT + s * SLAB), SLAB)],
                              ("zatt_ready", i * 4 + (2 * s - 2)))

            def group_slabs(g, x0_after, x1_after, bc_after):
                x0, z0 = g * (2 * SLAB) + O_X, g * (2 * SLAB) + O_Z
                load_slab(eng, 0, w_in_rows[:, :, bass.ds(x0, SLAB)], x0_after)
                load_slab(eng, 1, w_in_rows[:, :, bass.ds(x0 + SLAB, SLAB)], x1_after)
                if bc_after:
                    eng.wait_ge(sem(bc_after[0]), bc_after[1])
                for part, off in ((0, O_B), (1, O_C)):
                    eng.dma_start(W[:, 2, :, part * P:part * P + P],
                                  w_in_rows[:, :, bass.ds(g * P + off, P)]).then_inc(sem("bc_loaded"), 16)
                for s in range(2):
                    load_slab(eng, s, w_in_rows[:, :, bass.ds(z0 + s * SLAB, SLAB)], ("projT_ready", g * 10 + (2 * s + 2)))
            group_slabs(0, ("zatt_ready", 14), ("zatt_ready", 16), None)
            with eng.Fori(1, SG) as g:
                group_slabs(g, ("projT_ready", g * 10 - 2), ("projT_ready", g * 10), ("projT_ready", g * 10 - 4))
            eng.wait_ge(sem("projT_ready"), 10 * SG)
            with eng.Fori(0, D_MODEL // SLAB) as i:
                cs = bass.ds(i * SLAB, SLAB)
                load_slab(eng, 0, w_in_rows[:, :, bass.ds(i * SLAB + O_GA, SLAB)], ("yb1_done", i))
                load_slab(eng, 1, w_in_rows[:, :, bass.ds(i * SLAB + O_GS, SLAB)], ("yb_ready", i * 2))
                eng.wait_ge(sem("ya_ready"), i * 2)
                apart(eng)
                eng.dma_start(W[:, 2, :, :], w_br_rows[:, 0:KC, cs]).then_inc(sem("branch_loaded"), 16)
                load_slab(eng, 0, w_br_rows[:, KC:2 * KC, cs], ("ga_ready", i * 2 + 2))
                load_slab(eng, 1, w_br_rows[:, 2 * KC:3 * KC, cs], ("gs_ready", i * 2 + 2))
            load_slab(eng, 0, w_out_rows[:, :, 0:SLAB], ("yb1_done", 8))
            load_slab(eng, 1, w_out_rows[:, :, SLAB:2 * SLAB], ("yb_ready", 16))
            with eng.Fori(1, 4) as i:
                for s in range(2):
                    load_slab(eng, s, w_out_rows[:, :, bass.ds(i * (2 * SLAB) + s * SLAB, SLAB)],
                              ("h_ready", i * 10 + (5 * s - 5)))

        @block.tensor
        def _(eng):
            def project_tokens(slot, t, bank_no, c0, cols):
                for kc in range(KC):
                    mm = eng.matmul(ps[0:ROWS[t], bank_no, 0:cols], xnT[:, kc, tok(t)], W[:, slot, kc, c0:c0 + cols],
                                    start=(kc == 0), stop=(kc == KC - 1))
                return mm

            def project_features(slot, j, pair, rhs=None, rows=P, k0=0, start=True, stop=True):
                rhs = xnT if rhs is None else rhs
                for kc in range(KC):
                    for h in range(2):
                        mm = eng.matmul(ps[0:rows, 2 * pair + h, 0:HALF], W[:, slot, kc, j:j + rows],
                                        rhs[:, k0 + kc, HALF * h:HALF * (h + 1)],
                                        start=(start and kc == 0), stop=(stop and kc == KC - 1))
                return mm

            eng.wait_ge(sem("consts_in"), 16 * N_CONST)
            eng.transpose(ps[:, 4, 0:KC], grow_rows, ident[0:KC, 0:KC])
            eng.transpose(ps[:, 4, KC:3 * KC], gnrow_rows, ident[0:2 * KC, 0:2 * KC]).then_inc(sem("rows_turned"), 1)
            NR = NSTATE + CW + 1
            for n in range(CONV_DIM // P):
                tr = eng.transpose(ps[:, 5 + n // 16, (n % 16) * NR:(n % 16 + 1) * NR], convrows[:, n * P:(n + 1) * P],
                                   ident[0:NR, 0:NR])
            tr.then_inc(sem("rows_turned"), 1)
            for t in range(TT):
                eng.wait_ge(sem("x_scaled"), t + 1)
                if t == 1:
                    eng.wait_ge(sem("rows_kept"), 3)
                if t >= 2:
                    eng.wait_ge(sem("xnT_kept"), t - 1)
                for k in range(KC):
                    tr = eng.transpose(ps[:, 4 * (t % 2) + k // 4, (k % 4) * P:(k % 4) * P + ROWS[t]],
                                       xt[0:ROWS[t], t % 2, k * P:(k + 1) * P], ident[0:ROWS[t], 0:ROWS[t]])
                tr.then_inc(sem("xT_turned"), 1)
            stage_end(eng, "A")

            def turn_rot(n, t, heads, width):
                eng.wait_ge(sem("rot_ready"), n + 1)
                eng.wait_ge(sem("rotT_kept"), n)
                apart(eng)
                for h in range(heads):
                    tr = eng.transpose(ps[0:width, 5 + t % 3, h * P:h * P + ROWS[t]],
                                       rot[0:ROWS[t], t % 2, h * width:(h + 1) * width], ident[0:ROWS[t], 0:ROWS[t]])
                tr.then_inc(sem("rot_turned"), 1)

            def slab_tokens(slot, use, n, turn_base, heads, width, cols=SLAB):
                await_slab(eng, slot, use)
                eng.wait_ge(sem("tok_kept"), n)
                for t in range(TT):
                    mm = project_tokens(slot, t, t, 0, cols)
                    mm.then_inc(sem("tok_ready"), 1)
                    if heads and t:
                        turn_rot(turn_base + (t - 1), t - 1, heads, width)
                if heads:
                    turn_rot(turn_base + (TT - 1), TT - 1, heads, width)

            with eng.Fori(0, 5) as i:
                for s in range(2):
                    slab_tokens(s, i, i * 10 + 5 * s, i * 10 + 5 * s, 2, HD)
            for s in range(2):
                slab_tokens(s, 5, 50 + 5 * s, None, 0, 0)
            with eng.Fori(6, 8) as i:
                for s in range(2):
                    slab_tokens(s, i, i * 10 + 5 * s, i * 10 + (5 * s - 10), 4, ID)
            eng.wait_ge(sem("slab2_loaded"), 32)
            eng.wait_ge(sem("tok_kept"), 80)
            for t in range(TT):
                project_tokens(2, t, t, 0, ID + IH).then_inc(sem("tok_ready"), 1)
            eng.wait_ge(sem("rotT_kept"), 71)
            project_features(2, ID + IH, 3, rows=SH).then_inc(sem("dt_ready"), 1)
            for t in range(TT):
                eng.wait_ge(sem("rot_ready"), 70 + t + 1)
                if t >= 1:
                    eng.wait_ge(sem("rotT_kept"), 70 + t + 1)
                eng.transpose(ps[0:ID, 5, 0:ROWS[t]], rot[0:ROWS[t], t % 2, 0:ID],
                              ident[0:ROWS[t], 0:ROWS[t]]).then_inc(sem("rot_turned"), 1)
            eng.wait_ge(sem("tok_kept"), 85)
            for k, src in enumerate((dtT, dtU)):
                eng.wait_ge(sem("dtT_ready"), k + 1)
                for t in range(TT):
                    tr = eng.transpose(ps[0:ROWS[t], k, t * SH:(t + 1) * SH], src[:, tok(t)], ident[0:SH, 0:SH])
                tr.then_inc(sem("dt_turned"), 1)
            eng.wait_ge(sem("expS_ready"), 1)
            for h in range(SH):
                mm = eng.matmul(ps[SP_ * (h % 2):SP_ * (h % 2 + 1), 2, h // 2 * DB:(h // 2 + 1) * DB],
                                ident[0:SH, h:h + 1].to_broadcast([SH, SP_]), expS, start=True, stop=True)
            mm.then_inc(sem("decS_ready"), 1)
            stage_end(eng, "B")

            eng.wait_ge(sem("idx_consts_in"), 32)
            for k, (lo, hi) in enumerate(((0, 512), (512, 1024), (1024, SKEYS))):
                eng.matmul(ps[0:NS, 5 + k, 0:hi - lo], ident[0:NS, 0:NS], dec_q[:, lo:hi], start=True, stop=False)

            def decode_index(n, i, k, last=False):
                eng.wait_ge(sem(f"kidx{k}_in"), i * (16 * PAGES) + 16 * PAGES)
                eng.wait_ge(sem("kisT_kept"), n)
                apart(eng)
                for p in range(PAGES):
                    tr = eng.transpose(ps[0:ID, p // 4, (p % 4) * P:(p % 4 + 1) * P], kidx[:, k, p * ID:(p + 1) * ID],
                                       ident[:, :])
                tr.then_inc(sem("kis_turned"), 1)
                eng.wait_ge(sem("kisT_kept"), n + 1)
                eng.wait_ge(sem("qis_ready"), n + 1)
                eng.wait_ge(sem("srelu_ready"), n)
                apart(eng)
                q = qis[:, k * IH * DS:(k + 1) * IH * DS]
                for h in range(2):
                    eng.matmul(ps[0:IH * DS, 2 + h, :], q, kisT[:, k, 512 * h:512 * (h + 1)], start=True, stop=True)
                eng.matmul(ps[0:IH * DS, 4, 0:NS], q, kiT[:, SEQ:NT], start=True, stop=True)\
                   .then_inc(sem("sdots_ready"), 1)
                eng.wait_ge(sem("srelu_ready"), n + 1)
                apart(eng)
                for j, (lo, hi) in enumerate(((0, 512), (512, 1024), (1024, SKEYS))):
                    mm = eng.matmul(ps[0:NS, 5 + j, 0:hi - lo], hw[:, k, :], srelu[:, k, lo:hi], start=False, stop=last)
                mm.then_inc(sem("sscore_added"), 1)
            with eng.Fori(0, DB // 2 - 1) as i:
                for k in range(2):
                    decode_index(i * 2 + k, i, k)
            for k in range(2):
                decode_index(DB - 2 + k, DB // 2 - 1, k, last=(k == 1))
            stage_end(eng, "C1")

            for qb in range(1, 4):
                n0 = 4 * (qb - 1)
                with eng.Fori(0, IH // 4) as i:
                    eng.wait_ge(sem("qist_ready"), i + (n0 + 1))
                    for h in range(4):
                        eng.wait_ge(sem("pdots_kept"), (i + n0) * 4)
                        eng.matmul(ps[:, h, 0:P * (qb + 1)], qist[:, h, :], kiT[:, 0:P * (qb + 1)], start=True, stop=True)\
                           .then_inc(sem("pdots_ready"), 1)
            stage_end(eng, "C2")

            for qb in range(4):
                nk = P * (qb + 1)
                with eng.Fori(0, KVH) as g:
                    n = g + KVH * qb
                    eng.wait_ge(sem("qst_ready"), n + 1)
                    for r in range(REP):
                        eng.wait_ge(sem("pexp_ready"), n * REP)
                        eng.matmul(ps[:, r, 0:nk], ident_bf[:, :], pmask[:, qb, 0:nk], start=True, stop=False)
                        eng.matmul(ps[:, r, 0:nk], qst[:, r, :],
                                   qkT[:, bass.ds(g + QH, 1), 0:nk].rearrange("p a n -> p (a n)"), start=False, stop=True)\
                           .then_inc(sem("pscore_ready"), 1)
                    for r in range(REP):
                        eng.wait_ge(sem("pexp_ready"), n * REP + (r + 1))
                        eng.wait_ge(sem("pT_kept"), n * REP + r)
                        for k in range(qb + 1):
                            tr = eng.transpose(ps[:, 4 + r % 2, k * P:(k + 1) * P], pexp[:, r, k * P:(k + 1) * P], ident[:, :])
                        tr.then_inc(sem("p_turned"), 1)
                        eng.wait_ge(sem("pT_kept"), n * REP + (r + 2))
                        if r == 0:
                            eng.wait_ge(sem("on_ready"), n)
                        for k in range(qb + 1):
                            mm = eng.matmul(ps[:, 6, r * P:(r + 1) * P], pT[:, r % 2, k * P:(k + 1) * P],
                                            vtok[:, k, bass.ds(g * HD, HD)], start=(k == 0), stop=(k == qb))
                        mm.then_inc(sem("po_ready"), 1)
                    eng.wait_ge(sem("on_ready"), n + 1)
                    eng.wait_ge(sem("poT_kept"), n)
                    for r in range(REP):
                        tr = eng.transpose(ps[:, 7, r * P:(r + 1) * P], on[:, r, :], ident[:, :])
                    tr.then_inc(sem("on_turned"), 1)
            def decode_attention(n, half, k):
                KB = ((0, 1), (5, 6))

                def turn_keys(g):
                    eng.wait_ge(sem(f"kTb{g % 2}_kept"), n * 2 + g // 2)
                    for p in range(PAGES):
                        tr = eng.transpose(ps[:, KB[g % 2][p // 4], (p % 4) * P:(p % 4 + 1) * P],
                                           Kb[:, k * PAGES + p, g * HD:(g + 1) * HD], ident[:, :])
                    tr.then_inc(sem("kb_turned"), 1)
                eng.wait_ge(sem(f"kpage{k}_in"), half * (16 * PAGES) + 16 * PAGES)
                eng.wait_ge(sem("qsb_ready"), n + 1)
                eng.wait_ge(sem("so_kept"), n)
                eng.wait_ge(sem("sT_kept"), n)
                for j, (lo, hi) in enumerate(((0, 512), (512, 1024), (1024, SKEYS))):
                    eng.matmul(ps[:, 2 + j, 0:hi - lo], selst, smask[:, lo:hi], start=True, stop=False)
                turn_keys(0)
                for g in range(KVH):
                    if g + 1 < KVH:
                        turn_keys(g + 1)
                    eng.wait_ge(sem(f"kTb{g % 2}_kept"), n * 2 + (g // 2 + 1))
                    q, rows = qsb[:, g, :], slice(32 * g, 32 * g + 32)
                    for j in range(2):
                        eng.matmul(ps[rows, 2 + j, :], q, kTb[:, g % 2, 512 * j:512 * (j + 1)],
                                   start=False, stop=True)
                    eng.matmul(ps[rows, 4, 0:NS], q, qkT[:, QH + g, SEQ:NT], start=False, stop=True)\
                       .then_inc(sem("dscore_done"), 1)
                eng.wait_ge(sem("sexp_ready"), n + 1)
                for p in range(PAGES):
                    eng.transpose(ps[:, 5 + p // 4, (p % 4) * P:(p % 4 + 1) * P], sexp[:, p * P:(p + 1) * P], ident[:, :])
                eng.transpose(ps[0:NS, 7, 0:P], sexp[:, PAST:SKEYS], ident[:, :]).then_inc(sem("s_turned"), 1)
                eng.wait_ge(sem("sT_kept"), n + 1)
                eng.wait_ge(sem(f"vpage{k}_in"), half * (16 * PAGES) + 16 * PAGES)
                for g in range(KVH):
                    o = ps[:, 0, g * 16:(g + 1) * 16]
                    for p in range(PAGES):
                        eng.matmul(o, Vb[k][:, p, g * HD:(g + 1) * HD], sT[:, p, 32 * g:32 * g + 16],
                                   start=(p == 0), stop=False)
                    mm = eng.matmul(o, vtok[0:NS, 4, g * HD:(g + 1) * HD], sT[0:NS, PAGES, 32 * g:32 * g + 16],
                                    start=False, stop=True)
                mm.then_inc(sem("so_ready"), 1)
            eng.wait_ge(sem("poT_kept"), 4 * KVH)
            eng.wait_ge(sem("pT_kept"), 4 * KVH * REP + 1)
            stage_end(eng, "C3a")
            with eng.Fori(0, DB // 2) as i:
                for k in range(2):
                    decode_attention(i * 2 + k, i, k)
            stage_end(eng, "C3")

            u = FIRST_USE["D"]
            with eng.Fori(0, 4) as i:
                for s in range(2):
                    await_slab(eng, s, i + u[s])
                    for j in range(FT):
                        eng.wait_ge(sem("zatt_kept"), i * 4 + (2 * s + j))
                        project_features(s, j * P, j).then_inc(sem("zatt_ready"), 1)
            stage_end(eng, "D")
            stage_end(eng, "D2")

            def project_slot(g, n):
                u = FIRST_USE["E"]
                slot = (0, 1, 2, 0, 1)[n // 2]
                if n % 2 == 0:
                    if slot == 2:
                        eng.wait_ge(sem("bc_loaded"), g * 32 + 32)
                    else:
                        eng.wait_ge(sem(f"slab{slot}_loaded"), g * 32 + 16 * (u[slot] + 1 + n // 6))
                eng.wait_ge(sem("projT_kept"), g * 10 + n)
                project_features(slot, (n % 2) * P, n % 2).then_inc(sem("projT_ready"), 1)

            def turn_x(g, ci):
                R_, ts = ROWS[ci], tok(ci)
                if ci == 0:
                    eng.wait_ge(sem("xact_ready"), g * NJ + NJ)
                    eng.wait_ge(sem("cno_ready"), g + 1)
                if ci >= 1:
                    eng.wait_ge(sem("s_ready"), g * 4 + ci)
                if ci >= 2:
                    eng.wait_ge(sem("c_done"), g * 5 + (ci - 1))
                if ci == 0:
                    eng.wait_ge(sem("c_done"), g * 5)
                for j in range(4):
                    eng.transpose(ps[0:R_, 4, j * P:(j + 1) * P], xact[:, j, ts], ident[:, :])
                eng.transpose(ps[0:R_, 5, 0:P], xact[:, 4, ts], ident[:, :])
                eng.matmul(ps[0:R_, 6, 0:R_], xact[:, 4, ts], xact[:, 5, ts], start=True, stop=True)\
                   .then_inc(sem("a_ready"), 1)

            def await_factors(g, ci):
                eng.wait_ge(sem("m_ready"), g * 5 + (ci + 1))
                eng.wait_ge(sem("xdtd_ready"), g * 5 + (ci + 1))
                if ci < 4:
                    eng.wait_ge(sem("btok_ready"), g * 4 + (ci + 1))
                else:
                    eng.wait_ge(sem("bblk_ready"), g + 1)

            def within_chunk(R_):
                for h in range(GH):
                    mm = eng.matmul(ps[0:R_, 6, h * SP_:(h + 1) * SP_], E[0:R_, h, 0:R_], xdt[0:R_, h, :],
                                    start=True, stop=True)
                return mm

            def scan_chunk(g, ci):
                await_factors(g, ci)
                if ci:
                    eng.wait_ge(sem("s_ready"), g * 4 + ci)
                    eng.matmul(ps[:, 7, :], xact[:, 5, tok(ci)], S, start=True, stop=True)
                eng.matmul(ps[:, 5, :], Btok, xdtd.rearrange("p a b -> p (a b)"), start=True, stop=True)
                within_chunk(P).then_inc(sem("b_ready"), 1)

            def turn_y(g, ci):
                eng.wait_ge(sem("ytok_ready"), g * 5 + (ci + 1))
                if ci < 4:
                    eng.wait_ge(sem("m_ready"), g * 5 + (ci + 2))
                else:
                    eng.wait_ge(sem("st_new"), g * 8 + 8)
                apart(eng)
                for j in range(4):
                    tr = eng.transpose(ps[:, 4, j * P:j * P + ROWS[ci]], ytok[0:ROWS[ci], j * P:(j + 1) * P],
                                       ident[0:ROWS[ci], 0:ROWS[ci]])
                tr.then_inc(sem("y_turned"), 1)

            def turn_tails(g):
                eng.wait_ge(sem("cn_ready"), g + 1)
                eng.wait_ge(sem("c_done"), g * 5)
                for j in range(NJ):
                    dst = ps[0:NC, 7, j * P:(j + 1) * P] if j < 4 else ps[0:NC, 5, (j - 4) * P:(j - 3) * P]
                    tr = eng.transpose(dst, cn[:, j, :], ident[:, :])
                tr.then_inc(sem("tails_turned"), 1)

            def turn_final_state(g):
                eng.wait_ge(sem("s_ready"), g * 4 + 4)
                for j in range(4):
                    tr = eng.transpose(ps[:, 5, j * P:(j + 1) * P], S[:, j * P:(j + 1) * P], ident[:, :])
                tr.then_inc(sem("final_turned"), 1)

            def decode_states(g, half):
                if half == 0:
                    await_factors(g, 4)
                    eng.wait_ge(sem("fsb_ready"), g + 1)
                    eng.wait_ge(sem("c_done"), g * 5 + 4)
                    apart(eng)
                    within_chunk(NS)
                eng.wait_ge(sem("st_in"), g * 128 + 64 * (half + 1))
                eng.wait_ge(sem("cm_ready"), g + 1)
                eng.wait_ge(sem("st_new"), (g * 2 + half) * 4)
                for b in range(4):
                    m = g * 8 + (4 * half + b)
                    if b >= 2:
                        eng.wait_ge(sem("ST_kept"), g * 8 + (4 * half + b - 1))
                    for j in range(4):
                        tr = eng.transpose(ps[:, 4 + b % 2, j * P:(j + 1) * P], st[:, b, j, :], ident[:, :])
                    tr.then_inc(sem("st_turned"), 1)
                    eng.wait_ge(sem("ST_kept"), m + 1)
                    mm = eng.matmul(ps[0:NS, 7, :], Cm[:, 4 * half + b, :], ST[:, b % 2, :],
                                    start=(half == 0 and b == 0), stop=(half == 1 and b == 3))
                    mm.then_inc(sem("st_applied"), 1)
                for j in range(4):
                    if j >= 2:
                        eng.wait_ge(sem("st_new"), g * 8 + (4 * half + j - 1))
                    eng.matmul(ps[:, 4 + j % 2, :], xdtd[0:NS, 2 * j:2 * j + 2, :].rearrange("p a b -> p (a b)"),
                               Bblk[:, 4 * half:4 * half + 4, :].rearrange("p a b -> p (a b)"), start=True, stop=True)\
                       .then_inc(sem("st_added"), 1)

            def sum_squares(g):
                eng.wait_ge(sem("sq_ready"), g + 1)
                for j in range(4):
                    for h in range(2):
                        mm = eng.matmul(ps[:, 6 + h, 0:HALF], ones[:, :], sq[:, j, HALF * h:HALF * (h + 1)],
                                        start=(j == 0), stop=(j == 3))
                mm.then_inc(sem("sumsq_ready"), 1)

            def scan_before(g, n):
                if 3 <= n <= 6:
                    turn_y(g, n - 3)
                if 2 <= n <= 5:
                    scan_chunk(g, n - 2)
                if n == 6:
                    turn_final_state(g)
                    decode_states(g, 0)
                if n == 8:
                    decode_states(g, 1)
                if n == 9:
                    turn_y(g, 4)

            def scan_after(g, n):
                if n == 1:
                    turn_tails(g)
                if 1 <= n <= 5:
                    turn_x(g, n - 1)
                if n == 9:
                    sum_squares(g)

            for n in range(10):
                project_slot(0, n)
            with eng.Fori(1, SG) as i:
                for n in range(10):
                    scan_before(i - 1, n)
                    project_slot(i, n)
                    scan_after(i - 1, n)
            for n in range(10):
                scan_before(SG - 1, n)
                scan_after(SG - 1, n)
            stage_end(eng, "E")

            u = FIRST_USE["F"]
            eng.wait_ge(sem("branch_in"), 32)
            with eng.Fori(0, D_MODEL // SLAB) as i:
                def feat(slot, j, pair, **kw):
                    return project_features(slot, j * P, pair, **kw)
                eng.wait_ge(sem("slab0_loaded"), i * 32 + 16 * (u[0] + 1))
                eng.wait_ge(sem("ya_used"), i * 2)
                for j in range(FT):
                    feat(0, j, j).then_inc(sem("ga_ready"), 1)
                eng.wait_ge(sem("slab1_loaded"), i * 32 + 16 * (u[1] + 1))
                eng.wait_ge(sem("yb_used"), i * 2)
                for j in range(FT):
                    feat(1, j, 2 + j).then_inc(sem("gs_ready"), 1)
                eng.wait_ge(sem("branch_loaded"), i * 16 + 16)
                for j in range(FT):
                    eng.wait_ge(sem("ga_kept"), i * 2 + (j + 1))
                    feat(2, j, j, rhs=yattF).then_inc(sem("ya_ready"), 1)
                eng.wait_ge(sem("slab0_loaded"), i * 32 + 16 * (u[0] + 2))
                for j in range(FT):
                    eng.wait_ge(sem("gs_kept"), i * 2 + (j + 1))
                    mm = feat(0, j, 2 + j, rhs=yssdF, stop=False)
                mm.then_inc(sem("yb1_done"), 1)
                eng.wait_ge(sem("slab1_loaded"), i * 32 + 16 * (u[1] + 2))
                for j in range(FT):
                    feat(1, j, 2 + j, rhs=yssdF, k0=KC, start=False).then_inc(sem("yb_ready"), 1)
            stage_end(eng, "F")

            u = FIRST_USE["G"]
            eng.wait_ge(sem("merged_in"), 16)
            with eng.Fori(0, 4) as i:
                for s in range(2):
                    await_slab(eng, s, i + u[s])
                    for t in range(TT):
                        eng.wait_ge(sem("h_added"), i * 10 + 5 * s)
                        for kc in range(KC):
                            mm = eng.matmul(ps[0:ROWS[t], t, 0:SLAB], mergedT[:, kc, tok(t)], W[:, s, kc, :],
                                            start=(kc == 0), stop=(kc == KC - 1))
                        mm.then_inc(sem("h_ready"), 1)

        @block.scalar
        def _(eng):
            steps = Steps(eng, sem("act_steps"))

            def root(v, n):
                eng.wait_ge(sem("inverse_ready"), n + 1)
                eng.activation(v, v, ACT.Sqrt).then_inc(sem("root_ready"), 1)

            eng.wait_ge(sem("consts_in"), 16 * N_CONST)
            eng.copy(ident_bf[:, :], ident[:, :])
            for t in range(2):
                eng.wait_ge(sem(f"x_in{t}"), 16)
                eng.activation(xsq, xt[:, t, :], ACT.Square, accum_out=sumsq[:, t:t + 1]).then_inc(sem("sumsq_x"), 1)
                root(rstd[:, t:t + 1], t)
            eng.wait_ge(sem("rows_turned"), 2)
            eng.copy(gT[:, :], ps[:, 4, 0:KC]).then_inc(sem("rows_kept"), 1)
            eng.copy(gnT[:, :], ps[:, 4, KC:3 * KC]).then_inc(sem("rows_kept"), 1)
            eng.copy(cwT.rearrange("p (a b) c -> p a (b c)", a=3), ps[:, 5:8, 0:16 * (NSTATE + CW + 1)])\
               .then_inc(sem("rows_kept"), 1)
            for t in range(2, TT):
                eng.wait_ge(sem(f"x_in{t % 2}"), 16 * (t // 2 + 1))
                eng.activation(xsq[0:ROWS[t], :], xt[0:ROWS[t], t % 2, :], ACT.Square,
                               accum_out=sumsq[0:ROWS[t], t:t + 1]).then_inc(sem("sumsq_x"), 1)
                root(rstd[0:ROWS[t], t:t + 1], t)
            stage_end(eng, "A")

            with eng.Fori(0, 5) as i:
                for s in range(2):
                    for t in range(TT):
                        eng.wait_ge(sem("rot_turned"), i * 10 + (5 * s + t + 1))
                        eng.copy(qkT[:, bass.ds(i * 4 + 2 * s, 2), tok(t)],
                                 ps[:, 5 + t % 3, 0:2 * P].rearrange("p (a b) -> p a b", a=2)[:, :, 0:ROWS[t]])\
                           .then_inc(sem("rotT_kept"), 1)
            with eng.Fori(6, 8) as i:
                for s in range(2):
                    for t in range(TT):
                        eng.wait_ge(sem("rot_turned"), i * 10 + (5 * s + t + 1 - 10))
                        eng.copy(qiT[0:ID, bass.ds(i * 8 + (4 * s - 48), 4), tok(t)],
                                 ps[0:ID, 5 + t % 3, :].rearrange("p (a b) -> p a b", a=4)[:, :, 0:ROWS[t]])\
                           .then_inc(sem("rotT_kept"), 1)
            for t in range(3):
                root(lnr[0:ROWS[t], :], ROOTS_B + t)
            eng.wait_ge(sem("dt_ready"), 1)
            steps.add(eng.activation(dtT.rearrange("p (a b) -> p a b", a=2), ps[0:SH, 6:8, 0:HALF], ACT.Identity,
                                     bias=c_dtb[0:SH, :]))
            steps.wait()
            steps.add(eng.activation(dtE, dtT, ACT.Abs))
            eng.wait_ge(sem("alog_in"), 16)
            steps.wait()
            eng.activation(dtE, dtE, ACT.Exp, scale=-1.0).then_inc(sem("dt_exp_ready"), 1)
            eng.activation(c_aneg[0:SH, :], c_alog[0:SH, :], ACT.Exp).then_inc(sem("dt_exp_ready"), 1)
            for t in range(TT):
                if 1 <= t <= 2:
                    root(lnr[0:ROWS[t + 2], :], ROOTS_B + t + 2)
                eng.wait_ge(sem("rot_turned"), 70 + t + 1)
                eng.copy(kiT[:, tok(t)], ps[0:ID, 5, 0:ROWS[t]]).then_inc(sem("rotT_kept"), 1)
            eng.wait_ge(sem("dt_u_ready"), 1)
            eng.activation(dtL, dtU, ACT.Ln).then_inc(sem("dt_ln_ready"), 1)
            eng.wait_ge(sem("dtT_ready"), 2)
            eng.activation(expS, dtU[:, SEQ + DS - 1:NT:DS], ACT.Exp).then_inc(sem("expS_ready"), 1)
            eng.wait_ge(sem("acs_kept"), 2)
            eng.activation(grow_tok[:, 0:4, :], acs_tok[:, 0:4, :], ACT.Exp)
            eng.activation(grow_tok[0:NS, 4, :], acs_tok[0:NS, 4, :], ACT.Exp)
            eng.wait_ge(sem("dec_ready"), 2)
            eng.activation(dec_tok[:, 0:4, :], dec_tok[:, 0:4, :], ACT.Exp)
            eng.activation(dec_tok[0:NS, 4, :], dec_tok[0:NS, 4, :], ACT.Exp)
            eng.activation(cdec[:, :, :], cdec[:, :, :], ACT.Exp)
            stage_end(eng, "B")

            def decode_index(n, k):
                eng.wait_ge(sem("kis_turned"), n + 1)
                eng.copy(kisT[:, k, :], ps[0:ID, 0:2, :].rearrange("p a b -> p (a b)")).then_inc(sem("kisT_kept"), 1)
                eng.wait_ge(sem("sdots_ready"), n + 1)
                eng.activation(srelu[:, k, :], ps[0:IH * DS, 2:5, :].rearrange("p a b -> p (a b)")[:, 0:SKEYS], ACT.Relu)\
                   .then_inc(sem("srelu_ready"), 1)
            with eng.Fori(0, DB // 2) as i:
                for k in range(2):
                    decode_index(i * 2 + k, k)
            stage_end(eng, "C1")

            for qb in range(1, 4):
                n0 = 4 * (qb - 1)
                with eng.Fori(0, IH // 4) as i:
                    for h in range(4):
                        eng.wait_ge(sem("pdots_ready"), (i + n0) * 4 + (h + 1))
                        eng.wait_ge(sem("prelu_used"), (i + n0) * 4)
                        eng.activation(prelu[:, h, 0:P * (qb + 1)], ps[:, h, 0:P * (qb + 1)], ACT.Relu)\
                           .then_inc(sem("pdots_kept"), 1)
            stage_end(eng, "C2")

            eng.wait_ge(sem("selrow_in"), 16)
            eng.copy(selrow, selrow_f)
            for qb in range(4):
                nk = P * (qb + 1)
                with eng.Fori(0, KVH) as g:
                    n = g + KVH * qb
                    eng.wait_ge(sem("p_turned"), n * REP)
                    for r in range(REP):
                        eng.wait_ge(sem("nmx_ready"), n * REP + (r + 1))
                        eng.activation(pexp[:, r, 0:nk], ps[:, r, 0:nk], ACT.Exp, bias=nmx4[:, r:r + 1],
                                       scale=ATT_SCALE, accum_out=rsum4[:, r:r + 1]).then_inc(sem("pexp_ready"), 1)
                    eng.wait_ge(sem("on_turned"), n + 1)
                    eng.copy(qkT[:, bass.ds(g * REP, REP), tok(qb)], ps[:, 7, :].rearrange("p (a b) -> p a b", a=REP))\
                       .then_inc(sem("poT_kept"), 1)
            stage_end(eng, "C3a")

            def decode_attention(n, k):
                for g in (0, 2):
                    eng.wait_ge(sem("kb_turned"), n * KVH + (g + 1))
                    eng.copy(kTb[:, 0, :], ps[:, 0:2, :].rearrange("p a b -> p (a b)")).then_inc(sem("kTb0_kept"), 1)
                eng.wait_ge(sem("snmx_ready"), n + 1)
                eng.wait_ge(sem("s_turned"), n)
                eng.activation(sexp, ps[:, 2:5, :].rearrange("p a b -> p (a b)")[:, 0:SKEYS], ACT.Exp, bias=nmx[:, :],
                               scale=ATT_SCALE, accum_out=rsum[:, :]).then_inc(sem("sraw_ready"), 1)
                eng.wait_ge(sem("s_turned"), n + 1)
                eng.wait_ge(sem("so_ready"), n)
                eng.copy(sT[:, 0:PAGES, :].rearrange("p a b -> p (a b)"), ps[:, 5:7, :].rearrange("p a b -> p (a b)"))
                eng.copy(sT[0:NS, PAGES, :], ps[0:NS, 7, 0:P]).then_inc(sem("sT_kept"), 1)
            with eng.Fori(0, DB // 2) as i:
                for k in range(2):
                    decode_attention(i * 2 + k, k)
            stage_end(eng, "C3")

            with eng.Fori(0, 4) as i:
                for j in range(4):
                    eng.wait_ge(sem("zatt_ready"), i * 4 + (j + 1))
                    eng.wait_ge(sem("zatt_applied"), i * 4 + j)
                    eng.activation(zt[:, j % 2, :].rearrange("p (a b) -> p a b", a=2),
                                   ps[:, 2 * (j % 2):2 * (j % 2) + 2, 0:HALF], ACT.Silu).then_inc(sem("zatt_kept"), 1)
            stage_end(eng, "D")
            stage_end(eng, "D2")

            def keep_slot(g, n):
                pair = 2 * (n % 2)
                eng.wait_ge(sem("projT_ready"), g * 10 + (n + 1))
                if n < NJ:
                    eng.wait_ge(sem("conv_done"), g * NJ)
                    eng.copy(raw[:, n, CW - 1:CW - 1 + HALF], ps[:, pair, 0:HALF])
                    eng.copy(raw[:, n, CW - 1 + HALF:RAW_S], ps[:, pair + 1, 0:SEQ - HALF])
                    eng.copy(raw[:, n, RAW_S:RAW].rearrange("p (b k) -> p b k", b=DB)[:, :, CW - 1:],
                             ps[:, pair + 1, SEQ - HALF:HALF].rearrange("p (b k) -> p b k", b=DB))\
                       .then_inc(sem("projT_kept"), 1)
                else:
                    eng.wait_ge(sem("zs_ready"), g)
                    eng.copy(zraw[:, n - NJ, :].rearrange("p (a b) -> p a b", a=2), ps[:, pair:pair + 2, 0:HALF])\
                       .then_inc(sem("projT_kept"), 1)

            def activate_group(g):
                for j in range(NJ):
                    eng.wait_ge(sem("conv_done"), g * NJ + (j + 1))
                    eng.activation(xact[:, j, 0:SEQ], acc[:, j % 2, 0:SEQ], ACT.Silu)
                    eng.activation(xact[:, j, SEQ:NT].rearrange("p (b k) -> p b k", b=DB), decode_acc(j), ACT.Silu)\
                       .then_inc(sem("xact_ready"), 1)
                eng.wait_ge(sem("projT_kept"), g * 10 + 11)
                eng.activation(zs, zraw, ACT.Silu).then_inc(sem("zs_ready"), 1)

            def state_copies(g, half):
                for b in range(4):
                    eng.wait_ge(sem("st_turned"), g * 8 + (4 * half + b + 1))
                    eng.copy(ST[:, b % 2, :], ps[:, 4 + b % 2, :]).then_inc(sem("ST_kept"), 1)

            def scan_before(g, n):
                if n == 0:
                    activate_group(g)
                if n == 6:
                    eng.wait_ge(sem("final_turned"), g + 1)
                    eng.copy(fsb, ps[:, 5, :]).then_inc(sem("fsb_ready"), 1)
                    state_copies(g, 0)
                if n == 8:
                    state_copies(g, 1)
                if 1 <= n <= 5:
                    R_ = ROWS[n - 1]
                    eng.wait_ge(sem("seg_masked"), g * 5 + n)
                    eng.activation(E[0:R_, :, 0:R_], E[0:R_, :, 0:R_], ACT.Exp).then_inc(sem("decay_ready"), 1)
                if n == 9:
                    eng.wait_ge(sem("c_done"), g * 5 + 5)
                    eng.activation(sq[:, 0:4, :], yT, ACT.Square).then_inc(sem("sq_ready"), 1)

            def scan_after(g, n):
                if n == 9:
                    root(rn, g + ROOTS_E)
                if n == 1:
                    eng.wait_ge(sem("tails_turned"), g + 1)
                    eng.wait_ge(sem("tails_out"), g * 96)
                    eng.copy(cno[:, 0:4 * P], ps[0:NC, 7, :])
                    eng.copy(cno[:, 4 * P:6 * P], ps[0:NC, 5, 0:2 * P]).then_inc(sem("cno_ready"), 1)
                if 1 <= n <= 4:
                    eng.wait_ge(sem("a_ready"), g * 5 + n)
                    eng.copy(Btok, ps[:, 5, 0:P]).then_inc(sem("btok_ready"), 1)

            for n in range(10):
                keep_slot(0, n)
            with eng.Fori(1, SG) as i:
                for n in range(10):
                    scan_before(i - 1, n)
                    keep_slot(i, n)
                    scan_after(i - 1, n)
            for n in range(10):
                scan_before(SG - 1, n)
                scan_after(SG - 1, n)
            stage_end(eng, "E")

            with eng.Fori(0, D_MODEL // SLAB) as i:
                for j in range(FT):
                    eng.wait_ge(sem("ga_ready"), i * 2 + (j + 1))
                    eng.wait_ge(sem("merged_out"), i * 32)
                    eng.activation(gateA[:, j, :].rearrange("p (a b) -> p a b", a=2), ps[:, 2 * j:2 * j + 2, 0:HALF],
                                   ACT.Sigmoid).then_inc(sem("ga_kept"), 1)
                for j in range(FT):
                    eng.wait_ge(sem("gs_ready"), i * 2 + (j + 1))
                    eng.activation(gateS[:, j, :].rearrange("p (a b) -> p a b", a=2), ps[:, 4 + 2 * j:6 + 2 * j, 0:HALF],
                                   ACT.Sigmoid).then_inc(sem("gs_kept"), 1)
            stage_end(eng, "F")

            for t in range(TT):
                eng.wait_ge(sem("h_added"), 8 * TT)
                eng.activation(gsq[0:ROWS[t], :], h_out[0:ROWS[t], t, :], ACT.Square,
                               accum_out=sumsq[0:ROWS[t], t:t + 1]).then_inc(sem("sumsq_h"), 1)
                root(rstd[0:ROWS[t], t:t + 1], ROOTS_G + t)

        @block.vector
        def _(eng):
            steps = Steps(eng, sem("dve_steps"))
            R_S = PAST + NS

            def inverse_rms(dst, src, width, n):
                steps.add(eng.tensor_scalar(dst, src, 1.0 / width, EPS, ALU.mult, ALU.add))
                steps.wait()
                eng.reciprocal(dst, dst).then_inc(sem("inverse_ready"), 1)
                eng.wait_ge(sem("root_ready"), n + 1)

            def keep_xT(t):
                eng.wait_ge(sem("xT_turned"), t + 1)
                eng.wait_ge(sem("rows_kept"), 3)
                for q in range(4):
                    ins = eng.tensor_tensor(xnT[:, 4 * q:4 * q + 4, tok(t)],
                                            ps[:, 4 * (t % 2) + q, :].rearrange("p (a b) -> p a b", a=4)[:, :, 0:ROWS[t]],
                                            bc(gT[:, 4 * q:4 * q + 4], [P, 4, ROWS[t]], 2), ALU.mult)
                ins.then_inc(sem("xnT_kept"), 1)
            for t in range(TT):
                r = ROWS[t]
                eng.wait_ge(sem("sumsq_x"), t + 1)
                inverse_rms(rstd[0:r, t:t + 1], sumsq[0:r, t:t + 1], D_MODEL, t)
                eng.tensor_scalar(xt[0:r, t % 2, :], xt[0:r, t % 2, :], rstd[0:r, t:t + 1], None, ALU.mult)\
                   .then_inc(sem("x_scaled"), 1)
                if t:
                    keep_xT(t - 1)
            keep_xT(TT - 1)
            stage_end(eng, "A")

            def rotate(n, m, t, src, heads, width, tab, free):
                r, hw_ = ROWS[t], width // 2
                cos = bc(rope[0:r, t, tab:tab + hw_], [r, heads * 2, hw_], 1)
                sin = bc(rope[0:r, t, tab + hw_:tab + width], [r, heads * 2, hw_], 1)
                v = src.rearrange("p (a b) -> p a b", b=hw_)
                shaped = lambda x: x[0:r, 0:heads * width].rearrange("p (a b) -> p a b", b=hw_)
                eng.wait_ge(sem("rot_ready"), m)
                eng.tensor_tensor(shaped(tcos), v, cos, ALU.mult)
                eng.tensor_tensor(shaped(tsin), v, sin, ALU.mult).then_inc(sem("tok_kept"), 1)
                eng.wait_ge(sem("tok_kept"), n + 1)
                eng.wait_ge(sem("rot_turned"), m if t == 0 else m - 1)
                free()
                four = lambda x: x[0:r, 0:heads * width].rearrange("p (a two b) -> p a two b", two=2, b=hw_)
                o, c_, s_ = four(rot[:, t % 2, :]), four(tcos), four(tsin)
                eng.tensor_tensor(o[:, :, 0, :], c_[:, :, 0, :], s_[:, :, 1, :], ALU.subtract)
                eng.tensor_tensor(o[:, :, 1, :], c_[:, :, 1, :], s_[:, :, 0, :], ALU.add).then_inc(sem("rot_ready"), 1)

            def rotate_slab(n, m, heads, width, tab, free=lambda t: None):
                for t in range(TT):
                    eng.wait_ge(sem("tok_ready"), n + (t + 1))
                    rotate(n + t, m + t, t, ps[0:ROWS[t], t, 0:SLAB], heads, width, tab, lambda: free(t))

            with eng.Fori(0, 4) as i:
                for s in range(2):
                    rotate_slab(i * 10 + 5 * s, i * 10 + 5 * s, 2, HD, 0)
            rows_out = [0, 0]

            def sent(t):
                eng.wait_ge(sem(f"rot{t % 2}_out"), 16 * rows_out[t % 2])
                rows_out[t % 2] += 1
            for s in range(2):
                rotate_slab(40 + 5 * s, 40 + 5 * s, 2, HD, 0, sent)
            for s in range(2):
                for t in range(TT):
                    eng.wait_ge(sem("tok_ready"), 50 + 5 * s + t + 1)
                    eng.tensor_copy(vtok[0:ROWS[t], t, s * SLAB:(s + 1) * SLAB], ps[0:ROWS[t], t, 0:SLAB])\
                       .then_inc(sem("tok_kept"), 1)
            for k in range(2):
                eng.wait_ge(sem(f"rot{k}_out"), 16 * rows_out[k])
            with eng.Fori(6, 8) as i:
                for s in range(2):
                    rotate_slab(i * 10 + 5 * s, i * 10 + (5 * s - 10), IH // 4, ID, HD)
            for t in range(TT):
                r = ROWS[t]
                eng.wait_ge(sem("tok_ready"), 80 + t + 1)
                src = ps[0:r, t, 0:ID]
                steps.add(eng.bn_stats(lnst[0:r, :], src))
                steps.wait()
                steps.add(eng.bn_aggr(lnagg[0:r, :], lnst[0:r, :]))
                steps.wait()
                inverse_rms(lnr[0:r, :], lnagg[0:r, 1:2], 1, ROOTS_B + t)
                kk = kin[0:r, t % 2, :]
                steps.add(eng.tensor_scalar(kk, src, lnagg[0:r, 0:1], lnr[0:r, :], ALU.subtract, ALU.mult))
                steps.add(eng.tensor_scalar(wi_tok[0:r, t, :], ps[0:r, t, ID:ID + IH], IDX_SCALE, None, ALU.mult))
                steps.wait()
                steps.add(eng.tensor_tensor(kk, kk, lnw[0:r, :], ALU.mult))
                steps.wait()
                steps.add(eng.tensor_tensor(kk, kk, lnb[0:r, :], ALU.add))
                steps.wait()
                rotate(80 + t, 70 + t, t, kk, 1, ID, HD, lambda: sent(t))
            for k in range(2):
                eng.wait_ge(sem(f"rot{k}_out"), 16 * rows_out[k])
            eng.wait_ge(sem("rot_turned"), 75)
            eng.wait_ge(sem("dt_exp_ready"), 2)
            eng.tensor_scalar(dtU, dtE, 1.0, None, ALU.add).then_inc(sem("dt_u_ready"), 1)
            eng.wait_ge(sem("dt_u_ready"), 1)
            steps.add(eng.reciprocal(dtR, dtU))
            steps.add(eng.scalar_tensor_tensor(dtE, dtU, -1.0, dtE, ALU.add, ALU.subtract))
            steps.wait()
            steps.add(eng.tensor_tensor(dtE, dtE, dtR, ALU.mult))
            steps.wait()
            eng.wait_ge(sem("dt_ln_ready"), 1)
            steps.add(eng.tensor_tensor(dtL, dtL, dtE, ALU.subtract))
            steps.wait()
            eng.scalar_tensor_tensor(dtT, dtT, 0.0, dtL, ALU.max, ALU.add).then_inc(sem("dtT_ready"), 1)
            eng.wait_ge(sem("dtT_ready"), 1)
            steps.add(eng.tensor_scalar(dtE, dtT, c_aneg[0:SH, :], -1.0, ALU.mult, ALU.mult))
            steps.add(eng.memset(dtL, 1.0))
            steps.wait()
            steps.add(eng.memset(dtL[:, 0:SEQ:P], 0.0))
            steps.add(eng.memset(dtL[:, SEQ:NT:DS], 0.0))
            steps.wait()
            eng.tensor_tensor_scan(dtU, dtL, dtE, 0.0, ALU.mult, ALU.add).then_inc(sem("dtT_ready"), 1)
            for k, dst in enumerate((dt_tok, acs_tok)):
                eng.wait_ge(sem("dt_turned"), k + 1)
                eng.tensor_copy(dst[:, 0:4, :], ps[:, k, 0:4 * SH].rearrange("p (a b) -> p a b", a=4))
                eng.tensor_copy(dst[0:NS, 4, :], ps[0:NS, k, 4 * SH:5 * SH]).then_inc(sem("acs_kept"), 1)
            eng.wait_ge(sem("last_in"), 32)
            eng.tensor_tensor(dec_tok[:, 0:4, :], cdec[:, :, :], acs_tok[:, 0:4, :], ALU.subtract).then_inc(sem("dec_ready"), 1)
            eng.tensor_tensor(dec_tok[0:NS, 4, :], dec_tok[0:NS, 4, :], acs_tok[0:NS, 4, :], ALU.subtract)\
               .then_inc(sem("dec_ready"), 1)
            eng.wait_ge(sem("decS_ready"), 1)
            eng.tensor_copy(decS.rearrange("p a b -> p (a b)"), ps[:, 2, 0:SH // 2 * DB])
            stage_end(eng, "B")

            eng.wait_ge(sem("idx_consts_in"), 32)
            eng.wait_ge(sem("wcol_in"), 16 * DB)

            def decode_index(n, k):
                eng.wait_ge(sem("sscore_added"), n)
                apart(eng)
                eng.tensor_copy(qis[:, k * IH * DS:(k + 1) * IH * DS].rearrange("p (a b) -> p a b", a=IH),
                                qiT[0:ID, :, bass.ds(n * DS + SEQ, DS)])
                eng.tensor_tensor(hw[:, k, :], headmask[:, bass.ds(n, 1), :].rearrange("p a b -> p (a b)"),
                                  wcol[:, bass.ds(n, 1)].to_broadcast([IH * DS, NS]), ALU.mult)\
                   .then_inc(sem("qis_ready"), 1)
            with eng.Fori(0, DB // 2) as i:
                for k in range(2):
                    decode_index(i * 2 + k, k)
            eng.wait_ge(sem("sscore_added"), DB + 1)
            eng.tensor_copy(ssc, ps[0:NS, 5:8, :].rearrange("p a b -> p (a b)")[:, 0:SKEYS])
            stage_end(eng, "C1")

            steps.add(eng.memset(psc, 0.0))
            steps.wait()
            for qb in range(1, 4):
                steps.add(eng.tensor_copy(psc[:, qb - 1, qb * P:(qb + 1) * P], causal_q[:, :]))
            steps.wait()
            for qb in range(1, 4):
                nk, n0 = P * (qb + 1), 4 * (qb - 1)
                row = psc[:, qb - 1, 0:nk]
                with steps.loop(0, IH // 4, 1) as i:
                    eng.wait_ge(sem("pdots_ready"), (i + n0) * 4)
                    steps.add(eng.tensor_copy(wi4, wi_tok[:, qb, bass.ds(i * 4, 4)]))
                    eng.tensor_copy(qist, qiT[0:ID, bass.ds(i * 4, 4), tok(qb)]).then_inc(sem("qist_ready"), 1)
                    steps.wait()
                    for h in range(4):
                        eng.wait_ge(sem("pdots_kept"), (i + n0) * 4 + (h + 1))
                        eng.scalar_tensor_tensor(row, prelu[:, h, 0:nk], wi4[:, h:h + 1], row, ALU.mult, ALU.add)\
                           .then_inc(sem("prelu_used"), 1)
                        eng.wait_ge(sem("prelu_used"), (i + n0) * 4 + (h + 1))

            def take_top(v, r, k):
                with steps.loop(0, k // 8, 2):
                    steps.add(eng.max(top8[0:r, :], v))
                    steps.wait()
                    apart(eng)
                    steps.add(eng.match_replace(v, top8[0:r, :], v, PICKED))
                    steps.wait()
            for qb in range(1, 4):
                nk = P * (qb + 1)
                take_top(psc[:, qb - 1, 0:nk], P, TOPK_P)
                eng.tensor_scalar(pmask[:, qb, 0:nk], psc[:, qb - 1, 0:nk], PICKED, NEG, ALU.not_equal, ALU.mult)
            eng.tensor_copy(pmask[:, 0, 0:P], causal_q[:, :])
            take_top(ssc, NS, TOPK_S)
            eng.tensor_scalar(smask, ssc, PICKED, NEG, ALU.not_equal, ALU.mult)
            stage_end(eng, "C2")

            for qb in range(4):
                nk = P * (qb + 1)
                with steps.loop(0, KVH, REP + 1) as g:
                    n = g + KVH * qb
                    eng.wait_ge(sem("pscore_ready"), n * REP)
                    eng.wait_ge(sem("poT_kept"), n)
                    apart(eng)
                    eng.tensor_copy(qst, qkT[:, bass.ds(g * REP, REP), tok(qb)]).then_inc(sem("qst_ready"), 1)
                    for r in range(REP):
                        eng.wait_ge(sem("pscore_ready"), n * REP + (r + 1))
                        steps.add(eng.tensor_reduce(mx4[:, r:r + 1], ps[:, r, 0:nk], AX.X, ALU.max))
                        steps.wait()
                        eng.tensor_scalar(nmx4[:, r:r + 1], mx4[:, r:r + 1], -ATT_SCALE, None, ALU.mult)\
                           .then_inc(sem("nmx_ready"), 1)
                    for r in range(REP):
                        eng.wait_ge(sem("p_turned"), n * REP + (r + 1))
                        eng.tensor_copy(pT[:, r % 2, 0:nk], ps[:, 4 + r % 2, 0:nk]).then_inc(sem("pT_kept"), 1)
                    eng.wait_ge(sem("pexp_ready"), n * REP + REP)
                    steps.add(eng.reciprocal(rinv4, rsum4))
                    steps.wait()
                    eng.wait_ge(sem("po_ready"), n * REP + REP)
                    eng.wait_ge(sem("on_turned"), n)
                    eng.tensor_tensor(on, ps[:, 6, :].rearrange("p (a b) -> p a b", a=REP), bc(rinv4, [P, REP, HD], 2),
                                      ALU.mult).then_inc(sem("on_ready"), 1)
            stage_end(eng, "C3a")

            steps.add(eng.memset(qsb[:, :, REP * DS:], 0.0))
            steps.wait()

            def decode_attention(n, k):
                eng.wait_ge(sem("so_ready"), n)
                apart(eng)
                eng.tensor_copy(selst, selrow[:, bass.ds(n, 1), :].rearrange("p a b -> p (a b)"))
                eng.tensor_copy(qsb[:, :, 0:REP * DS].rearrange("p g (r d) -> p g r d", d=DS),
                                qkT[:, 0:QH, bass.ds(n * DS + SEQ, DS)].rearrange("p (g r) d -> p g r d", r=REP))\
                   .then_inc(sem("qsb_ready"), 1)
                for g in (1, 3):
                    eng.wait_ge(sem("kb_turned"), n * KVH + (g + 1))
                    eng.tensor_copy(kTb[:, 1, :], ps[:, 5:7, :].rearrange("p a b -> p (a b)")).then_inc(sem("kTb1_kept"), 1)
                eng.wait_ge(sem("dscore_done"), n * KVH + KVH)
                steps.add(eng.tensor_reduce(mx[:, :], ps[:, 2:5, :].rearrange("p a b -> p (a b)")[:, 0:SKEYS], AX.X, ALU.max))
                steps.wait()
                eng.tensor_scalar(nmx[:, :], mx[:, :], -ATT_SCALE, None, ALU.mult).then_inc(sem("snmx_ready"), 1)
                eng.wait_ge(sem("sraw_ready"), n + 1)
                steps.add(eng.reciprocal(rinv[:, :], rsum[:, :]))
                steps.wait()
                eng.tensor_scalar(sexp, sexp, rinv[:, :], None, ALU.mult).then_inc(sem("sexp_ready"), 1)
                eng.wait_ge(sem("so_ready"), n + 1)
                apart(eng)
                eng.tensor_copy(qkT[:, 0:QH, bass.ds(n * DS + SEQ, DS)],
                                ps[:, 0, 0:QH * DS].rearrange("p (a b) -> p a b", a=QH)).then_inc(sem("so_kept"), 1)
            with steps.loop(0, DB // 2, 4) as i:
                for k in range(2):
                    decode_attention(i * 2 + k, k)
            stage_end(eng, "C3")

            with eng.Fori(0, 4) as i:
                for j in range(4):
                    eng.wait_ge(sem("zatt_kept"), i * 4 + (j + 2))
                    o = qkT[:, bass.ds(i * 4 + j, 1), :].rearrange("p a b -> p (a b)")
                    eng.tensor_tensor(o, o, zt[:, j % 2, :], ALU.mult).then_inc(sem("zatt_applied"), 1)
            stage_end(eng, "D")
            stage_end(eng, "D2")

            eng.memset(raw[:, :, 0:CW - 1], 0.0)
            decode_raw = raw[:, :, RAW_S:RAW].rearrange("p j (b k) -> p j b k", b=DB)

            def convolve(g):
                eng.wait_ge(sem("yn_done"), g)
                steps.add(eng.tensor_copy(cw_g[:, 0:4, :], cwT[:, bass.ds(g * 4, 4), :]))
                steps.add(eng.tensor_copy(cw_g[:, 4:5, :], cwT[:, bass.ds(g + 4 * SG, 1), :]))
                steps.add(eng.tensor_copy(cw_g[:, 5:6, :], cwT[:, bass.ds(g + 5 * SG, 1), :]))
                steps.add(eng.tensor_copy(gn_g, gnT[:, bass.ds(g * 4, 4)]))
                steps.wait()
                for b in range(2):
                    steps.add(eng.tensor_copy(decode_raw[:, :, 4 * b:4 * b + 4, 0:CW - 1],
                                              cw_g[:, :, 12 * b:12 * b + 12].rearrange("p j (b k) -> p j b k", b=4)))
                steps.wait()
                eng.wait_ge(sem("projT_kept"), g * 10 + (NJ + 1))
                eng.wait_ge(sem("tails_turned"), g)
                eng.tensor_copy(cn[:, :, 0:CW - 1], raw[:, :, RAW_S - (CW - 1):RAW_S])
                eng.tensor_copy(cn[:, :, CW - 1:].rearrange("p j (b k) -> p j b k", b=DB), decode_raw[:, :, :, DS:])\
                   .then_inc(sem("cn_ready"), 1)
                eng.wait_ge(sem("final_out"), g * 16)
                for j in range(NJ):
                    eng.wait_ge(sem("xact_ready"), g * NJ + max(j - 1, 0))
                    at_ = acc[:, j % 2, 0:ACC]
                    tap = lambda k: cw_g[:, j, NSTATE + k:NSTATE + k + 1]
                    steps.add(eng.tensor_scalar(at_, raw[:, j, 0:ACC], tap(0), tap(CW), ALU.mult, ALU.add))
                    for k in range(1, CW):
                        steps.wait()
                        ins = eng.scalar_tensor_tensor(at_, raw[:, j, k:k + ACC], tap(k), at_, ALU.mult, ALU.add)
                        if k < CW - 1:
                            steps.add(ins)
                    ins.then_inc(sem("conv_done"), 1)

            per_head = lambda v, r: bc(v, [r, GH, SP_], 2)
            heads = lambda ap: ap.rearrange("p (a b) -> p a b", a=GH)

            def gate_chunk(g, ci):
                eng.wait_ge(sem("y_turned"), g * 5 + (ci + 1))
                if ci == 0:
                    eng.wait_ge(sem("yn_out"), g * 16)
                    eng.wait_ge(sem("zs_ready"), g + 1)
                eng.tensor_tensor(yT[:, :, tok(ci)], ps[:, 4, :].rearrange("p (a b) -> p a b", a=4)[:, :, 0:ROWS[ci]],
                                  zs[:, :, tok(ci)], ALU.mult).then_inc(sem("c_done"), 1)

            def finish_chunk(g, ci):
                r = ROWS[ci]
                y = heads(ytok[0:r, :])
                if ci < 4:
                    eng.wait_ge(sem("b_ready"), g * 4 + (ci + 1))
                else:
                    eng.wait_ge(sem("st_applied"), g * 8 + 8)
                ins = eng.tensor_tensor(y, heads(ps[0:r, 6, :]), xD[0:r], ALU.add)
                if ci:
                    steps.add(ins)
                    steps.wait()
                    steps.add(eng.tensor_tensor(xD[0:r], heads(ps[0:r, 7, :]),
                                                per_head(grow_tok[0:r, ci, bass.ds(g * GH, GH)], r), ALU.mult))
                    steps.wait()
                    ins = eng.tensor_tensor(y, y, xD[0:r], ALU.add)
                ins.then_inc(sem("ytok_ready"), 1)
                if ci == 0:
                    eng.tensor_copy(S, ps[:, 5, :]).then_inc(sem("s_ready"), 1)
                elif ci < 4:
                    steps.add(eng.tensor_tensor(heads(S), heads(S), per_head(cdec[:, ci, bass.ds(g * GH, GH)], P), ALU.mult))
                    steps.wait()
                    eng.tensor_tensor(S, S, ps[:, 5, :], ALU.add).then_inc(sem("s_ready"), 1)

            def segment_sums(g, ci):
                r = ROWS[ci]
                if ci == 0:
                    eng.wait_ge(sem("acs_in"), g * 16 + 16)
                eng.tensor_tensor(E[0:r, :, 0:r], acsbc[0:r, :, tok(ci)],
                                  bc(acs_tok[0:r, ci, bass.ds(g * GH, GH)], [r, GH, r], 2), ALU.subtract)\
                   .then_inc(sem("seg_ready"), 1)

            def factors(g, ci):
                r = ROWS[ci]
                eng.wait_ge(sem("a_ready"), g * 5 + (ci + 1))
                x = heads(ps[0:r, 4, :])
                eng.tensor_tensor(xdt[0:r], x, per_head(dt_tok[0:r, ci, bass.ds(g * GH, GH)], r), ALU.mult)\
                   .then_inc(sem("xdt_ready"), 1)
                steps.add(eng.tensor_tensor(xD[0:r], x, per_head(dskip[0:r, bass.ds(g * GH, GH)], r), ALU.mult))
                if ci == 4:
                    eng.tensor_tensor(Bblk, bc(ps[0:NS, 5, 0:NST], [NS, DB, NST], 1), bc(in_batch[:, :], [NS, DB, NST], 2),
                                      ALU.mult).then_inc(sem("bblk_ready"), 1)
                mask = causal_k[:, :] if ci < 4 else dec_k[:, :]
                steps.add(eng.tensor_tensor(cbm[0:r, 0:r], ps[0:r, 6, 0:r], mask, ALU.mult))
                steps.wait()
                eng.wait_ge(sem("decay_ready"), g * 5 + (ci + 1))
                eng.tensor_tensor(E[0:r, :, 0:r], E[0:r, :, 0:r], bc(cbm[0:r, 0:r], [r, GH, r], 1), ALU.mult)\
                   .then_inc(sem("m_ready"), 1)

            def new_states(g, half):
                eng.wait_ge(sem("st_applied"), g * 8 + (4 * half + 4))
                for b in range(4):
                    ins = eng.tensor_tensor(st[:, b], st[:, b],
                                            bc(decS[:, bass.ds(g * 4, 4), 4 * half + b:4 * half + b + 1]
                                               .rearrange("p a b -> p (a b)"), [P, 4, NST], 2), ALU.mult)
                steps.add(ins)
                steps.wait()
                for j in range(4):
                    eng.wait_ge(sem("st_added"), g * 8 + (4 * half + j + 1))
                    eng.tensor_tensor(st[:, :, j, :], st[:, :, j, :],
                                      ps[:, 4 + j % 2, :].rearrange("p (a b) -> p a b", a=4), ALU.add)\
                       .then_inc(sem("st_new"), 1)

            def normalise(g):
                eng.wait_ge(sem("sumsq_ready"), g + 1)
                inverse_rms(rn, ps[:, 6:8, 0:HALF], D_INNER // SG, g + ROOTS_E)
                for j in range(4):
                    ins = eng.scalar_tensor_tensor(yT[:, j, :], yT[:, j, :], gn_g[:, j:j + 1], rn_row, ALU.mult, ALU.mult)
                ins.then_inc(sem("yn_done"), 1)

            def scan_before(g, n):
                if n == 0:
                    convolve(g)
                if 3 <= n <= 6:
                    gate_chunk(g, n - 3)
                if 2 <= n <= 5:
                    finish_chunk(g, n - 2)
                if 1 <= n <= 5:
                    segment_sums(g, n - 1)
                if n == 6:
                    new_states(g, 0)
                if n == 8:
                    finish_chunk(g, 4)
                    new_states(g, 1)
                if n == 9:
                    gate_chunk(g, 4)

            def scan_after(g, n):
                if n == 1:
                    eng.wait_ge(sem("xact_ready"), g * NJ + NJ)
                    eng.tensor_tensor(Cm, bc(xact[:, 5, SEQ:NT], [P, DB, NS], 1), batch_cols[:, :, :], ALU.mult)\
                       .then_inc(sem("cm_ready"), 1)
                if 1 <= n <= 5:
                    factors(g, n - 1)
                if n == 9:
                    normalise(g)

            SCAN_STEPS = 48
            with steps.loop(0, SG, SCAN_STEPS) as g:
                for n in range(10):
                    scan_before(g, n)
                    scan_after(g, n)
            stage_end(eng, "E")

            with eng.Fori(0, D_MODEL // SLAB) as i:
                for j in range(FT):
                    eng.wait_ge(sem("ya_ready"), i * 2 + (j + 1))
                    eng.tensor_tensor(gateA[:, j, :].rearrange("p (a b) -> p a b", a=2),
                                      gateA[:, j, :].rearrange("p (a b) -> p a b", a=2), ps[:, 2 * j:2 * j + 2, 0:HALF],
                                      ALU.mult).then_inc(sem("ya_used"), 1)
                for j in range(FT):
                    eng.wait_ge(sem("yb_ready"), i * 2 + (j + 1))
                    eng.tensor_tensor(gateS[:, j, :].rearrange("p (a b) -> p a b", a=2),
                                      gateS[:, j, :].rearrange("p (a b) -> p a b", a=2), ps[:, 4 + 2 * j:6 + 2 * j, 0:HALF],
                                      ALU.mult).then_inc(sem("yb_used"), 1)
                    eng.wait_ge(sem("yb_used"), i * 2 + (j + 1))
                    eng.tensor_tensor(gateA[:, j, :], gateA[:, j, :], gateS[:, j, :], ALU.add)\
                       .then_inc(sem("merged_ready"), 1)
            stage_end(eng, "F")

            for k in range(2):
                eng.wait_ge(sem("resid_in"), 32)
            with eng.Fori(0, 4) as i:
                for s in range(2):
                    for t in range(TT):
                        eng.wait_ge(sem("h_ready"), i * 10 + (5 * s + t + 1))
                        h = h_out[0:ROWS[t], t, bass.ds(i * (2 * SLAB) + s * SLAB, SLAB)]
                        eng.tensor_tensor(h, h, ps[0:ROWS[t], t, 0:SLAB], ALU.add).then_inc(sem("h_added"), 1)
            eng.wait_ge(sem("fg_in"), 16)
            for t in range(TT):
                r = ROWS[t]
                eng.wait_ge(sem("sumsq_h"), t + 1)
                inverse_rms(rstd[0:r, t:t + 1], sumsq[0:r, t:t + 1], D_MODEL, ROOTS_G + t)
                eng.scalar_tensor_tensor(h_out[0:r, t, :], h_out[0:r, t, :], rstd[0:r, t:t + 1], fg_bc[0:r, :],
                                         ALU.mult, ALU.mult).then_inc(sem("y_ready"), 1)

        @block.gpsimd
        def _(eng):
            (y_p, y_s, k_p, v_p, ki_p, ssm_p, conv_p, k_s, v_s, ki_s, ssm_s, conv_s) = out
            for name in ("rotT_kept", "pT_kept", "zatt_kept", "zatt_applied", "projT_kept", "sscore_added"):
                eng.sem_inc(sem(name), 1)
            eng.memset(ones[:, :], 1.0)
            stage_end(eng, "A")
            flat = lambda ap: ap.rearrange("b t h d -> (b t) (h d)")
            kp, ks_, vp, vs = flat(k_p[0]), flat(k_s[0]), flat(v_p[0]), flat(v_s[0])
            kip, kis = ki_p[0, 0], ki_s[0].rearrange("b t d -> (b t) d")
            rows = lambda p_, s_, t: p_[tok(t), :] if t < 4 else s_
            for s in range(2):
                for t in range(TT):
                    eng.wait_ge(sem("rot_ready"), 40 + 5 * s + t + 1)
                    eng.dma_start(rows(kp, ks_, t)[:, s * SLAB:(s + 1) * SLAB], rot[0:ROWS[t], t % 2, :])\
                       .then_inc(sem(f"rot{t % 2}_out"), 16)
            eng.wait_ge(sem("tok_kept"), 60)
            eng.dma_start(vp.rearrange("(a p) n -> p a n", p=P), vtok[:, 0:4, :]).then_inc(sem("v_out"), 16)
            eng.dma_start(vs, vtok[0:NS, 4, :]).then_inc(sem("v_out"), 16)
            for t in range(TT):
                eng.wait_ge(sem("rot_ready"), 70 + t + 1)
                eng.dma_start(rows(kip, kis, t), rot[0:ROWS[t], t % 2, 0:ID]).then_inc(sem(f"rot{t % 2}_out"), 16)
            eng.wait_ge(sem("dtT_ready"), 2)
            eng.dma_start(acsT_dram, dtU).then_inc(sem("acsT_out"), 16)
            eng.wait_ge(sem("acs_kept"), 2)
            eng.dma_start(acs_dram[0:4].rearrange("t p n -> p t n"), acs_tok[:, 0:4, :]).then_inc(sem("acs_out"), 16)
            eng.dma_start(acs_dram[4, 0:NS, :], acs_tok[0:NS, 4, :]).then_inc(sem("acs_out"), 16)
            eng.dma_start(wi_dram, wi_tok[0:NS, 4, :]).then_inc(sem("acs_out"), 16)
            eng.wait_ge(sem("acs_out"), 48)
            eng.dma_start(cdec[:, :, :], acs_dram[0:4, P - 1, :].partition_broadcast(P)).then_inc(sem("last_in"), 16)
            eng.dma_start(dec_tok[0:NS, 4, :],
                          bc(acs_dram[4, DS - 1:NS:DS, :], [DB, DS, SH], 1)).then_inc(sem("last_in"), 16)
            eng.wait_ge(sem("rot0_out"), 16 * (6 + 3))
            eng.wait_ge(sem("rot1_out"), 16 * (4 + 2))
            eng.wait_ge(sem("v_out"), 32)
            eng.wait_ge(sem("acsT_out"), 16)
            stage_end(eng, "B")

            cache_ki = a["cache_idx_k"][0]
            eng.dma_start(headmask, c["headmask"]).then_inc(sem("idx_consts_in"), 16)
            eng.dma_start(dec_q, c["dec_q"]).then_inc(sem("idx_consts_in"), 16)
            for b in range(DB):
                eng.dma_start(wcol[:, b:b + 1], wi_dram[b * DS:(b + 1) * DS, :].rearrange("t h -> h t"),
                              allow_slow_non_contiguous=True)\
                   .then_inc(sem("wcol_in"), 16)

            def page_of(n, p):
                return eng.value_load(pt_sb[0:1, bass.ds(n * PAGES + p, 1)], min_val=0, max_val=NPHYS - 1)

            def index_pages(n, k):
                for p in range(PAGES):
                    eng.dma_start(kidx[:, k, p * ID:(p + 1) * ID], cache_ki[bass.ds(page_of(n, p), 1)]
                                  .rearrange("a p n -> (a p) n")).then_inc(sem(f"kidx{k}_in"), 16)
            for k in range(2):
                index_pages(k, k)
            with eng.Fori(1, DB // 2) as i:
                for k in range(2):
                    eng.wait_ge(sem("kis_turned"), i * 2 + (k - 1))
                    index_pages(i * 2 + k, k)
            stage_end(eng, "C1")
            stage_end(eng, "C2")
            eng.dma_start(selrow_f, c["selrow"]).then_inc(sem("selrow_in"), 16)
            stage_end(eng, "C3a")

            ck, cv = (a[x][0].rearrange("n p h d -> n p (h d)") for x in ("cache_k", "cache_v"))

            def kv_pages(n, k):
                for name, cache, dst in (("kpage", ck, lambda p: Kb[:, k * PAGES + p, :]), ("vpage", cv, lambda p: Vb[k][:, p, :])):
                    for p in range(PAGES):
                        eng.dma_start(dst(p), cache[bass.ds(page_of(n, p), 1)].rearrange("a p n -> (a p) n"))\
                           .then_inc(sem(f"{name}{k}_in"), 16)
            for k in range(2):
                kv_pages(k, k)
            with eng.Fori(1, DB // 2) as i:
                for k in range(2):
                    eng.wait_ge(sem("so_ready"), i * 2 + (k - 1))
                    kv_pages(i * 2 + k, k)
            stage_end(eng, "C3")
            stage_end(eng, "D")
            eng.dma_start(yatt_dram, qkT[:, 0:QH, :].rearrange("p a b -> p (a b)")).then_inc(sem("yatt_out"), 16)
            eng.wait_ge(sem("yatt_out"), 16)
            stage_end(eng, "D2")

            state_in = a["state_ssm"][0].rearrange("b (t q) p n -> b t (q p) n", q=2)
            state_out = ssm_s[0].rearrange("b (t q) p n -> b t (q p) n", q=2)
            final_out = ssm_p[0, 0].rearrange("(t q) p n -> t (q p) n", q=2)
            conv_rows = conv_s[0].rearrange("b k n -> (b k) n")

            def state_loads(g, half):
                for b in range(4):
                    eng.dma_start(st[:, b], state_in[4 * half + b, bass.ds(g * 4, 4)].rearrange("t q n -> q t n"))\
                       .then_inc(sem("st_in"), 16)

            def state_stores(g, half):
                eng.wait_ge(sem("st_new"), g * 8 + (4 * half + 4))
                apart(eng)
                for b in range(4):
                    eng.dma_start(state_out[4 * half + b, bass.ds(g * 4, 4)].rearrange("t q n -> q t n"), st[:, b])\
                       .then_inc(sem("st_out"), 16)
                eng.wait_ge(sem("st_out"), g * 128 + (64 * half + 64))

            def chunk_work(g, ci):
                r = ROWS[ci]
                mask = causal_k[:, :] if ci < 4 else dec_k[:, :]
                eng.wait_ge(sem("seg_ready"), g * 5 + (ci + 1))
                eng.tensor_tensor(E[0:r, :, 0:r], E[0:r, :, 0:r], bc(mask, [r, GH, r], 1), ALU.mult)\
                   .then_inc(sem("seg_masked"), 1)
                eng.wait_ge(sem("xdt_ready"), g * 5 + (ci + 1))
                eng.tensor_tensor(xdtd[0:r], xdt[0:r], bc(dec_tok[0:r, ci, bass.ds(g * GH, GH)], [r, GH, SP_], 2), ALU.mult)\
                   .then_inc(sem("xdtd_ready"), 1)

            with eng.Fori(0, SG) as g:
                eng.wait_ge(sem("yn_done"), g)
                apart(eng)
                eng.dma_start(acsbc, acsT_dram[bass.ds(g * GH, GH), :].partition_broadcast(P)).then_inc(sem("acs_in"), 16)
                state_loads(g, 0)
                for ci in range(5):
                    chunk_work(g, ci)
                    if ci == 0:
                        eng.wait_ge(sem("cno_ready"), g + 1)
                        for c0, w, col in ((0, 4 * P, g * (4 * P)), (4 * P, P, g * P + D_INNER),
                                           (5 * P, P, g * P + (D_INNER + SG * NST))):
                            apart(eng)
                            eng.dma_start(conv_p[0, 0, :, bass.ds(col, w)], cno[0:CW - 1, c0:c0 + w])\
                               .then_inc(sem("tails_out"), 16)
                            eng.dma_start(conv_rows[:, bass.ds(col, w)], cno[CW - 1:NC, c0:c0 + w])\
                               .then_inc(sem("tails_out"), 16)
                eng.wait_ge(sem("fsb_ready"), g + 1)
                apart(eng)
                eng.dma_start(final_out[bass.ds(g * 4, 4)].rearrange("t q n -> q t n"),
                              fsb.rearrange("p (t n) -> p t n", t=4)).then_inc(sem("final_out"), 16)
                state_stores(g, 0)
                state_loads(g, 1)
                state_stores(g, 1)
                eng.wait_ge(sem("yn_done"), g + 1)
                apart(eng)
                eng.dma_start(yssd_dram[:, bass.ds(g * (4 * NT), 4 * NT)], yT.rearrange("p a b -> p (a b)"))\
                   .then_inc(sem("yn_out"), 16)
            eng.wait_ge(sem("yn_out"), 16 * SG)
            eng.wait_ge(sem("tails_out"), 96 * SG)
            eng.wait_ge(sem("final_out"), 16 * SG)
            stage_end(eng, "E")

            eng.dma_start(yattF.rearrange("p a b -> p (a b)"), yatt_dram).then_inc(sem("branch_in"), 16)
            eng.dma_start(yssdF.rearrange("p a b -> p (a b)"), yssd_dram).then_inc(sem("branch_in"), 16)
            with eng.Fori(0, D_MODEL // SLAB) as i:
                for j in range(FT):
                    eng.wait_ge(sem("merged_ready"), i * 2 + (j + 1))
                    apart(eng)
                    eng.dma_start(merged_dram[:, bass.ds(i * (2 * NT) + j * NT, NT)], gateA[:, j, :])\
                       .then_inc(sem("merged_out"), 16)
            eng.wait_ge(sem("merged_out"), 2 * 16 * (D_MODEL // SLAB))
            stage_end(eng, "F")

            eng.dma_start(mergedT.rearrange("p a b -> p (a b)"), merged_dram).then_inc(sem("merged_in"), 16)
            eng.dma_start(h_out[:, 0:4, :], a["x_prompt"][0].rearrange("(t p) n -> p t n", p=P)).then_inc(sem("resid_in"), 16)
            eng.dma_start(h_out[0:NS, 4, :], a["x_sample"].rearrange("b t d -> (b t) d")).then_inc(sem("resid_in"), 16)
            eng.dma_start(fg_bc, a["final_norm_g"].partition_broadcast(P)).then_inc(sem("fg_in"), 16)
            for t in range(TT):
                eng.wait_ge(sem("y_ready"), t + 1)
                eng.dma_start(y_p[0, tok(t), :] if t < 4 else y_s.rearrange("b t d -> (b t) d"), h_out[0:ROWS[t], t, :])\
                   .then_inc(sem("y_out"), 16)
            eng.wait_ge(sem("y_out"), 16 * TT)


_NAMES = ["x_prompt", "x_sample", "cache_k", "cache_v", "cache_idx_k", "state_ssm", "state_conv", "page_table",
          "norm_g", "w_in", "conv_w", "conv_b", "dt_bias", "a_log", "d_skip", "ssd_norm_g", "idx_ln_w", "idx_ln_b",
          "w_branch", "w_out", "final_norm_g"]
_OUTS = [(1, SEQ, D_MODEL), (DB, DS, D_MODEL), (1, 1, SEQ, KVH, HD), (1, 1, SEQ, KVH, HD), (1, 1, SEQ, ID),
         (1, 1, SH, SP_, NST), (1, 1, CW - 1, CONV_DIM), (1, DB, DS, KVH, HD), (1, DB, DS, KVH, HD), (1, DB, DS, ID),
         (1, DB, SH, SP_, NST), (1, DB, CW - 1, CONV_DIM)]


def kernel(**inputs):
    import concourse.bacc as bacc
    from concourse.bass_utils import run_bass_kernel_spmd

    nc = bacc.Bacc("TRN2", target_bir_lowering=False, num_devices=1)
    arrays = {}

    def given(prefix, name, value):
        value = np.ascontiguousarray(value)
        arrays[prefix + name] = value
        return nc.dram_tensor(prefix + name, value.shape, mybir.dt.from_np(value.dtype), kind="ExternalInput").ap()
    a = {name: given("in_", name, inputs[name]) for name in _NAMES}
    c = {name: given("const_", name, value) for name, value in constant_arrays().items()}
    out = [nc.dram_tensor(f"out_{i}", shape, F32, kind="ExternalOutput").ap() for i, shape in enumerate(_OUTS)]
    build(nc, a, out, c)
    r = run_bass_kernel_spmd(nc, [arrays], core_ids=[0])
    return tuple(r.results[0][f"out_{i}"] for i in range(len(_OUTS)))
```

```python
from contextlib import ExitStack

import numpy as np
import concourse.bass as bass
import concourse.mybir as mybir

ALU = mybir.AluOpType
ACT = mybir.ActivationFunctionType
AX = mybir.AxisListType
F32 = mybir.dt.float32
BF16 = mybir.dt.bfloat16
I32 = mybir.dt.int32

P = 128
D_MODEL = 2048
KC = D_MODEL // P
SEQ = 512
DB, DS = 8, 4
NS = DB * DS
NT = SEQ + NS
HALF = NT // 2
TT = 5
ROWS = [P, P, P, P, NS]
PAGES, PAGE = 8, 128
PAST = PAGES * PAGE
NPHYS = DB * PAGES * 5 // 4
SKEYS = PAST + NS
HD = 128
QH, KVH = 16, 4
REP = QH // KVH
IH, ID = 16, 64
IDX_SCALE = IH ** -0.5 * ID ** -0.5
ATT_SCALE = HD ** -0.5
TOPK_P = SEQ // 4
TOPK_S = 256
THETA = 10000.0
D_INNER = 4096
SH, SP_ = 64, 64
SG = 8
GH = SH // SG
NST = 128
CW = 4
CONV_DIM = D_INNER + 2 * SG * NST
EPS = 1e-6
SLAB = 256
FT = SLAB // P

O_Q = 0
O_K = 2048
O_V = O_K + 512
O_ZATT = O_V + 512
O_QI = O_ZATT + 2048
O_KI = O_QI + IH * ID
O_WI = O_KI + ID
O_Z = O_WI + IH
O_X = O_Z + D_INNER
O_B = O_X + D_INNER
O_C = O_B + SG * NST
O_DT = O_C + SG * NST
O_GA = O_DT + SH
O_GS = O_GA + D_MODEL

RAW_S = SEQ + CW - 1
RAW = RAW_S + DB * (CW - 1 + DS)
ACC = RAW - (CW - 1)

NEG = -1e30
PICKED = -3e38


def constant_arrays():
    c = {}
    c["ident"] = np.eye(P, dtype=np.float32)
    pos = np.zeros(TT * P, np.int64)
    pos[:SEQ] = np.arange(SEQ)
    pos[SEQ:SEQ + NS] = PAST + np.arange(NS) % DS
    rope = np.zeros((TT, P, 2 * (HD // 2) + 2 * (ID // 2)), np.float32)
    for d, at in ((HD, 0), (ID, HD)):
        inv = np.float32(THETA) ** (-np.arange(0, d, 2, dtype=np.float32) / np.float32(d))
        ang = pos.astype(np.float32)[:, None] * inv[None].astype(np.float32)
        rope[:, :, at:at + d // 2] = np.cos(ang).reshape(TT, P, -1)
        rope[:, :, at + d // 2:at + d] = np.sin(ang).reshape(TT, P, -1)
    c["rope"] = rope
    i = np.arange(P)
    c["causal_q"] = np.where(i[None, :] <= i[:, None], 0, NEG).astype(np.float32)
    c["causal_k"] = (i[:, None] <= i[None, :]).astype(np.float32)
    s = np.arange(NS)
    same = s[:, None] // DS == s[None, :] // DS
    c["dec_k"] = (same & (s[:, None] <= s[None, :])).astype(np.float32)
    dec_q = np.zeros((NS, SKEYS), np.float32)
    dec_q[:, PAST:] = np.where(same & (s[None, :] <= s[:, None]), 0, NEG)
    c["dec_q"] = dec_q
    selrow = np.zeros((NS, DB, P), np.float32)
    for b in range(DB):
        for g in range(KVH):
            for r in range(REP):
                for t in range(DS):
                    selrow[DS * b + t, b, 32 * g + DS * r + t] = 1
    c["selrow"] = selrow
    headmask = np.zeros((IH * DS, DB, NS), np.float32)
    for b in range(DB):
        for h in range(IH):
            for t in range(DS):
                headmask[DS * h + t, b, DS * b + t] = 1
    c["headmask"] = headmask
    c["in_batch"] = (s[:, None] // DS == np.arange(DB)[None]).astype(np.float32)
    c["batch_cols"] = np.broadcast_to((np.arange(DB)[:, None] == s[None] // DS), (P, DB, NS)).astype(np.float32)
    return c


class Steps:

    def __init__(self, eng, semaphore):
        self.eng, self.sem, self.count, self.frame = eng, semaphore, 0, 0

    def add(self, instruction):
        instruction.then_inc(self.sem, 1)
        self.count += 1

    def wait(self):
        self.eng.wait_ge(self.sem, self.frame + self.count)

    def loop(self, start, trips, per):
        return _Loop(self, start, trips, per)


class _Loop:
    def __init__(self, steps, start, trips, per):
        self.s, self.start, self.trips, self.per = steps, start, trips, per

    def __enter__(self):
        self.fori = self.s.eng.Fori(self.start, self.start + self.trips)
        i = self.fori.__enter__()
        self.before = self.s.count
        self.s.frame = (i - self.start) * self.per + self.before if self.per else self.before
        self.s.count = 0
        return i

    def __exit__(self, *exc):
        if exc[0] is None:
            assert self.s.count == self.per, f"the body adds {self.s.count}, the loop was told {self.per}"
        self.s.count = self.before + self.trips * self.per
        self.s.frame = 0
        return self.fori.__exit__(*exc)


def build(nc, a, out, c):
    with ExitStack() as ctx:
        sems = {}

        def sem(name):
            if name not in sems:
                sems[name] = ctx.enter_context(nc.semaphore(name))
            return sems[name]

        def sb(name, shape, dt=F32):
            return ctx.enter_context(nc.sbuf_tensor(name, shape, dt))

        ps = ctx.enter_context(nc.psum_tensor("ps", [P, 8, 512], F32))

        def dram(name, shape):
            return nc.dram_tensor(name, shape, F32, kind="Internal").ap()

        zatt_dram = dram("zatt_dram", (P, QH * NT))
        NF = D_MODEL // SLAB
        EARLY = 5
        LATE = NF - EARLY
        yatt_dram = dram("yatt_dram", (P, QH * NT))
        yssd_dram = dram("yssd_dram", (P, 2 * KC * NT))
        merged_dram = dram("merged_dram", (P, KC * NT))
        early_dram = dram("early_dram", (P, 2 * EARLY * NT))
        acsT_dram = dram("acsT_dram", (SH, NT))
        acs_dram = dram("acs_dram", (TT, P, SH))
        wi_dram = dram("wi_dram", (NS, IH))

        xnT = sb("xnT", [P, KC, NT])
        W = sb("W", [P, 3, KC, SLAB])
        ident = sb("ident", [P, P])
        ident_bf = sb("ident_bf", [P, P], BF16)
        ones = sb("ones", [P, P])
        causal_q = sb("causal_q", [P, P])
        causal_k = sb("causal_k", [P, P])
        dec_k = sb("dec_k", [NS, NS])
        gT = sb("gT", [P, KC])
        gnT = sb("gnT", [P, 2 * KC])
        cwT = sb("cwT", [P, CONV_DIM // P, DB * (CW - 1) + CW + 1])
        dskip = sb("dskip", [P, SH])
        in_batch = sb("in_batch", [NS, DB])
        batch_cols = sb("batch_cols", [P, DB, NS])
        dt_tok = sb("dt_tok", [P, TT, SH])
        acs_tok = sb("acs_tok", [P, TT, SH])
        grow_tok = sb("grow_tok", [P, TT, SH])
        dec_tok = sb("dec_tok", [P, TT, SH])
        cdec = sb("cdec", [P, 4, SH])
        decS = sb("decS", [P, SH // 2, DB])
        small = sb("small", [P, 64])
        sumsq, rstd = small[:, 0:8], small[:, 8:16]
        lnst, lnagg, lnr = small[:, 16:22], small[:, 22:24], small[:, 24:25]
        c_small = sb("c_small", [P, 32])
        wi4 = c_small[:, 28:32]
        pt_sb = sb("pt_sb", [1, DB * PAGES], I32)
        ARENA = 27880
        R = sb("R", [P, ARENA])

        def carve(at, *shape, rows=P, dt=F32):
            n = int(np.prod(shape))
            words = n if dt == F32 else n // 2
            assert at + words <= ARENA, (at, words)
            v = R[0:rows, at:at + words]
            if dt != F32:
                v = v.bitcast(dt)
            if len(shape) == 2:
                v = v.rearrange("p (a b) -> p a b", a=shape[0])
            if len(shape) == 3:
                v = v.rearrange("p (a b c) -> p a b c", a=shape[0], b=shape[1])
            return v, at + words

        qkT, at = carve(0, QH + KVH, NT)
        vtok, at = carve(at, TT, KVH * HD)
        att_free = at
        qiT, at = carve(at, IH, NT)
        kiT, at = carve(at, NT, rows=ID)
        wi_tok, at = carve(at, TT, IH)
        b_free = at
        rope, at = carve(b_free, TT, HD + ID)
        tcos, at = carve(at, SLAB)
        tsin, at = carve(at, SLAB)
        rot, at = carve(at, 2, SLAB)
        lnw, at = carve(at, ID)
        lnb, at = carve(at, ID)
        kin, at = carve(at, 2, ID)
        dtT, at = carve(at, NT, rows=SH)
        dtE, at = carve(at, NT, rows=SH)
        dtU, at = carve(at, NT, rows=SH)
        dtL, at = carve(at, NT, rows=SH)
        xt, at = carve(0, 2, D_MODEL)
        xsq, at = carve(at, D_MODEL)
        convrows, at = carve(at, CONV_DIM, rows=DB * (CW - 1) + CW + 1)
        grow_rows, at = carve(at, P, rows=KC)
        gnrow_rows, at = carve(at, P, rows=2 * KC)
        dtR = R[0:SH, b_free + TT * (HD + ID):b_free + TT * (HD + ID) + NT]

        def tok(t):
            return slice(P * t, P * t + ROWS[t])

        def bc(ap, shape, *axes):
            for x in axes:
                ap = ap.unsqueeze(x)
            return ap.to_broadcast(shape)

        Wflat = W[:, :, :, :].rearrange("p a b c -> p (a b c)")

        def wcarve(at, *shape, rows=P):
            n = int(np.prod(shape))
            assert at + n <= 3 * KC * SLAB
            v = Wflat[0:rows, at:at + n]
            if len(shape) == 2:
                v = v.rearrange("p (a b) -> p a b", a=shape[0])
            if len(shape) == 3:
                v = v.rearrange("p (a b c) -> p a b c", a=shape[0], b=shape[1])
            return v, at + n

        kidx, at = wcarve(0, 2, PAGES * ID)
        kisT, at = wcarve(at, 2, PAST, rows=ID)
        srelu, at = wcarve(at, 2, SKEYS, rows=IH * DS)
        prelu, at = wcarve(at, 4, SEQ)
        qist, at = wcarve(at, 4, P, rows=ID)
        qis, at = wcarve(at, 2 * IH * DS, rows=ID)
        hw, at = wcarve(at, 2, NS, rows=IH * DS)
        headmask, at = wcarve(at, DB, NS, rows=IH * DS)
        wcol, at = wcarve(at, DB, rows=IH * DS)
        dec_q, at = wcarve(at, SKEYS, rows=NS)
        psc, at = carve(b_free, 3, SEQ)
        ssc, at = carve(at, SKEYS, rows=NS)
        pmask, at = carve(at, 4, SEQ, dt=BF16)
        smask, at = carve(at, SKEYS, rows=NS, dt=BF16)
        top8, at = carve(at, 4, 8)
        at_masks = at
        qst, at = carve(att_free, REP, P)
        pexp, at = carve(at, REP, SEQ)
        pT, at = carve(at, 2, SEQ)
        on, at = carve(at, REP, P)
        zg, at = carve(at, REP, P)
        assert at <= b_free
        zt, at = carve(att_free, 2, NT)
        Kb, at = wcarve(0, 2 * PAGES, KVH * HD)
        V0, at = wcarve(at, PAGES, KVH * HD)
        V1, at = carve(att_free, PAGES, KVH * HD)
        Vb = [V0, V1]
        kTb, at = carve(at, 2, PAST)
        sexp, at = carve(at, SKEYS)
        sT, at = carve(at, PAGES + 1, P)
        qsb, at = carve(at, KVH, 32)
        zdec, at = carve(at, QH, NS)
        osb, at = carve(at, HD)
        assert at <= b_free
        selrow, at = carve(at_masks, DB, P, rows=NS, dt=BF16)
        selst, at = carve(at, P, rows=NS, dt=BF16)
        selrow_f = psc.rearrange("p a b -> p (a b)")[0:NS, 0:DB * P].rearrange("p (a b) -> p a b", a=DB)

        NJ = GH // 2 + 2
        raw, at = carve(0, NJ, RAW)
        zraw, at = carve(at, 4, NT)
        acc, at = carve(at, 2, RAW)
        xact, at = carve(at, NJ, NT)
        zs, at = carve(at, 4, NT)
        acsbc, at = carve(at, GH, NT)
        xdt, at = carve(at, GH, SP_)
        xD, at = carve(at, GH, SP_)
        xdtd, at = carve(at, GH, SP_)
        E, at = carve(at, GH, P)
        Btok, at = carve(at, P)
        Bblk, at = carve(at, DB, NST, rows=NS)
        ytok, at = carve(at, GH * SP_)
        yT, at = carve(at, 4, NT)
        S, at = carve(at, GH * SP_)
        st, at = carve(at, DB // 2, 4, NST)
        ST, at = carve(at, 2, GH * SP_)
        Cm, at = carve(at, DB, NS)
        cn, at = carve(at, NJ, CW - 1 + DB * (CW - 1))
        cno, at = carve(at, NJ * P, rows=CW - 1 + DB * (CW - 1))
        cw_g, at = carve(at, NJ, DB * (CW - 1) + CW + 1)
        gn_g = small[:, 28:32]
        cbm = causal_q
        NC = CW - 1 + DB * (CW - 1)
        sq = xact
        rn_row = acsbc[:, 0, :]
        rn = rn_row.rearrange("p (a b) -> p a b", a=2)
        fsb = acc.rearrange("p a b -> p (a b)")[:, 0:4 * NST]

        early, _ = carve(0, 2 * EARLY, NT)
        assert 2 * EARLY * NT <= NJ * RAW + 4 * NT
        yattF, at = carve(0, QH, NT)
        yssdF, at = carve(at, 2 * KC, NT)
        gateA, at = carve(at, 2, NT)
        gateS = cwT.rearrange("p a b -> p (a b)")[:, 0:2 * NT].rearrange("p (a b) -> p a b", a=2)
        mergedT, at = carve(0, KC, NT)
        h_out, at = carve(at, TT, D_MODEL)
        fg_bc, at = carve(at, D_MODEL)
        gsq, at = carve(at, D_MODEL)

        def decode_acc(j):
            return acc[:, j % 2, RAW_S:RAW].rearrange("p (b k) -> p b k", b=DB)[:, :, 0:DS]

        c_dtb, c_alog, c_aneg, nmx, mx, rsum, rinv = (c_small[:, k:k + 1] for k in (0, 1, 2, 3, 7, 11, 15))
        expS = c_small[0:SH, 20:20 + DB]
        nmx4, mx4, rsum4, rinv4 = (c_small[:, k:k + 4] for k in (3, 7, 11, 15))

        ROOTS_B, ROOTS_E, ROOTS_G = TT, 2 * TT, 2 * TT + SG

        STAGE_ENDS = {"A": 5, "B": 10, "C1": 15, "C2": 19, "C3a": 23, "C3": 27, "E": 31}

        def stage_end(eng, name, wait=True):
            eng.drain().then_inc(sem("stage_ended"), 1)
            if wait:
                eng.wait_ge(sem("stage_ended"), STAGE_ENDS[name])

        TOK0 = TT - 1

        def apart(eng):
            eng.sem_inc(sem("waited"), 1)

        FIRST_USE = {"C2": (8, 8), "E": (12, 12), "F": (30, 30), "G": (46, 41)}
        w_in_rows = a["w_in"][0].rearrange("(kc p) n -> p kc n", p=P)
        w_br_rows = a["w_branch"][0].rearrange("(kc p) n -> p kc n", p=P)
        w_out_rows = a["w_out"][0].rearrange("(kc p) n -> p kc n", p=P)

        def load_slab(eng, slot, src, after=None):
            if after:
                eng.wait_ge(sem(after[0]), after[1])
            eng.dma_start(W[:, slot, :, :], src).then_inc(sem(f"slab{slot}_loaded"), 16)

        def await_slab(eng, slot, use):
            eng.wait_ge(sem(f"slab{slot}_loaded"), (use + 1) * 16)

        def gate_slab(k):
            at = O_GA + (LATE + k) * SLAB
            return w_in_rows[:, :, at:at + SLAB]

        NSTATE = DB * (CW - 1)
        N_CONST = 17
        block = ctx.enter_context(nc.Block())

        @block.sync
        def _(eng):
            for t in range(2):
                eng.dma_start(xt[:, t, :], a["x_prompt"][0, tok(t), :]).then_inc(sem(f"x_in{t}"), 16)
            row = lambda ap: ap.rearrange("(a n) -> a n", a=1)
            col = lambda ap: ap.rearrange("(n a) -> n a", a=1)
            for dst, src in ((ident[:, :], c["ident"]), (grow_rows, a["norm_g"][0].rearrange("(a b) -> a b", b=P)),
                             (gnrow_rows, a["ssd_norm_g"][0].rearrange("(a b) -> a b", b=P)),
                             (convrows[0:NSTATE, :], a["state_conv"][0].rearrange("b k n -> (b k) n")),
                             (convrows[NSTATE:NSTATE + CW, :], a["conv_w"][0]),
                             (convrows[NSTATE + CW:NSTATE + CW + 1, :], a["conv_b"]),
                             (causal_q[:, :], c["causal_q"]), (causal_k[:, :], c["causal_k"]),
                             (dec_k[:, :], c["dec_k"]), (in_batch[:, :], c["in_batch"]),
                             (batch_cols[:, :, :], c["batch_cols"]),
                             (pt_sb[:, :], row(a["page_table"].rearrange("b n -> (b n)"))),
                             (dskip[:, :], a["d_skip"][0].partition_broadcast(P)),
                             (rope[:, :, :], c["rope"].rearrange("t p n -> p t n")),
                             (lnw, a["idx_ln_w"][0].partition_broadcast(P)),
                             (lnb, a["idx_ln_b"][0].partition_broadcast(P)),
                             (c_dtb[0:SH, :], col(a["dt_bias"][0]))):
                eng.dma_start(dst, src).then_inc(sem("consts_in"), 16)
            eng.dma_start(c_alog[0:SH, :], col(a["a_log"][0])).then_inc(sem("alog_in"), 16)
            eng.dma_start(W[:, 2, :, 0:ID + IH], w_in_rows[:, :, O_KI:O_KI + ID + IH]).then_inc(sem("slab2_loaded"), 16)
            eng.dma_start(W[:, 2, :, ID + IH:ID + IH + SH], w_in_rows[:, :, O_DT:O_DT + SH]).then_inc(sem("slab2_loaded"), 16)
            for s in range(2):
                load_slab(eng, s, w_in_rows[:, :, s * SLAB:(s + 1) * SLAB])
            for t in range(2, TT):
                eng.wait_ge(sem("xT_turned"), t - 1)
                src = a["x_prompt"][0, tok(t), :] if t < 4 else a["x_sample"].rearrange("b t d -> (b t) d")
                eng.dma_start(xt[0:ROWS[t], t % 2, :], src).then_inc(sem(f"x_in{t % 2}"), 16)
            stage_end(eng, "A")
            with eng.Fori(1, 6) as i:
                for s in range(2):
                    load_slab(eng, s, w_in_rows[:, :, bass.ds(i * (2 * SLAB) + s * SLAB, SLAB)],
                              ("tok_ready", i * 10 + (5 * s - 5)))
            with eng.Fori(6, 8) as i:
                for s in range(2):
                    load_slab(eng, s, w_in_rows[:, :, bass.ds((i - 6) * (2 * SLAB) + (O_QI + s * SLAB), SLAB)],
                              ("tok_ready", i * 10 + (5 * s - 5)))
            stage_end(eng, "B")
            eng.dma_start(dec_q, c["dec_q"]).then_inc(sem("idx_consts_in"), 16)
            eng.dma_start(headmask, c["headmask"]).then_inc(sem("idx_consts_in"), 16)
            for b in range(DB):
                eng.dma_start(wcol[:, b:b + 1], wi_dram[b * DS:(b + 1) * DS, :].rearrange("t h -> h t"),
                              allow_slow_non_contiguous=True).then_inc(sem("wcol_in"), 16)
            stage_end(eng, "C1")
            load_slab(eng, 0, w_in_rows[:, :, O_ZATT:O_ZATT + SLAB])
            eng.wait_ge(sem("prelu_used"), 3 * IH)
            eng.wait_ge(sem("pdots_ready"), 3 * IH)
            load_slab(eng, 1, w_in_rows[:, :, O_ZATT + SLAB:O_ZATT + 2 * SLAB])
            with eng.Fori(1, 4) as i:
                for s in range(2):
                    load_slab(eng, s, w_in_rows[:, :, bass.ds(i * (2 * SLAB) + (O_ZATT + s * SLAB), SLAB)],
                              ("zatt_ready", i * 4 + (2 * s - 2)))

            def group_slabs(g, x0_after, x1_after, bc_after):
                x0, z0 = g * (2 * SLAB) + O_X, g * (2 * SLAB) + O_Z
                load_slab(eng, 0, w_in_rows[:, :, bass.ds(x0, SLAB)], x0_after)
                load_slab(eng, 1, w_in_rows[:, :, bass.ds(x0 + SLAB, SLAB)], x1_after)
                if bc_after:
                    eng.wait_ge(sem(bc_after[0]), bc_after[1])
                for part, off in ((0, O_B), (1, O_C)):
                    eng.dma_start(W[:, 2, :, part * P:part * P + P],
                                  w_in_rows[:, :, bass.ds(g * P + off, P)]).then_inc(sem("bc_loaded"), 16)
                for s in range(2):
                    load_slab(eng, s, w_in_rows[:, :, bass.ds(z0 + s * SLAB, SLAB)], ("projT_ready", g * 10 + (2 * s + 2)))
            group_slabs(0, ("kb_turned", (DB - 1) * KVH), ("kb_turned", DB * KVH), ("so_ready", DB - 1))
            with eng.Fori(1, SG) as g:
                group_slabs(g, ("projT_ready", g * 10 - 2), ("projT_ready", g * 10), ("projT_ready", g * 10 - 4))
            load_slab(eng, 0, gate_slab(0), ("projT_ready", SG * 10 - 2))
            load_slab(eng, 1, gate_slab(1), ("projT_ready", SG * 10))
            eng.dma_start(W[:, 2, :, :], gate_slab(2)).then_inc(sem("bc_loaded"), 16)
            load_slab(eng, 0, gate_slab(3), ("projT_ready", SG * 10 + 2))
            load_slab(eng, 1, gate_slab(4), ("projT_ready", SG * 10 + 4))

            def branch_slabs(i, both_gates):
                cs, ssd_gate = bass.ds(i * SLAB, SLAB), w_in_rows[:, :, bass.ds(i * SLAB + O_GS, SLAB)]
                if both_gates:
                    load_slab(eng, 0, w_in_rows[:, :, bass.ds(i * SLAB + O_GA, SLAB)], ("yb1_done", i))
                    load_slab(eng, 1, ssd_gate, ("yb_ready", i * 2))
                eng.wait_ge(sem("ya_ready"), i * 2)
                apart(eng)
                eng.dma_start(W[:, 2, :, :], w_br_rows[:, 0:KC, cs]).then_inc(sem("branch_loaded"), 16)
                if both_gates:
                    load_slab(eng, 0, w_br_rows[:, KC:2 * KC, cs], ("ga_ready", i * 2 + 2))
                    load_slab(eng, 1, w_br_rows[:, 2 * KC:3 * KC, cs], ("gs_ready", i * 2 + 2))
                else:
                    load_slab(eng, 0, ssd_gate, ("yb_ready", i * 2))
                    load_slab(eng, 1, w_br_rows[:, KC:2 * KC, cs], ("yb_ready", i * 2))
                    load_slab(eng, 0, w_br_rows[:, 2 * KC:3 * KC, cs], ("gs_ready", i * 2 + 2))
            eng.wait_ge(sem("projT_ready"), 10 * (SG + 1))
            with eng.Fori(0, LATE) as i:
                branch_slabs(i, True)
            with eng.Fori(LATE, NF) as i:
                branch_slabs(i, False)
            load_slab(eng, 1, w_out_rows[:, :, 0:SLAB], ("yb1_done", 8))
            load_slab(eng, 0, w_out_rows[:, :, SLAB:2 * SLAB], ("yb_ready", 16))
            with eng.Fori(1, 4) as i:
                for s in range(2):
                    load_slab(eng, 1 - s, w_out_rows[:, :, bass.ds(i * (2 * SLAB) + s * SLAB, SLAB)],
                              ("h_ready", i * 10 + (5 * s - 5)))
            for t in range(TT):
                eng.wait_ge(sem("y_ready"), t + 1)
                eng.dma_start(out[0][0, tok(t), :] if t < 4 else out[1].rearrange("b t d -> (b t) d"), h_out[0:ROWS[t], t, :])\
                   .then_inc(sem("y_out"), 16)
            eng.wait_ge(sem("y_out"), 16 * TT)

        @block.tensor
        def _(eng):
            def project_tokens(slot, t, bank_no, c0, cols):
                for kc in range(KC):
                    mm = eng.matmul(ps[0:ROWS[t], bank_no, 0:cols], xnT[:, kc, tok(t)], W[:, slot, kc, c0:c0 + cols],
                                    start=(kc == 0), stop=(kc == KC - 1))
                return mm

            def project_features(slot, j, pair, rhs=None, rows=P, k0=0, start=True, stop=True, part=range(KC)):
                rhs = xnT if rhs is None else rhs
                for kc in part:
                    for h in range(2):
                        mm = eng.matmul(ps[0:rows, 2 * pair + h, 0:HALF], W[:, slot, kc, j:j + rows],
                                        rhs[:, k0 + kc, HALF * h:HALF * (h + 1)],
                                        start=(start and kc == 0), stop=(stop and kc == KC - 1))
                return mm

            eng.wait_ge(sem("consts_in"), 16 * N_CONST)
            eng.transpose(ps[:, 4, 0:KC], grow_rows, ident[0:KC, 0:KC])
            eng.transpose(ps[:, 4, KC:3 * KC], gnrow_rows, ident[0:2 * KC, 0:2 * KC]).then_inc(sem("rows_turned"), 1)
            NR = NSTATE + CW + 1
            for n in range(CONV_DIM // P):
                tr = eng.transpose(ps[:, 5 + n // 16, (n % 16) * NR:(n % 16 + 1) * NR], convrows[:, n * P:(n + 1) * P],
                                   ident[0:NR, 0:NR])
            tr.then_inc(sem("rows_turned"), 1)
            for t in range(TT):
                eng.wait_ge(sem("x_scaled"), t + 1)
                if t == 1:
                    eng.wait_ge(sem("rows_kept"), 3)
                if t >= 2:
                    eng.wait_ge(sem("xnT_kept"), t - 1)
                for k in range(KC):
                    tr = eng.transpose(ps[:, 4 * (t % 2) + k // 4, (k % 4) * P:(k % 4) * P + ROWS[t]],
                                       xt[0:ROWS[t], t % 2, k * P:(k + 1) * P], ident[0:ROWS[t], 0:ROWS[t]])
                tr.then_inc(sem("xT_turned"), 1)
            stage_end(eng, "A")

            def turn_rot(n, t, heads, width):
                eng.wait_ge(sem("rot_ready"), n + 1)
                eng.wait_ge(sem("rotT_kept"), n)
                apart(eng)
                for h in range(heads):
                    tr = eng.transpose(ps[0:width, 5 + t % 3, h * P:h * P + ROWS[t]],
                                       rot[0:ROWS[t], t % 2, h * width:(h + 1) * width], ident[0:ROWS[t], 0:ROWS[t]])
                tr.then_inc(sem("rot_turned"), 1)

            def slab_tokens(slot, use, n, m, heads, width, before=None, rest=True):
                await_slab(eng, slot, use)
                for t in range(TT):
                    eng.wait_ge(sem("tok_kept"), n + t)
                    project_tokens(slot, t, t, 0, SLAB).then_inc(sem("tok_ready"), 1)
                    if before is not None and t == 0:
                        turn_rot(before, TT - 1, heads, width)
                    if heads and t:
                        turn_rot(m + (t - 1), t - 1, heads, width)
                if heads and rest:
                    turn_rot(m + (TT - 1), TT - 1, heads, width)

            with eng.Fori(0, 5) as i:
                slab_tokens(0, i, i * 10, i * 10, 2, HD, rest=False)
                slab_tokens(1, i, i * 10 + 5, i * 10 + 5, 2, HD, before=i * 10 + 4)
            for s in range(2):
                slab_tokens(s, 5, 50 + 5 * s, None, 0, 0)
            with eng.Fori(6, 8) as i:
                slab_tokens(0, i, i * 10, i * 10 - 10, 4, ID, rest=False)
                slab_tokens(1, i, i * 10 + 5, i * 10 - 5, 4, ID, before=i * 10 - 6)
            eng.wait_ge(sem("slab2_loaded"), 32)
            for t in range(TT):
                eng.wait_ge(sem("tok_kept"), 80 + t)
                project_tokens(2, t, t, 0, ID + IH).then_inc(sem("tok_ready"), 1)
            eng.wait_ge(sem("rotT_kept"), 71)
            project_features(2, ID + IH, 3, rows=SH).then_inc(sem("dt_ready"), 1)
            for t in range(TT):
                eng.wait_ge(sem("rot_ready"), 70 + t + 1)
                if t >= 1:
                    eng.wait_ge(sem("rotT_kept"), 70 + t + 1)
                eng.transpose(ps[0:ID, 5, 0:ROWS[t]], rot[0:ROWS[t], t % 2, 0:ID],
                              ident[0:ROWS[t], 0:ROWS[t]]).then_inc(sem("rot_turned"), 1)
            eng.wait_ge(sem("tok_kept"), 85 + TOK0)
            for k, src in enumerate((dtT, dtU)):
                eng.wait_ge(sem("dtT_ready"), k + 1)
                for t in range(TT):
                    tr = eng.transpose(ps[0:ROWS[t], k, t * SH:(t + 1) * SH], src[:, tok(t)], ident[0:SH, 0:SH])
                tr.then_inc(sem("dt_turned"), 1)
            eng.wait_ge(sem("expS_ready"), 1)
            for h in range(SH):
                mm = eng.matmul(ps[SP_ * (h % 2):SP_ * (h % 2 + 1), 2, h // 2 * DB:(h // 2 + 1) * DB],
                                ident[0:SH, h:h + 1].to_broadcast([SH, SP_]), expS, start=True, stop=True)
            mm.then_inc(sem("decS_ready"), 1)
            stage_end(eng, "B")

            eng.wait_ge(sem("idx_consts_in"), 32)
            for k, (lo, hi) in enumerate(((0, 512), (512, 1024), (1024, SKEYS))):
                eng.matmul(ps[0:NS, 5 + k, 0:hi - lo], ident[0:NS, 0:NS], dec_q[:, lo:hi], start=True, stop=False)

            def decode_index(n, i, k, last=False):
                eng.wait_ge(sem(f"kidx{k}_in"), i * (16 * PAGES) + 16 * PAGES)
                eng.wait_ge(sem("kisT_kept"), n)
                apart(eng)
                for p in range(PAGES):
                    tr = eng.transpose(ps[0:ID, p // 4, (p % 4) * P:(p % 4 + 1) * P], kidx[:, k, p * ID:(p + 1) * ID],
                                       ident[:, :])
                tr.then_inc(sem("kis_turned"), 1)
                eng.wait_ge(sem("kisT_kept"), n + 1)
                eng.wait_ge(sem("qis_ready"), n + 1)
                eng.wait_ge(sem("srelu_ready"), n)
                apart(eng)
                q = qis[:, k * IH * DS:(k + 1) * IH * DS]
                for h in range(2):
                    eng.matmul(ps[0:IH * DS, 2 + h, :], q, kisT[:, k, 512 * h:512 * (h + 1)], start=True, stop=True)
                eng.matmul(ps[0:IH * DS, 4, 0:NS], q, kiT[:, SEQ:NT], start=True, stop=True)\
                   .then_inc(sem("sdots_ready"), 1)
                eng.wait_ge(sem("srelu_ready"), n + 1)
                apart(eng)
                for j, (lo, hi) in enumerate(((0, 512), (512, 1024), (1024, SKEYS))):
                    mm = eng.matmul(ps[0:NS, 5 + j, 0:hi - lo], hw[:, k, :], srelu[:, k, lo:hi], start=False, stop=last)
                mm.then_inc(sem("sscore_added"), 1)
            with eng.Fori(0, DB // 2 - 1) as i:
                for k in range(2):
                    decode_index(i * 2 + k, i, k)
            for k in range(2):
                decode_index(DB - 2 + k, DB // 2 - 1, k, last=(k == 1))
            stage_end(eng, "C1")

            for qb in range(1, 4):
                n0 = 4 * (qb - 1)
                with eng.Fori(0, IH // 4) as i:
                    eng.wait_ge(sem("qist_ready"), i + (n0 + 1))
                    for h in range(4):
                        eng.wait_ge(sem("pdots_kept"), (i + n0) * 4)
                        eng.matmul(ps[:, h, 0:P * (qb + 1)], qist[:, h, :], kiT[:, 0:P * (qb + 1)], start=True, stop=True)\
                           .then_inc(sem("pdots_ready"), 1)
            u = FIRST_USE["C2"]
            eng.wait_ge(sem("pdots_kept"), 3 * IH)
            with eng.Fori(0, 4) as i:
                for s in range(2):
                    await_slab(eng, s, i + u[s])
                    for j in range(FT):
                        eng.wait_ge(sem("zatt_kept"), i * 4 + (2 * s + j))
                        project_features(s, j * P, j).then_inc(sem("zatt_ready"), 1)
            stage_end(eng, "C2")

            def score(qb, g, r):
                nk = P * (qb + 1)
                eng.matmul(ps[:, r, 0:nk], ident_bf[:, :], pmask[:, qb, 0:nk], start=True, stop=False)
                eng.matmul(ps[:, r, 0:nk], qst[:, r, :],
                           qkT[:, bass.ds(g + QH, 1), 0:nk].rearrange("p a n -> p (a n)"), start=False, stop=True)\
                   .then_inc(sem("pscore_ready"), 1)

            def turn_output(m):
                eng.wait_ge(sem("on_ready"), m + 1)
                eng.wait_ge(sem("poT_kept"), m)
                for r in range(REP):
                    tr = eng.transpose(ps[:, 7, r * P:(r + 1) * P], on[:, r, :], ident[:, :])
                tr.then_inc(sem("on_turned"), 1)

            def attend(qb, g, first, more):
                n = g + KVH * qb
                for r in range(REP):
                    eng.wait_ge(sem("pexp_ready"), n * REP + (r + 1))
                    eng.wait_ge(sem("pT_kept"), n * REP + r)
                    for k in range(qb + 1):
                        tr = eng.transpose(ps[:, 4 + r % 2, k * P:(k + 1) * P], pexp[:, r, k * P:(k + 1) * P], ident[:, :])
                    tr.then_inc(sem("p_turned"), 1)
                    if more:
                        eng.wait_ge(sem("qst_ready"), n + 2)
                        score(qb, g + 1, r)
                    if r == 0 and not first:
                        turn_output(n - 1)
                    eng.wait_ge(sem("pT_kept"), n * REP + (r + 2))
                    for k in range(qb + 1):
                        mm = eng.matmul(ps[:, 6, r * P:(r + 1) * P], pT[:, r % 2, k * P:(k + 1) * P],
                                        vtok[:, k, bass.ds(g * HD, HD)], start=(k == 0), stop=(k == qb))
                    mm.then_inc(sem("po_ready"), 1)
            for qb in range(4):
                eng.wait_ge(sem("qst_ready"), KVH * qb + 1)
                for r in range(REP):
                    score(qb, 0, r)
                attend(qb, 0, True, True)
                with eng.Fori(1, KVH - 1) as g:
                    attend(qb, g, False, True)
                attend(qb, KVH - 1, False, False)
                turn_output(KVH * qb + KVH - 1)
            def decode_attention(n, half, k):
                KB = ((0, 1), (5, 6))

                def turn_keys(g):
                    eng.wait_ge(sem(f"kTb{g % 2}_kept"), n * 2 + g // 2)
                    for p in range(PAGES):
                        tr = eng.transpose(ps[:, KB[g % 2][p // 4], (p % 4) * P:(p % 4 + 1) * P],
                                           Kb[:, k * PAGES + p, g * HD:(g + 1) * HD], ident[:, :])
                    tr.then_inc(sem("kb_turned"), 1)
                eng.wait_ge(sem(f"kpage{k}_in"), half * (16 * PAGES) + 16 * PAGES)
                eng.wait_ge(sem("qsb_ready"), n + 1)
                eng.wait_ge(sem("osb_ready"), n)
                eng.wait_ge(sem("sT_kept"), n)
                for j, (lo, hi) in enumerate(((0, 512), (512, 1024), (1024, SKEYS))):
                    eng.matmul(ps[:, 2 + j, 0:hi - lo], selst, smask[:, lo:hi], start=True, stop=False)
                turn_keys(0)
                for g in range(KVH):
                    if g + 1 < KVH:
                        turn_keys(g + 1)
                    eng.wait_ge(sem(f"kTb{g % 2}_kept"), n * 2 + (g // 2 + 1))
                    q, rows = qsb[:, g, :], slice(32 * g, 32 * g + 32)
                    for j in range(2):
                        eng.matmul(ps[rows, 2 + j, :], q, kTb[:, g % 2, 512 * j:512 * (j + 1)],
                                   start=False, stop=True)
                    eng.matmul(ps[rows, 4, 0:NS], q, qkT[:, QH + g, SEQ:NT], start=False, stop=True)\
                       .then_inc(sem("dscore_done"), 1)
                eng.wait_ge(sem("sexp_ready"), n + 1)
                eng.wait_ge(sem("so_kept"), n)
                apart(eng)
                for p in range(PAGES):
                    eng.transpose(ps[:, 5 + p // 4, (p % 4) * P:(p % 4 + 1) * P], sexp[:, p * P:(p + 1) * P], ident[:, :])
                eng.transpose(ps[0:NS, 7, 0:P], sexp[:, PAST:SKEYS], ident[:, :]).then_inc(sem("s_turned"), 1)
                eng.wait_ge(sem("sT_kept"), n + 1)
                eng.wait_ge(sem(f"vpage{k}_in"), half * (16 * PAGES) + 16 * PAGES)
                for p in range(PAGES):
                    eng.matmul(ps[:, 0, :], sT[:, p, :], Vb[k][:, p, :], start=(p == 0), stop=False)
                eng.matmul(ps[:, 0, :], sT[0:NS, PAGES, :], vtok[0:NS, 4, :], start=False, stop=True)\
                   .then_inc(sem("so_ready"), 1)
                eng.wait_ge(sem("osb_ready"), n + 1)
                apart(eng)
                eng.transpose(ps[:, 7, 0:P], osb[:, :], ident[:, :]).then_inc(sem("o_turned"), 1)
            eng.wait_ge(sem("poT_kept"), 4 * KVH)
            eng.wait_ge(sem("pT_kept"), 4 * KVH * REP + 1)
            stage_end(eng, "C3a")
            with eng.Fori(0, DB // 2) as i:
                for k in range(2):
                    decode_attention(i * 2 + k, i, k)
            stage_end(eng, "C3")

            HALVES = (range(0, KC // 2), range(KC // 2, KC))

            def project_slot(g, n, half, bc_loads=2):
                u = FIRST_USE["E"]
                slot = (0, 1, 2, 0, 1)[n // 2]
                if n % 2 == 0 and half == 0:
                    if slot == 2:
                        eng.wait_ge(sem("bc_loaded"), g * 32 + 16 * bc_loads)
                    else:
                        eng.wait_ge(sem(f"slab{slot}_loaded"), g * 32 + 16 * (u[slot] + 1 + n // 6))
                if half == 0:
                    eng.wait_ge(sem("projT_kept"), g * 10 + n)
                mm = project_features(slot, (n % 2) * P, n % 2, part=HALVES[half])
                if half == 1:
                    mm.then_inc(sem("projT_ready"), 1)

            def turn_x(g, ci):
                R_, ts = ROWS[ci], tok(ci)
                if ci == 0:
                    eng.wait_ge(sem("xact_ready"), g * NJ + NJ)
                    eng.wait_ge(sem("cno_ready"), g + 1)
                if ci >= 1:
                    eng.wait_ge(sem("s_ready"), g * 4 + ci)
                if ci >= 2:
                    eng.wait_ge(sem("c_done"), g * 5 + (ci - 1))
                if ci == 0:
                    eng.wait_ge(sem("c_done"), g * 5)
                for j in range(4):
                    eng.transpose(ps[0:R_, 4, j * P:(j + 1) * P], xact[:, j, ts], ident[:, :])
                eng.transpose(ps[0:R_, 5, 0:P], xact[:, 4, ts], ident[:, :])
                eng.matmul(ps[0:R_, 6, 0:R_], xact[:, 4, ts], xact[:, 5, ts], start=True, stop=True)\
                   .then_inc(sem("a_ready"), 1)

            def await_factors(g, ci):
                eng.wait_ge(sem("m_ready"), g * 5 + (ci + 1))
                eng.wait_ge(sem("xdtd_ready"), g * 5 + (ci + 1))
                if ci < 4:
                    eng.wait_ge(sem("btok_ready"), g * 4 + (ci + 1))
                else:
                    eng.wait_ge(sem("bblk_ready"), g + 1)

            def within_chunk(R_):
                for h in range(GH):
                    mm = eng.matmul(ps[0:R_, 6, h * SP_:(h + 1) * SP_], E[0:R_, h, 0:R_], xdt[0:R_, h, :],
                                    start=True, stop=True)
                return mm

            def scan_chunk(g, ci):
                await_factors(g, ci)
                if ci:
                    eng.wait_ge(sem("s_ready"), g * 4 + ci)
                    eng.matmul(ps[:, 7, :], xact[:, 5, tok(ci)], S, start=True, stop=True)
                eng.matmul(ps[:, 5, :], Btok, xdtd.rearrange("p a b -> p (a b)"), start=True, stop=True)
                within_chunk(P).then_inc(sem("b_ready"), 1)

            def turn_y(g, ci):
                eng.wait_ge(sem("ytok_ready"), g * 5 + (ci + 1))
                if ci < 4:
                    eng.wait_ge(sem("m_ready"), g * 5 + (ci + 2))
                else:
                    eng.wait_ge(sem("st_new"), g * 8 + 8)
                apart(eng)
                for j in range(4):
                    tr = eng.transpose(ps[:, 4, j * P:j * P + ROWS[ci]], ytok[0:ROWS[ci], j * P:(j + 1) * P],
                                       ident[0:ROWS[ci], 0:ROWS[ci]])
                tr.then_inc(sem("y_turned"), 1)

            def turn_tails(g):
                eng.wait_ge(sem("cn_ready"), g + 1)
                eng.wait_ge(sem("c_done"), g * 5)
                for j in range(NJ):
                    dst = ps[0:NC, 7, j * P:(j + 1) * P] if j < 4 else ps[0:NC, 5, (j - 4) * P:(j - 3) * P]
                    tr = eng.transpose(dst, cn[:, j, :], ident[:, :])
                tr.then_inc(sem("tails_turned"), 1)

            def turn_final_state(g):
                eng.wait_ge(sem("s_ready"), g * 4 + 4)
                for j in range(4):
                    tr = eng.transpose(ps[:, 5, j * P:(j + 1) * P], S[:, j * P:(j + 1) * P], ident[:, :])
                tr.then_inc(sem("final_turned"), 1)

            def decode_states(g, half):
                if half == 0:
                    await_factors(g, 4)
                    eng.wait_ge(sem("fsb_ready"), g + 1)
                    eng.wait_ge(sem("c_done"), g * 5 + 4)
                    apart(eng)
                    within_chunk(NS)
                eng.wait_ge(sem("st_in"), g * 128 + 64 * (half + 1))
                eng.wait_ge(sem("cm_ready"), g + 1)
                eng.wait_ge(sem("st_new"), (g * 2 + half) * 4)
                def turn_state(b):
                    if b >= 2:
                        eng.wait_ge(sem("ST_kept"), g * 8 + (4 * half + b - 1))
                    for j in range(4):
                        tr = eng.transpose(ps[:, 4 + b % 2, j * P:(j + 1) * P], st[:, b, j, :], ident[:, :])
                    tr.then_inc(sem("st_turned"), 1)

                def apply_state(b):
                    eng.wait_ge(sem("ST_kept"), g * 8 + (4 * half + b + 1))
                    mm = eng.matmul(ps[0:NS, 7, :], Cm[:, 4 * half + b, :], ST[:, b % 2, :],
                                    start=(half == 0 and b == 0), stop=(half == 1 and b == 3))
                    mm.then_inc(sem("st_applied"), 1)
                turn_state(0)
                for b in range(1, 4):
                    turn_state(b)
                    apply_state(b - 1)
                apply_state(3)
                add_to_states(g, half, (0, 1))

            def add_to_states(g, half, tiles):
                for j in tiles:
                    if j >= 2:
                        eng.wait_ge(sem("st_new"), g * 8 + (4 * half + j - 1))
                        apart(eng)
                    eng.matmul(ps[:, 4 + j % 2, :], xdtd[0:NS, 2 * j:2 * j + 2, :].rearrange("p a b -> p (a b)"),
                               Bblk[:, 4 * half:4 * half + 4, :].rearrange("p a b -> p (a b)"), start=True, stop=True)\
                       .then_inc(sem("st_added"), 1)

            def sum_squares(g):
                eng.wait_ge(sem("sq_ready"), g + 1)
                for j in range(4):
                    for h in range(2):
                        mm = eng.matmul(ps[:, 6 + h, 0:HALF], ones[:, :], sq[:, j, HALF * h:HALF * (h + 1)],
                                        start=(j == 0), stop=(j == 3))
                mm.then_inc(sem("sumsq_ready"), 1)

            def scan_before(g, n):
                if 3 <= n <= 6:
                    turn_y(g, n - 3)
                if 2 <= n <= 5:
                    scan_chunk(g, n - 2)
                if n == 6:
                    turn_final_state(g)
                    decode_states(g, 0)
                if n == 8:
                    decode_states(g, 1)
                if n == 9:
                    turn_y(g, 4)

            def scan_after(g, n):
                if n == 1:
                    turn_tails(g)
                if 1 <= n <= 5:
                    turn_x(g, n - 1)
                if n == 6 or n == 8:
                    add_to_states(g, n // 8, (2, 3))
                if n == 9:
                    sum_squares(g)

            for n in range(10):
                project_slot(0, n, 0)
                project_slot(0, n, 1)
            with eng.Fori(1, SG) as i:
                for n in range(10):
                    scan_before(i - 1, n)
                    project_slot(i, n, 0)
                    scan_after(i - 1, n)
                    project_slot(i, n, 1)
            for n in range(10):
                scan_before(SG - 1, n)
                project_slot(SG, n, 0, bc_loads=1)
                scan_after(SG - 1, n)
                project_slot(SG, n, 1, bc_loads=1)
            stage_end(eng, "E", wait=False)
            eng.wait_ge(sem("projT_kept"), 10 * (SG + 1) + 1)
            eng.wait_ge(sem("yn_done"), SG)

            u = FIRST_USE["F"]

            def feat(slot, j, pair, **kw):
                return project_features(slot, j * P, pair, **kw)

            def ssd_gate(i, slot):
                eng.wait_ge(sem("yb_used"), i * 2)
                for j in range(FT):
                    feat(slot, j, 2 + j).then_inc(sem("gs_ready"), 1)

            def branches(i, both_gates):
                if both_gates:
                    eng.wait_ge(sem("slab0_loaded"), i * 32 + 16 * (u[0] + 1))
                    eng.wait_ge(sem("ya_used"), i * 2)
                    for j in range(FT):
                        feat(0, j, j).then_inc(sem("ga_ready"), 1)
                    eng.wait_ge(sem("slab1_loaded"), i * 32 + 16 * (u[1] + 1))
                    ssd_gate(i, 1)
                eng.wait_ge(sem("branch_loaded"), i * 16 + 16)
                eng.wait_ge(sem("yatt_in"), 16)
                for j in range(FT):
                    if both_gates:
                        eng.wait_ge(sem("ga_kept"), i * 2 + (j + 1))
                    else:
                        eng.wait_ge(sem("ya_used"), i * 2)
                    feat(2, j, j, rhs=yattF).then_inc(sem("ya_ready"), 1)
                if not both_gates:
                    eng.wait_ge(sem("slab0_loaded"), i * 32 + 16 * (u[0] + 1))
                    ssd_gate(i, 0)
                first, second = (0, 1) if both_gates else (1, 0)
                if both_gates:
                    eng.wait_ge(sem("slab0_loaded"), i * 32 + 16 * (u[0] + 2))
                else:
                    eng.wait_ge(sem("slab1_loaded"), i * 16 + 16 * (u[1] + LATE + 1))
                eng.wait_ge(sem("yssd_in"), 16)
                for j in range(FT):
                    eng.wait_ge(sem("gs_kept"), i * 2 + (j + 1))
                    mm = feat(first, j, 2 + j, rhs=yssdF, stop=False)
                mm.then_inc(sem("yb1_done"), 1)
                eng.wait_ge(sem(f"slab{second}_loaded"), i * 32 + 16 * (u[second] + 2))
                for j in range(FT):
                    feat(second, j, 2 + j, rhs=yssdF, k0=KC, start=False).then_inc(sem("yb_ready"), 1)
            with eng.Fori(0, LATE) as i:
                branches(i, True)
            with eng.Fori(LATE, NF) as i:
                branches(i, False)

            u = FIRST_USE["G"]
            eng.wait_ge(sem("merged_in"), 16)
            eng.wait_ge(sem("merged_ready"), KC)
            with eng.Fori(0, 4) as i:
                for s in range(2):
                    await_slab(eng, 1 - s, i + u[1 - s])
                    for t in range(TT):
                        eng.wait_ge(sem("h_added"), i * 10 + 5 * s)
                        for kc in range(KC):
                            mm = eng.matmul(ps[0:ROWS[t], t, 0:SLAB], mergedT[:, kc, tok(t)], W[:, 1 - s, kc, :],
                                            start=(kc == 0), stop=(kc == KC - 1))
                        mm.then_inc(sem("h_ready"), 1)

        @block.scalar
        def _(eng):
            steps = Steps(eng, sem("act_steps"))

            def root(v, n):
                eng.wait_ge(sem("inverse_ready"), n + 1)
                eng.activation(v, v, ACT.Sqrt).then_inc(sem("root_ready"), 1)

            eng.wait_ge(sem("consts_in"), 16 * N_CONST)
            eng.copy(ident_bf[:, :], ident[:, :])
            for t in range(2):
                eng.wait_ge(sem(f"x_in{t}"), 16)
                eng.activation(xsq, xt[:, t, :], ACT.Square, accum_out=sumsq[:, t:t + 1]).then_inc(sem("sumsq_x"), 1)
                root(rstd[:, t:t + 1], t)
            eng.wait_ge(sem("rows_turned"), 2)
            eng.copy(gT[:, :], ps[:, 4, 0:KC]).then_inc(sem("rows_kept"), 1)
            eng.copy(gnT[:, :], ps[:, 4, KC:3 * KC]).then_inc(sem("rows_kept"), 1)
            eng.copy(cwT.rearrange("p (a b) c -> p a (b c)", a=3), ps[:, 5:8, 0:16 * (NSTATE + CW + 1)])\
               .then_inc(sem("rows_kept"), 1)
            for t in range(2, TT):
                eng.wait_ge(sem(f"x_in{t % 2}"), 16 * (t // 2 + 1))
                eng.activation(xsq[0:ROWS[t], :], xt[0:ROWS[t], t % 2, :], ACT.Square,
                               accum_out=sumsq[0:ROWS[t], t:t + 1]).then_inc(sem("sumsq_x"), 1)
                root(rstd[0:ROWS[t], t:t + 1], t)
            stage_end(eng, "A")

            with eng.Fori(0, 5) as i:
                for s in range(2):
                    for t in range(TT):
                        eng.wait_ge(sem("rot_turned"), i * 10 + (5 * s + t + 1))
                        eng.copy(qkT[:, bass.ds(i * 4 + 2 * s, 2), tok(t)],
                                 ps[:, 5 + t % 3, 0:2 * P].rearrange("p (a b) -> p a b", a=2)[:, :, 0:ROWS[t]])\
                           .then_inc(sem("rotT_kept"), 1)
            with eng.Fori(6, 8) as i:
                for s in range(2):
                    for t in range(TT):
                        eng.wait_ge(sem("rot_turned"), i * 10 + (5 * s + t + 1 - 10))
                        eng.copy(qiT[0:ID, bass.ds(i * 8 + (4 * s - 48), 4), tok(t)],
                                 ps[0:ID, 5 + t % 3, :].rearrange("p (a b) -> p a b", a=4)[:, :, 0:ROWS[t]])\
                           .then_inc(sem("rotT_kept"), 1)
            for t in range(3):
                root(lnr[0:ROWS[t], :], ROOTS_B + t)
            eng.wait_ge(sem("dt_ready"), 1)
            steps.add(eng.activation(dtT.rearrange("p (a b) -> p a b", a=2), ps[0:SH, 6:8, 0:HALF], ACT.Identity,
                                     bias=c_dtb[0:SH, :]))
            steps.wait()
            steps.add(eng.activation(dtE, dtT, ACT.Abs))
            eng.wait_ge(sem("alog_in"), 16)
            steps.wait()
            eng.activation(dtE, dtE, ACT.Exp, scale=-1.0).then_inc(sem("dt_exp_ready"), 1)
            eng.activation(c_aneg[0:SH, :], c_alog[0:SH, :], ACT.Exp).then_inc(sem("dt_exp_ready"), 1)
            for t in range(TT):
                if 1 <= t <= 2:
                    root(lnr[0:ROWS[t + 2], :], ROOTS_B + t + 2)
                eng.wait_ge(sem("rot_turned"), 70 + t + 1)
                eng.copy(kiT[:, tok(t)], ps[0:ID, 5, 0:ROWS[t]]).then_inc(sem("rotT_kept"), 1)
            eng.wait_ge(sem("dt_u_ready"), 1)
            eng.activation(dtL, dtU, ACT.Ln).then_inc(sem("dt_ln_ready"), 1)
            eng.wait_ge(sem("dtT_ready"), 2)
            eng.activation(expS, dtU[:, SEQ + DS - 1:NT:DS], ACT.Exp).then_inc(sem("expS_ready"), 1)
            eng.wait_ge(sem("acs_kept"), 2)
            eng.activation(grow_tok[:, 0:4, :], acs_tok[:, 0:4, :], ACT.Exp)
            eng.activation(grow_tok[0:NS, 4, :], acs_tok[0:NS, 4, :], ACT.Exp)
            eng.wait_ge(sem("dec_ready"), 2)
            eng.activation(dec_tok[:, 0:4, :], dec_tok[:, 0:4, :], ACT.Exp)
            eng.activation(dec_tok[0:NS, 4, :], dec_tok[0:NS, 4, :], ACT.Exp)
            eng.activation(cdec[:, :, :], cdec[:, :, :], ACT.Exp)
            stage_end(eng, "B")

            def decode_index(n, k):
                eng.wait_ge(sem("kis_turned"), n + 1)
                eng.copy(kisT[:, k, :], ps[0:ID, 0:2, :].rearrange("p a b -> p (a b)")).then_inc(sem("kisT_kept"), 1)
                eng.wait_ge(sem("sdots_ready"), n + 1)
                eng.activation(srelu[:, k, :], ps[0:IH * DS, 2:5, :].rearrange("p a b -> p (a b)")[:, 0:SKEYS], ACT.Relu)\
                   .then_inc(sem("srelu_ready"), 1)
            with eng.Fori(0, DB // 2) as i:
                for k in range(2):
                    decode_index(i * 2 + k, k)
            stage_end(eng, "C1")

            for qb in range(1, 4):
                n0 = 4 * (qb - 1)
                with eng.Fori(0, IH // 4) as i:
                    for h in range(4):
                        eng.wait_ge(sem("pdots_ready"), (i + n0) * 4 + (h + 1))
                        eng.wait_ge(sem("prelu_used"), (i + n0) * 4)
                        eng.activation(prelu[:, h, 0:P * (qb + 1)], ps[:, h, 0:P * (qb + 1)], ACT.Relu)\
                           .then_inc(sem("pdots_kept"), 1)
            eng.wait_ge(sem("prelu_used"), 3 * IH)
            with eng.Fori(0, 4) as i:
                for j in range(4):
                    eng.wait_ge(sem("zatt_ready"), i * 4 + (j + 1))
                    eng.wait_ge(sem(f"zt{j % 2}_out"), i * 32 + 16 * (j // 2))
                    eng.activation(zt[:, j % 2, :].rearrange("p (a b) -> p a b", a=2),
                                   ps[:, 2 * (j % 2):2 * (j % 2) + 2, 0:HALF], ACT.Silu).then_inc(sem("zatt_kept"), 1)
            stage_end(eng, "C2")

            eng.wait_ge(sem("selrow_in"), 16)
            eng.copy(selrow, selrow_f)

            def exponentials(qb, m):
                nk = P * (qb + 1)
                for r in range(REP):
                    if not (isinstance(m, int) and m == 0):
                        eng.wait_ge(sem("p_turned"), m * REP + (r + 1 - REP))
                    eng.wait_ge(sem("nmx_ready"), m * REP + (r + 1))
                    eng.activation(pexp[:, r, 0:nk], ps[:, r, 0:nk], ACT.Exp, bias=nmx4[:, r:r + 1],
                                   scale=ATT_SCALE, accum_out=rsum4[:, r:r + 1]).then_inc(sem("pexp_ready"), 1)
            for qb in range(4):
                exponentials(qb, KVH * qb)
                with eng.Fori(KVH * qb + 1, KVH * qb + KVH) as m:
                    exponentials(qb, m)
            stage_end(eng, "C3a")

            def decode_attention(n, k):
                for g in (0, 2):
                    eng.wait_ge(sem("kb_turned"), n * KVH + (g + 1))
                    eng.copy(kTb[:, 0, :], ps[:, 0:2, :].rearrange("p a b -> p (a b)")).then_inc(sem("kTb0_kept"), 1)
                eng.wait_ge(sem("snmx_ready"), n + 1)
                eng.wait_ge(sem("s_turned"), n)
                eng.activation(sexp, ps[:, 2:5, :].rearrange("p a b -> p (a b)")[:, 0:SKEYS], ACT.Exp, bias=nmx[:, :],
                               scale=ATT_SCALE, accum_out=rsum[:, :]).then_inc(sem("sraw_ready"), 1)
                eng.wait_ge(sem("s_turned"), n + 1)
                eng.wait_ge(sem("so_ready"), n)
                eng.copy(sT[:, 0:PAGES, :].rearrange("p a b -> p (a b)"), ps[:, 5:7, :].rearrange("p a b -> p (a b)"))
                eng.copy(sT[0:NS, PAGES, :], ps[0:NS, 7, 0:P]).then_inc(sem("sT_kept"), 1)
            with eng.Fori(0, DB // 2) as i:
                for k in range(2):
                    decode_attention(i * 2 + k, k)
            stage_end(eng, "C3")

            eng.wait_ge(sem("yatt_out"), 16)

            def keep_slot(g, n):
                pair = 2 * (n % 2)
                eng.wait_ge(sem("projT_ready"), g * 10 + (n + 1))
                if n < NJ:
                    eng.wait_ge(sem("conv_done"), g * NJ)
                    eng.copy(raw[:, n, CW - 1:CW - 1 + HALF], ps[:, pair, 0:HALF])
                    eng.copy(raw[:, n, CW - 1 + HALF:RAW_S], ps[:, pair + 1, 0:SEQ - HALF])
                    eng.copy(raw[:, n, RAW_S:RAW].rearrange("p (b k) -> p b k", b=DB)[:, :, CW - 1:],
                             ps[:, pair + 1, SEQ - HALF:HALF].rearrange("p (b k) -> p b k", b=DB))\
                       .then_inc(sem("projT_kept"), 1)
                else:
                    eng.wait_ge(sem("zs_ready"), g)
                    eng.copy(zraw[:, n - NJ, :].rearrange("p (a b) -> p a b", a=2), ps[:, pair:pair + 2, 0:HALF])\
                       .then_inc(sem("projT_kept"), 1)

            def activate_group(g):
                for j in range(NJ):
                    eng.wait_ge(sem("conv_done"), g * NJ + (j + 1))
                    eng.activation(xact[:, j, 0:SEQ], acc[:, j % 2, 0:SEQ], ACT.Silu)
                    eng.activation(xact[:, j, SEQ:NT].rearrange("p (b k) -> p b k", b=DB), decode_acc(j), ACT.Silu)\
                       .then_inc(sem("xact_ready"), 1)
                eng.wait_ge(sem("projT_kept"), g * 10 + 11)
                eng.activation(zs, zraw, ACT.Silu).then_inc(sem("zs_ready"), 1)

            def state_copies(g, half):
                for b in range(4):
                    eng.wait_ge(sem("st_turned"), g * 8 + (4 * half + b + 1))
                    eng.copy(ST[:, b % 2, :], ps[:, 4 + b % 2, :]).then_inc(sem("ST_kept"), 1)

            def scan_before(g, n):
                if n == 0:
                    activate_group(g)
                if n == 6:
                    eng.wait_ge(sem("final_turned"), g + 1)
                    eng.copy(fsb, ps[:, 5, :]).then_inc(sem("fsb_ready"), 1)
                    state_copies(g, 0)
                if n == 8:
                    state_copies(g, 1)
                if 1 <= n <= 5:
                    R_ = ROWS[n - 1]
                    eng.wait_ge(sem("seg_masked"), g * 5 + n)
                    eng.activation(E[0:R_, :, 0:R_], E[0:R_, :, 0:R_], ACT.Exp).then_inc(sem("decay_ready"), 1)
                if n == 9:
                    eng.wait_ge(sem("c_done"), g * 5 + 5)
                    eng.activation(sq[:, 0:4, :], yT, ACT.Square).then_inc(sem("sq_ready"), 1)

            def scan_after(g, n):
                if n == 9:
                    root(rn, g + ROOTS_E)
                if n == 1:
                    eng.wait_ge(sem("tails_turned"), g + 1)
                    eng.wait_ge(sem("tails_out"), g * 96)
                    eng.copy(cno[:, 0:4 * P], ps[0:NC, 7, :])
                    eng.copy(cno[:, 4 * P:6 * P], ps[0:NC, 5, 0:2 * P]).then_inc(sem("cno_ready"), 1)
                if 1 <= n <= 4:
                    eng.wait_ge(sem("a_ready"), g * 5 + n)
                    eng.copy(Btok, ps[:, 5, 0:P]).then_inc(sem("btok_ready"), 1)

            for n in range(10):
                keep_slot(0, n)
            with eng.Fori(1, SG) as i:
                for n in range(10):
                    scan_before(i - 1, n)
                    scan_after(i - 1, n)
                    keep_slot(i, n)
            for n in range(10):
                scan_before(SG - 1, n)
                scan_after(SG - 1, n)
                eng.wait_ge(sem("projT_ready"), SG * 10 + n + 1)
                eng.wait_ge(sem("cn_ready"), SG)
                eng.wait_ge(sem("zs_ready"), SG)
                eng.activation(early[:, n, :].rearrange("p (a b) -> p a b", a=2),
                               ps[:, 2 * (n % 2):2 * (n % 2) + 2, 0:HALF], ACT.Sigmoid).then_inc(sem("projT_kept"), 1)
            stage_end(eng, "E", wait=False)
            eng.wait_ge(sem("yn_done"), SG)
            eng.wait_ge(sem("tails_out"), 96 * SG)

            def gates(i, both_gates):
                if both_gates:
                    for j in range(FT):
                        eng.wait_ge(sem("ga_ready"), i * 2 + (j + 1))
                        eng.wait_ge(sem("merged_out"), i * 32)
                        eng.activation(gateA[:, j, :].rearrange("p (a b) -> p a b", a=2), ps[:, 2 * j:2 * j + 2, 0:HALF],
                                       ACT.Sigmoid).then_inc(sem("ga_kept"), 1)
                for j in range(FT):
                    eng.wait_ge(sem("gs_ready"), i * 2 + (j + 1))
                    eng.wait_ge(sem("merged_ready"), i * 2)
                    eng.activation(gateS[:, j, :].rearrange("p (a b) -> p a b", a=2), ps[:, 4 + 2 * j:6 + 2 * j, 0:HALF],
                                   ACT.Sigmoid).then_inc(sem("gs_kept"), 1)
            with eng.Fori(0, LATE) as i:
                gates(i, True)
            with eng.Fori(LATE, NF) as i:
                gates(i, False)

            for t in range(TT):
                eng.wait_ge(sem("h_added"), 7 * TT + t + 1)
                eng.activation(gsq[0:ROWS[t], :], h_out[0:ROWS[t], t, :], ACT.Square,
                               accum_out=sumsq[0:ROWS[t], t:t + 1]).then_inc(sem("sumsq_h"), 1)
                root(rstd[0:ROWS[t], t:t + 1], ROOTS_G + t)

        @block.vector
        def _(eng):
            steps = Steps(eng, sem("dve_steps"))
            R_S = PAST + NS

            def inverse_rms(dst, src, width, n):
                steps.add(eng.tensor_scalar(dst, src, 1.0 / width, EPS, ALU.mult, ALU.add))
                steps.wait()
                eng.reciprocal(dst, dst).then_inc(sem("inverse_ready"), 1)
                eng.wait_ge(sem("root_ready"), n + 1)

            def keep_xT(t):
                eng.wait_ge(sem("xT_turned"), t + 1)
                eng.wait_ge(sem("rows_kept"), 3)
                for q in range(4):
                    ins = eng.tensor_tensor(xnT[:, 4 * q:4 * q + 4, tok(t)],
                                            ps[:, 4 * (t % 2) + q, :].rearrange("p (a b) -> p a b", a=4)[:, :, 0:ROWS[t]],
                                            bc(gT[:, 4 * q:4 * q + 4], [P, 4, ROWS[t]], 2), ALU.mult)
                ins.then_inc(sem("xnT_kept"), 1)
            for t in range(TT):
                r = ROWS[t]
                eng.wait_ge(sem("sumsq_x"), t + 1)
                inverse_rms(rstd[0:r, t:t + 1], sumsq[0:r, t:t + 1], D_MODEL, t)
                eng.tensor_scalar(xt[0:r, t % 2, :], xt[0:r, t % 2, :], rstd[0:r, t:t + 1], None, ALU.mult)\
                   .then_inc(sem("x_scaled"), 1)
                if t:
                    keep_xT(t - 1)
            keep_xT(TT - 1)
            stage_end(eng, "A")

            def rotate(n, m, t, src, heads, width, tab, free):
                r, hw_ = ROWS[t], width // 2
                cos = bc(rope[0:r, t, tab:tab + hw_], [r, heads * 2, hw_], 1)
                sin = bc(rope[0:r, t, tab + hw_:tab + width], [r, heads * 2, hw_], 1)
                v = src.rearrange("p (a b) -> p a b", b=hw_)
                shaped = lambda x: x[0:r, 0:heads * width].rearrange("p (a b) -> p a b", b=hw_)
                eng.wait_ge(sem("rot_ready"), m)
                eng.tensor_tensor(shaped(tcos), v, cos, ALU.mult)
                eng.tensor_tensor(shaped(tsin), v, sin, ALU.mult).then_inc(sem("tok_kept"), 1)
                eng.wait_ge(sem("tok_kept"), n + (1 + TOK0))
                eng.wait_ge(sem("rot_turned"), m if t == 0 else m - 1)
                free()
                four = lambda x: x[0:r, 0:heads * width].rearrange("p (a two b) -> p a two b", two=2, b=hw_)
                o, c_, s_ = four(rot[:, t % 2, :]), four(tcos), four(tsin)
                eng.tensor_tensor(o[:, :, 0, :], c_[:, :, 0, :], s_[:, :, 1, :], ALU.subtract)
                eng.tensor_tensor(o[:, :, 1, :], c_[:, :, 1, :], s_[:, :, 0, :], ALU.add).then_inc(sem("rot_ready"), 1)

            def rotate_slab(n, m, heads, width, tab, free=lambda t: None):
                for t in range(TT):
                    eng.wait_ge(sem("tok_ready"), n + (t + 1))
                    rotate(n + t, m + t, t, ps[0:ROWS[t], t, 0:SLAB], heads, width, tab, lambda: free(t))

            with eng.Fori(0, 4) as i:
                for s in range(2):
                    rotate_slab(i * 10 + 5 * s, i * 10 + 5 * s, 2, HD, 0)
            rows_out = [0, 0]

            def sent(t):
                eng.wait_ge(sem(f"rot{t % 2}_out"), 16 * rows_out[t % 2])
                rows_out[t % 2] += 1
            for s in range(2):
                rotate_slab(40 + 5 * s, 40 + 5 * s, 2, HD, 0, sent)
            for s in range(2):
                for t in range(TT):
                    eng.wait_ge(sem("tok_ready"), 50 + 5 * s + t + 1)
                    eng.tensor_copy(vtok[0:ROWS[t], t, s * SLAB:(s + 1) * SLAB], ps[0:ROWS[t], t, 0:SLAB])\
                       .then_inc(sem("tok_kept"), 1)
            for k in range(2):
                eng.wait_ge(sem(f"rot{k}_out"), 16 * rows_out[k])
            with eng.Fori(6, 8) as i:
                for s in range(2):
                    rotate_slab(i * 10 + 5 * s, i * 10 + (5 * s - 10), IH // 4, ID, HD)
            for t in range(TT):
                r = ROWS[t]
                eng.wait_ge(sem("tok_ready"), 80 + t + 1)
                src = ps[0:r, t, 0:ID]
                steps.add(eng.bn_stats(lnst[0:r, :], src))
                steps.wait()
                steps.add(eng.bn_aggr(lnagg[0:r, :], lnst[0:r, :]))
                steps.wait()
                inverse_rms(lnr[0:r, :], lnagg[0:r, 1:2], 1, ROOTS_B + t)
                kk = kin[0:r, t % 2, :]
                steps.add(eng.tensor_scalar(kk, src, lnagg[0:r, 0:1], lnr[0:r, :], ALU.subtract, ALU.mult))
                steps.add(eng.tensor_scalar(wi_tok[0:r, t, :], ps[0:r, t, ID:ID + IH], IDX_SCALE, None, ALU.mult))
                steps.wait()
                steps.add(eng.tensor_tensor(kk, kk, lnw[0:r, :], ALU.mult))
                steps.wait()
                steps.add(eng.tensor_tensor(kk, kk, lnb[0:r, :], ALU.add))
                steps.wait()
                rotate(80 + t, 70 + t, t, kk, 1, ID, HD, lambda: sent(t))
            for k in range(2):
                eng.wait_ge(sem(f"rot{k}_out"), 16 * rows_out[k])
            eng.wait_ge(sem("rot_turned"), 75)
            eng.wait_ge(sem("dt_exp_ready"), 2)
            eng.tensor_scalar(dtU, dtE, 1.0, None, ALU.add).then_inc(sem("dt_u_ready"), 1)
            eng.wait_ge(sem("dt_u_ready"), 1)
            steps.add(eng.reciprocal(dtR, dtU))
            steps.add(eng.scalar_tensor_tensor(dtE, dtU, -1.0, dtE, ALU.add, ALU.subtract))
            steps.wait()
            steps.add(eng.tensor_tensor(dtE, dtE, dtR, ALU.mult))
            steps.wait()
            eng.wait_ge(sem("dt_ln_ready"), 1)
            steps.add(eng.tensor_tensor(dtL, dtL, dtE, ALU.subtract))
            steps.wait()
            eng.scalar_tensor_tensor(dtT, dtT, 0.0, dtL, ALU.max, ALU.add).then_inc(sem("dtT_ready"), 1)
            eng.wait_ge(sem("dtT_ready"), 1)
            steps.add(eng.tensor_scalar(dtE, dtT, c_aneg[0:SH, :], -1.0, ALU.mult, ALU.mult))
            steps.add(eng.memset(dtL, 1.0))
            steps.wait()
            steps.add(eng.memset(dtL[:, 0:SEQ:P], 0.0))
            steps.add(eng.memset(dtL[:, SEQ:NT:DS], 0.0))
            steps.wait()
            eng.tensor_tensor_scan(dtU, dtL, dtE, 0.0, ALU.mult, ALU.add).then_inc(sem("dtT_ready"), 1)
            for k, dst in enumerate((dt_tok, acs_tok)):
                eng.wait_ge(sem("dt_turned"), k + 1)
                eng.tensor_copy(dst[:, 0:4, :], ps[:, k, 0:4 * SH].rearrange("p (a b) -> p a b", a=4))
                eng.tensor_copy(dst[0:NS, 4, :], ps[0:NS, k, 4 * SH:5 * SH]).then_inc(sem("acs_kept"), 1)
            eng.wait_ge(sem("last_in"), 32)
            eng.tensor_tensor(dec_tok[:, 0:4, :], cdec[:, :, :], acs_tok[:, 0:4, :], ALU.subtract).then_inc(sem("dec_ready"), 1)
            eng.tensor_tensor(dec_tok[0:NS, 4, :], dec_tok[0:NS, 4, :], acs_tok[0:NS, 4, :], ALU.subtract)\
               .then_inc(sem("dec_ready"), 1)
            eng.wait_ge(sem("decS_ready"), 1)
            eng.tensor_copy(decS.rearrange("p a b -> p (a b)"), ps[:, 2, 0:SH // 2 * DB])
            stage_end(eng, "B")

            eng.wait_ge(sem("idx_consts_in"), 32)
            eng.wait_ge(sem("wcol_in"), 16 * DB)

            def decode_index(n, k):
                eng.wait_ge(sem("sscore_added"), n)
                apart(eng)
                eng.tensor_copy(qis[:, k * IH * DS:(k + 1) * IH * DS].rearrange("p (a b) -> p a b", a=IH),
                                qiT[0:ID, :, bass.ds(n * DS + SEQ, DS)])
                eng.tensor_tensor(hw[:, k, :], headmask[:, bass.ds(n, 1), :].rearrange("p a b -> p (a b)"),
                                  wcol[:, bass.ds(n, 1)].to_broadcast([IH * DS, NS]), ALU.mult)\
                   .then_inc(sem("qis_ready"), 1)
            with eng.Fori(0, DB // 2) as i:
                for k in range(2):
                    decode_index(i * 2 + k, k)
            eng.wait_ge(sem("sscore_added"), DB + 1)
            eng.tensor_copy(ssc, ps[0:NS, 5:8, :].rearrange("p a b -> p (a b)")[:, 0:SKEYS])
            stage_end(eng, "C1")

            steps.add(eng.memset(psc, 0.0))
            steps.wait()
            for qb in range(1, 4):
                steps.add(eng.tensor_copy(psc[:, qb - 1, qb * P:(qb + 1) * P], causal_q[:, :]))
            steps.wait()
            STEPS = IH // 4

            def stage_index_queries(qb, i):
                eng.tensor_copy(qist, qiT[0:ID, bass.ds(i * 4, 4), tok(qb)]).then_inc(sem("qist_ready"), 1)

            def add_heads(qb, i, following):
                m = i + STEPS * (qb - 1)
                row = psc[:, qb - 1, 0:P * (qb + 1)]
                steps.add(eng.tensor_copy(wi4, wi_tok[:, qb, bass.ds(i * 4, 4)]))
                steps.wait()
                for h in range(4):
                    if h == 3 and following:
                        eng.wait_ge(sem("pdots_ready"), m * 4 + 4)
                        apart(eng)
                        stage_index_queries(*following)
                    eng.wait_ge(sem("pdots_kept"), m * 4 + (h + 1))
                    eng.scalar_tensor_tensor(row, prelu[:, h, 0:P * (qb + 1)], wi4[:, h:h + 1], row, ALU.mult, ALU.add)\
                       .then_inc(sem("prelu_used"), 1)
                    eng.wait_ge(sem("prelu_used"), m * 4 + (h + 1))
            stage_index_queries(1, 0)
            for qb in range(1, 4):
                with steps.loop(0, STEPS - 1, 1) as i:
                    add_heads(qb, i, (qb, i + 1))
                add_heads(qb, STEPS - 1, (qb + 1, 0) if qb < 3 else None)

            rows = [(ssc, NS)] + [(psc[:, qb - 1, 0:P * (qb + 1)], P) for qb in range(1, 4)]

            def take_eight(which):
                for n in which:
                    v, r = rows[n]
                    steps.add(eng.max(top8[0:r, n, :], v))
                steps.wait()
                apart(eng)
                for n in which:
                    v, r = rows[n]
                    steps.add(eng.match_replace(v, top8[0:r, n, :], v, PICKED))
                steps.wait()
                apart(eng)
            assert TOPK_S == 2 * TOPK_P
            with steps.loop(0, TOPK_P // 8, 10):
                take_eight((0, 1, 2))
                take_eight((0, 3))
            for qb in range(1, 4):
                nk = P * (qb + 1)
                eng.tensor_scalar(pmask[:, qb, 0:nk], psc[:, qb - 1, 0:nk], PICKED, NEG, ALU.not_equal, ALU.mult)
            eng.tensor_copy(pmask[:, 0, 0:P], causal_q[:, :])
            eng.tensor_scalar(smask, ssc, PICKED, NEG, ALU.not_equal, ALU.mult)
            stage_end(eng, "C2")

            def stage_queries(qb, m):
                g = m - KVH * qb
                eng.tensor_copy(qst, qkT[:, bass.ds(g * REP, REP), tok(qb)]).then_inc(sem("qst_ready"), 1)

            def maximum(qb, m, r):
                eng.wait_ge(sem("pscore_ready"), m * REP + (r + 1))
                steps.add(eng.tensor_reduce(mx4[:, r:r + 1], ps[:, r, 0:P * (qb + 1)], AX.X, ALU.max))
                steps.wait()
                eng.tensor_scalar(nmx4[:, r:r + 1], mx4[:, r:r + 1], -ATT_SCALE, None, ALU.mult)\
                   .then_inc(sem("nmx_ready"), 1)

            def gate_output(qb, m):
                g = m - KVH * qb
                eng.wait_ge(sem("on_turned"), m + 1)
                eng.wait_ge(sem("zg_in"), m * 16 + 16)
                eng.tensor_tensor(qkT[:, bass.ds(g * REP, REP), tok(qb)],
                                  ps[:, 7, :].rearrange("p (a b) -> p a b", a=REP), zg[:, :, :], ALU.mult)\
                   .then_inc(sem("poT_kept"), 1)

            def attend(qb, n, first, more):
                if more:
                    eng.wait_ge(sem("pscore_ready"), n * REP + REP)
                    eng.wait_ge(sem("poT_kept"), n if first else n - 1)
                    apart(eng)
                    stage_queries(qb, n + 1)
                eng.wait_ge(sem("on_ready"), n)
                for r in range(REP):
                    eng.wait_ge(sem("p_turned"), n * REP + (r + 1))
                    steps.add(eng.reciprocal(rinv4[:, r:r + 1], rsum4[:, r:r + 1]))
                    eng.tensor_copy(pT[:, r % 2, 0:P * (qb + 1)], ps[:, 4 + r % 2, 0:P * (qb + 1)])\
                       .then_inc(sem("pT_kept"), 1)
                    if r == 0 and not first:
                        gate_output(qb, n - 1)
                    if more:
                        maximum(qb, n + 1, r)
                steps.wait()
                eng.wait_ge(sem("po_ready"), n * REP + REP)
                eng.tensor_tensor(on, ps[:, 6, :].rearrange("p (a b) -> p a b", a=REP), bc(rinv4, [P, REP, HD], 2),
                                  ALU.mult).then_inc(sem("on_ready"), 1)
            for qb in range(4):
                n0 = KVH * qb
                if qb:
                    eng.wait_ge(sem("pscore_ready"), n0 * REP)
                stage_queries(qb, n0)
                for r in range(REP):
                    maximum(qb, n0, r)
                attend(qb, n0, True, True)
                with steps.loop(n0 + 1, KVH - 2, 2 * REP) as n:
                    attend(qb, n, False, True)
                attend(qb, n0 + KVH - 1, False, False)
                gate_output(qb, n0 + KVH - 1)
                eng.wait_ge(sem("poT_kept"), n0 + KVH)
            stage_end(eng, "C3a")

            steps.add(eng.memset(qsb[:, :, REP * DS:], 0.0))
            steps.wait()
            eng.wait_ge(sem("zdec_in"), 16)

            def decode_attention(n, k):
                eng.wait_ge(sem("so_ready"), n)
                apart(eng)
                eng.tensor_copy(selst, selrow[:, bass.ds(n, 1), :].rearrange("p a b -> p (a b)"))
                eng.tensor_copy(qsb[:, :, 0:REP * DS].rearrange("p g (r d) -> p g r d", d=DS),
                                qkT[:, 0:QH, bass.ds(n * DS + SEQ, DS)].rearrange("p (g r) d -> p g r d", r=REP))\
                   .then_inc(sem("qsb_ready"), 1)
                for g in (1, 3):
                    eng.wait_ge(sem("kb_turned"), n * KVH + (g + 1))
                    eng.tensor_copy(kTb[:, 1, :], ps[:, 5:7, :].rearrange("p a b -> p (a b)")).then_inc(sem("kTb1_kept"), 1)
                eng.wait_ge(sem("dscore_done"), n * KVH + KVH)
                steps.add(eng.tensor_reduce(mx[:, :], ps[:, 2:5, :].rearrange("p a b -> p (a b)")[:, 0:SKEYS], AX.X, ALU.max))
                steps.wait()
                eng.tensor_scalar(nmx[:, :], mx[:, :], -ATT_SCALE, None, ALU.mult).then_inc(sem("snmx_ready"), 1)
                eng.wait_ge(sem("sraw_ready"), n + 1)
                steps.add(eng.reciprocal(rinv[:, :], rsum[:, :]))
                steps.wait()
                eng.tensor_scalar(sexp, sexp, rinv[:, :], None, ALU.mult).then_inc(sem("sexp_ready"), 1)
                eng.wait_ge(sem("so_ready"), n + 1)
                for g in range(KVH):
                    rows = slice(32 * g, 32 * g + 32)
                    ins = eng.tensor_copy(osb[rows, :], ps[rows, 0, g * HD:(g + 1) * HD])
                ins.then_inc(sem("osb_ready"), 1)
                eng.wait_ge(sem("o_turned"), n + 1)
                by_head = lambda v: v.rearrange("p (g r) d -> p g r d", g=KVH)
                eng.tensor_tensor(by_head(qkT[:, 0:QH, bass.ds(n * DS + SEQ, DS)]),
                                  ps[:, 7, 0:P].rearrange("p (g r d) -> p g r d", g=KVH, d=DS)[:, :, 0:REP, :],
                                  by_head(zdec[:, :, bass.ds(n * DS, DS)]), ALU.mult).then_inc(sem("so_kept"), 1)
            with steps.loop(0, DB // 2, 4) as i:
                for k in range(2):
                    decode_attention(i * 2 + k, k)
            stage_end(eng, "C3")

            eng.wait_ge(sem("yatt_out"), 16)

            eng.memset(raw[:, :, 0:CW - 1], 0.0)
            decode_raw = raw[:, :, RAW_S:RAW].rearrange("p j (b k) -> p j b k", b=DB)

            def convolve(g):
                eng.wait_ge(sem("yn_done"), g)
                steps.add(eng.tensor_copy(cw_g[:, 0:4, :], cwT[:, bass.ds(g * 4, 4), :]))
                steps.add(eng.tensor_copy(cw_g[:, 4:5, :], cwT[:, bass.ds(g + 4 * SG, 1), :]))
                steps.add(eng.tensor_copy(cw_g[:, 5:6, :], cwT[:, bass.ds(g + 5 * SG, 1), :]))
                steps.add(eng.tensor_copy(gn_g, gnT[:, bass.ds(g * 4, 4)]))
                steps.wait()
                for b in range(2):
                    steps.add(eng.tensor_copy(decode_raw[:, :, 4 * b:4 * b + 4, 0:CW - 1],
                                              cw_g[:, :, 12 * b:12 * b + 12].rearrange("p j (b k) -> p j b k", b=4)))
                steps.wait()
                eng.wait_ge(sem("projT_kept"), g * 10 + (NJ + 1))
                eng.wait_ge(sem("tails_turned"), g)
                eng.tensor_copy(cn[:, :, 0:CW - 1], raw[:, :, RAW_S - (CW - 1):RAW_S])
                eng.tensor_copy(cn[:, :, CW - 1:].rearrange("p j (b k) -> p j b k", b=DB), decode_raw[:, :, :, DS:])\
                   .then_inc(sem("cn_ready"), 1)
                eng.wait_ge(sem("final_out"), g * 16)
                for j in range(NJ):
                    eng.wait_ge(sem("xact_ready"), g * NJ + max(j - 1, 0))
                    at_ = acc[:, j % 2, 0:ACC]
                    tap = lambda k: cw_g[:, j, NSTATE + k:NSTATE + k + 1]
                    steps.add(eng.tensor_scalar(at_, raw[:, j, 0:ACC], tap(0), tap(CW), ALU.mult, ALU.add))
                    for k in range(1, CW):
                        steps.wait()
                        ins = eng.scalar_tensor_tensor(at_, raw[:, j, k:k + ACC], tap(k), at_, ALU.mult, ALU.add)
                        if k < CW - 1:
                            steps.add(ins)
                    ins.then_inc(sem("conv_done"), 1)

            per_head = lambda v, r: bc(v, [r, GH, SP_], 2)
            heads = lambda ap: ap.rearrange("p (a b) -> p a b", a=GH)

            def gate_chunk(g, ci):
                eng.wait_ge(sem("y_turned"), g * 5 + (ci + 1))
                if ci == 0:
                    eng.wait_ge(sem("yn_out"), g * 16)
                    eng.wait_ge(sem("zs_ready"), g + 1)
                eng.tensor_tensor(yT[:, :, tok(ci)], ps[:, 4, :].rearrange("p (a b) -> p a b", a=4)[:, :, 0:ROWS[ci]],
                                  zs[:, :, tok(ci)], ALU.mult).then_inc(sem("c_done"), 1)

            def finish_chunk(g, ci):
                r = ROWS[ci]
                y = heads(ytok[0:r, :])
                if ci < 4:
                    eng.wait_ge(sem("b_ready"), g * 4 + (ci + 1))
                else:
                    eng.wait_ge(sem("st_applied"), g * 8 + 8)
                ins = eng.tensor_tensor(y, heads(ps[0:r, 6, :]), xD[0:r], ALU.add)
                if ci:
                    steps.add(ins)
                    steps.wait()
                    steps.add(eng.tensor_tensor(xD[0:r], heads(ps[0:r, 7, :]),
                                                per_head(grow_tok[0:r, ci, bass.ds(g * GH, GH)], r), ALU.mult))
                    steps.wait()
                    ins = eng.tensor_tensor(y, y, xD[0:r], ALU.add)
                ins.then_inc(sem("ytok_ready"), 1)
                if ci == 0:
                    eng.tensor_copy(S, ps[:, 5, :]).then_inc(sem("s_ready"), 1)
                elif ci < 4:
                    steps.add(eng.tensor_tensor(heads(S), heads(S), per_head(cdec[:, ci, bass.ds(g * GH, GH)], P), ALU.mult))
                    steps.wait()
                    eng.tensor_tensor(S, S, ps[:, 5, :], ALU.add).then_inc(sem("s_ready"), 1)

            def segment_sums(g, ci):
                r = ROWS[ci]
                if ci == 0:
                    eng.wait_ge(sem("acs_in"), g * 16 + 16)
                eng.tensor_tensor(E[0:r, :, 0:r], acsbc[0:r, :, tok(ci)],
                                  bc(acs_tok[0:r, ci, bass.ds(g * GH, GH)], [r, GH, r], 2), ALU.subtract)\
                   .then_inc(sem("seg_ready"), 1)

            def factors(g, ci):
                r = ROWS[ci]
                eng.wait_ge(sem("a_ready"), g * 5 + (ci + 1))
                x = heads(ps[0:r, 4, :])
                eng.tensor_tensor(xdt[0:r], x, per_head(dt_tok[0:r, ci, bass.ds(g * GH, GH)], r), ALU.mult)\
                   .then_inc(sem("xdt_ready"), 1)
                steps.add(eng.tensor_tensor(xD[0:r], x, per_head(dskip[0:r, bass.ds(g * GH, GH)], r), ALU.mult))
                if ci == 4:
                    eng.tensor_tensor(Bblk, bc(ps[0:NS, 5, 0:NST], [NS, DB, NST], 1), bc(in_batch[:, :], [NS, DB, NST], 2),
                                      ALU.mult).then_inc(sem("bblk_ready"), 1)
                mask = causal_k[:, :] if ci < 4 else dec_k[:, :]
                steps.add(eng.tensor_tensor(cbm[0:r, 0:r], ps[0:r, 6, 0:r], mask, ALU.mult))
                steps.wait()
                eng.wait_ge(sem("decay_ready"), g * 5 + (ci + 1))
                eng.tensor_tensor(E[0:r, :, 0:r], E[0:r, :, 0:r], bc(cbm[0:r, 0:r], [r, GH, r], 1), ALU.mult)\
                   .then_inc(sem("m_ready"), 1)

            def new_states(g, half):
                eng.wait_ge(sem("st_applied"), g * 8 + (4 * half + 4))
                for b in range(4):
                    ins = eng.tensor_tensor(st[:, b], st[:, b],
                                            bc(decS[:, bass.ds(g * 4, 4), 4 * half + b:4 * half + b + 1]
                                               .rearrange("p a b -> p (a b)"), [P, 4, NST], 2), ALU.mult)
                steps.add(ins)
                steps.wait()
                for j in range(4):
                    eng.wait_ge(sem("st_added"), g * 8 + (4 * half + j + 1))
                    eng.tensor_tensor(st[:, :, j, :], st[:, :, j, :],
                                      ps[:, 4 + j % 2, :].rearrange("p (a b) -> p a b", a=4), ALU.add)\
                       .then_inc(sem("st_new"), 1)

            def normalise(g):
                eng.wait_ge(sem("sumsq_ready"), g + 1)
                inverse_rms(rn, ps[:, 6:8, 0:HALF], D_INNER // SG, g + ROOTS_E)
                for j in range(4):
                    ins = eng.scalar_tensor_tensor(yT[:, j, :], yT[:, j, :], gn_g[:, j:j + 1], rn_row, ALU.mult, ALU.mult)
                ins.then_inc(sem("yn_done"), 1)

            def scan_before(g, n):
                if n == 0:
                    convolve(g)
                if 3 <= n <= 6:
                    gate_chunk(g, n - 3)
                if 2 <= n <= 5:
                    finish_chunk(g, n - 2)
                if 1 <= n <= 5:
                    segment_sums(g, n - 1)
                if n == 6:
                    new_states(g, 0)
                if n == 8:
                    finish_chunk(g, 4)
                    new_states(g, 1)
                if n == 9:
                    gate_chunk(g, 4)

            def scan_after(g, n):
                if n == 1:
                    eng.wait_ge(sem("xact_ready"), g * NJ + NJ)
                    eng.tensor_tensor(Cm, bc(xact[:, 5, SEQ:NT], [P, DB, NS], 1), batch_cols[:, :, :], ALU.mult)\
                       .then_inc(sem("cm_ready"), 1)
                if 1 <= n <= 5:
                    factors(g, n - 1)
                if n == 9:
                    normalise(g)

            SCAN_STEPS = 48
            with steps.loop(0, SG, SCAN_STEPS) as g:
                for n in range(10):
                    scan_before(g, n)
                    scan_after(g, n)
            stage_end(eng, "E")

            def merge(i, dst, both_gates):
                for j in range(FT):
                    eng.wait_ge(sem("ya_ready"), i * 2 + (j + 1))
                    if both_gates:
                        eng.wait_ge(sem("ga_kept"), i * 2 + (j + 1))
                    else:
                        eng.wait_ge(sem("gate_in"), (i - LATE) * 16 + 16)
                    eng.tensor_tensor(gateA[:, j, :].rearrange("p (a b) -> p a b", a=2),
                                      gateA[:, j, :].rearrange("p (a b) -> p a b", a=2), ps[:, 2 * j:2 * j + 2, 0:HALF],
                                      ALU.mult).then_inc(sem("ya_used"), 1)
                for j in range(FT):
                    eng.wait_ge(sem("yb_ready"), i * 2 + (j + 1))
                    eng.tensor_tensor(gateS[:, j, :].rearrange("p (a b) -> p a b", a=2),
                                      gateS[:, j, :].rearrange("p (a b) -> p a b", a=2), ps[:, 4 + 2 * j:6 + 2 * j, 0:HALF],
                                      ALU.mult).then_inc(sem("yb_used"), 1)
                    eng.wait_ge(sem("yb_used"), i * 2 + (j + 1))
                    eng.tensor_tensor(dst(j), gateA[:, j, :], gateS[:, j, :], ALU.add).then_inc(sem("merged_ready"), 1)
            with eng.Fori(0, LATE) as i:
                merge(i, lambda j: gateA[:, j, :], True)
            with eng.Fori(LATE, NF - 1) as i:
                merge(i, lambda j: gateA[:, j, :], False)
            merge(NF - 1, lambda j: mergedT[:, KC - FT + j, :], False)

            def add_rows(i, s, t):
                eng.wait_ge(sem("h_ready"), i * 10 + (5 * s + t + 1))
                cs = slice((2 * i + s) * SLAB, (2 * i + s + 1) * SLAB) if isinstance(i, int) \
                    else bass.ds(i * (2 * SLAB) + s * SLAB, SLAB)
                h = h_out[0:ROWS[t], t, cs]
                eng.tensor_tensor(h, h, ps[0:ROWS[t], t, 0:SLAB], ALU.add).then_inc(sem("h_added"), 1)

            def finish_rows(t):
                r = ROWS[t]
                eng.wait_ge(sem("sumsq_h"), t + 1)
                inverse_rms(rstd[0:r, t:t + 1], sumsq[0:r, t:t + 1], D_MODEL, ROOTS_G + t)
                eng.scalar_tensor_tensor(h_out[0:r, t, :], h_out[0:r, t, :], rstd[0:r, t:t + 1], fg_bc[0:r, :],
                                         ALU.mult, ALU.mult).then_inc(sem("y_ready"), 1)
            eng.wait_ge(sem("resid_in"), 32)
            with eng.Fori(0, 3) as i:
                for s in range(2):
                    for t in range(TT):
                        add_rows(i, s, t)
            for t in range(TT):
                add_rows(3, 0, t)
            eng.wait_ge(sem("fg_in"), 16)
            for t in range(TT):
                add_rows(3, 1, t)
                if t:
                    finish_rows(t - 1)
            finish_rows(TT - 1)

        @block.gpsimd
        def _(eng):
            (y_p, y_s, k_p, v_p, ki_p, ssm_p, conv_p, k_s, v_s, ki_s, ssm_s, conv_s) = out
            for name in ("rotT_kept", "pT_kept", "zatt_kept", "projT_kept", "sscore_added"):
                eng.sem_inc(sem(name), 1)
            eng.sem_inc(sem("tok_kept"), TOK0)
            eng.memset(ones[:, :], 1.0)
            stage_end(eng, "A")
            flat = lambda ap: ap.rearrange("b t h d -> (b t) (h d)")
            kp, ks_, vp, vs = flat(k_p[0]), flat(k_s[0]), flat(v_p[0]), flat(v_s[0])
            kip, kis = ki_p[0, 0], ki_s[0].rearrange("b t d -> (b t) d")
            rows = lambda p_, s_, t: p_[tok(t), :] if t < 4 else s_
            for s in range(2):
                for t in range(TT):
                    eng.wait_ge(sem("rot_ready"), 40 + 5 * s + t + 1)
                    eng.dma_start(rows(kp, ks_, t)[:, s * SLAB:(s + 1) * SLAB], rot[0:ROWS[t], t % 2, :])\
                       .then_inc(sem(f"rot{t % 2}_out"), 16)
            eng.wait_ge(sem("tok_kept"), 60 + TOK0)
            eng.dma_start(vp.rearrange("(a p) n -> p a n", p=P), vtok[:, 0:4, :]).then_inc(sem("v_out"), 16)
            eng.dma_start(vs, vtok[0:NS, 4, :]).then_inc(sem("v_out"), 16)
            for t in range(TT):
                eng.wait_ge(sem("rot_ready"), 70 + t + 1)
                eng.dma_start(rows(kip, kis, t), rot[0:ROWS[t], t % 2, 0:ID]).then_inc(sem(f"rot{t % 2}_out"), 16)
            eng.wait_ge(sem("dtT_ready"), 2)
            eng.dma_start(acsT_dram, dtU).then_inc(sem("acsT_out"), 16)
            eng.wait_ge(sem("acs_kept"), 2)
            eng.dma_start(acs_dram[0:4].rearrange("t p n -> p t n"), acs_tok[:, 0:4, :]).then_inc(sem("acs_out"), 16)
            eng.dma_start(acs_dram[4, 0:NS, :], acs_tok[0:NS, 4, :]).then_inc(sem("acs_out"), 16)
            eng.dma_start(wi_dram, wi_tok[0:NS, 4, :]).then_inc(sem("acs_out"), 16)
            eng.wait_ge(sem("acs_out"), 48)
            eng.dma_start(cdec[:, :, :], acs_dram[0:4, P - 1, :].partition_broadcast(P)).then_inc(sem("last_in"), 16)
            eng.dma_start(dec_tok[0:NS, 4, :],
                          bc(acs_dram[4, DS - 1:NS:DS, :], [DB, DS, SH], 1)).then_inc(sem("last_in"), 16)
            eng.wait_ge(sem("rot0_out"), 16 * (6 + 3))
            eng.wait_ge(sem("rot1_out"), 16 * (4 + 2))
            eng.wait_ge(sem("v_out"), 32)
            eng.wait_ge(sem("acsT_out"), 16)
            stage_end(eng, "B")

            cache_ki = a["cache_idx_k"][0]

            def page_of(n, p):
                return eng.value_load(pt_sb[0:1, bass.ds(n * PAGES + p, 1)], min_val=0, max_val=NPHYS - 1)

            def index_pages(n, k):
                for p in range(PAGES):
                    eng.dma_start(kidx[:, k, p * ID:(p + 1) * ID], cache_ki[bass.ds(page_of(n, p), 1)]
                                  .rearrange("a p n -> (a p) n")).then_inc(sem(f"kidx{k}_in"), 16)
            for k in range(2):
                index_pages(k, k)
            with eng.Fori(1, DB // 2) as i:
                for k in range(2):
                    eng.wait_ge(sem("kis_turned"), i * 2 + (k - 1))
                    index_pages(i * 2 + k, k)
            stage_end(eng, "C1")

            ck, cv = (a[x][0].rearrange("n p h d -> n p (h d)") for x in ("cache_k", "cache_v"))

            def key_pages(n, k):
                for p in range(PAGES):
                    eng.dma_start(Kb[:, k * PAGES + p, :], ck[bass.ds(page_of(n, p), 1)].rearrange("a p n -> (a p) n"))\
                       .then_inc(sem(f"kpage{k}_in"), 16)

            def value_pages(n, k):
                for p in range(PAGES):
                    eng.dma_start(Vb[k][:, p, :], cv[bass.ds(page_of(n, p), 1)].rearrange("a p n -> (a p) n"))\
                       .then_inc(sem(f"vpage{k}_in"), 16)
            value_pages(0, 0)
            with eng.Fori(0, 4) as i:
                for j in range(4):
                    eng.wait_ge(sem("zatt_kept"), i * 4 + (j + 2))
                    apart(eng)
                    eng.dma_start(zatt_dram[:, bass.ds(i * (4 * NT) + j * NT, NT)], zt[:, j % 2, :])\
                       .then_inc(sem(f"zt{j % 2}_out"), 16)
            for k in range(2):
                eng.wait_ge(sem(f"zt{k}_out"), 16 * QH // 2)
            stage_end(eng, "C2")
            eng.dma_start(selrow_f, c["selrow"]).then_inc(sem("selrow_in"), 16)
            zatt = zatt_dram.rearrange("p (h n) -> p h n", h=QH)
            for qb in range(4):
                with eng.Fori(0, KVH) as g:
                    eng.wait_ge(sem("poT_kept"), g + KVH * qb)
                    apart(eng)
                    eng.dma_start(zg[:, :, :], zatt[:, bass.ds(g * REP, REP), tok(qb)]).then_inc(sem("zg_in"), 16)
                if qb < 2:
                    key_pages(qb, qb)
            stage_end(eng, "C3a")
            eng.dma_start(zdec, zatt[:, :, SEQ:NT]).then_inc(sem("zdec_in"), 16)
            value_pages(1, 1)
            with eng.Fori(1, DB // 2) as i:
                for k in range(2):
                    eng.wait_ge(sem("kb_turned"), i * (2 * KVH) + (k - 1) * KVH)
                    apart(eng)
                    key_pages(i * 2 + k, k)
                    eng.wait_ge(sem("so_ready"), i * 2 + (k - 1))
                    apart(eng)
                    value_pages(i * 2 + k, k)
            stage_end(eng, "C3")
            eng.dma_start(yatt_dram, qkT[:, 0:QH, :].rearrange("p a b -> p (a b)")).then_inc(sem("yatt_out"), 16)
            eng.wait_ge(sem("yatt_out"), 16)

            state_in = a["state_ssm"][0].rearrange("b (t q) p n -> b t (q p) n", q=2)
            state_out = ssm_s[0].rearrange("b (t q) p n -> b t (q p) n", q=2)
            final_out = ssm_p[0, 0].rearrange("(t q) p n -> t (q p) n", q=2)
            conv_rows = conv_s[0].rearrange("b k n -> (b k) n")

            def state_loads(g, half):
                for b in range(4):
                    eng.dma_start(st[:, b], state_in[4 * half + b, bass.ds(g * 4, 4)].rearrange("t q n -> q t n"))\
                       .then_inc(sem("st_in"), 16)

            def state_stores(g, half):
                eng.wait_ge(sem("st_new"), g * 8 + (4 * half + 4))
                apart(eng)
                for b in range(4):
                    eng.dma_start(state_out[4 * half + b, bass.ds(g * 4, 4)].rearrange("t q n -> q t n"), st[:, b])\
                       .then_inc(sem("st_out"), 16)
                eng.wait_ge(sem("st_out"), g * 128 + (64 * half + 64))

            def chunk_work(g, ci):
                r = ROWS[ci]
                mask = causal_k[:, :] if ci < 4 else dec_k[:, :]
                eng.wait_ge(sem("seg_ready"), g * 5 + (ci + 1))
                eng.tensor_tensor(E[0:r, :, 0:r], E[0:r, :, 0:r], bc(mask, [r, GH, r], 1), ALU.mult)\
                   .then_inc(sem("seg_masked"), 1)
                eng.wait_ge(sem("xdt_ready"), g * 5 + (ci + 1))
                eng.tensor_tensor(xdtd[0:r], xdt[0:r], bc(dec_tok[0:r, ci, bass.ds(g * GH, GH)], [r, GH, SP_], 2), ALU.mult)\
                   .then_inc(sem("xdtd_ready"), 1)

            with eng.Fori(0, SG) as g:
                eng.wait_ge(sem("yn_done"), g)
                apart(eng)
                eng.dma_start(acsbc, acsT_dram[bass.ds(g * GH, GH), :].partition_broadcast(P)).then_inc(sem("acs_in"), 16)
                state_loads(g, 0)
                for ci in range(5):
                    chunk_work(g, ci)
                    if ci == 0:
                        eng.wait_ge(sem("cno_ready"), g + 1)
                        for c0, w, col in ((0, 4 * P, g * (4 * P)), (4 * P, P, g * P + D_INNER),
                                           (5 * P, P, g * P + (D_INNER + SG * NST))):
                            apart(eng)
                            eng.dma_start(conv_p[0, 0, :, bass.ds(col, w)], cno[0:CW - 1, c0:c0 + w])\
                               .then_inc(sem("tails_out"), 16)
                            eng.dma_start(conv_rows[:, bass.ds(col, w)], cno[CW - 1:NC, c0:c0 + w])\
                               .then_inc(sem("tails_out"), 16)
                eng.wait_ge(sem("fsb_ready"), g + 1)
                apart(eng)
                eng.dma_start(final_out[bass.ds(g * 4, 4)].rearrange("t q n -> q t n"),
                              fsb.rearrange("p (t n) -> p t n", t=4)).then_inc(sem("final_out"), 16)
                state_stores(g, 0)
                state_loads(g, 1)
                state_stores(g, 1)
                eng.wait_ge(sem("yn_done"), g + 1)
                apart(eng)
                eng.dma_start(yssd_dram[:, bass.ds(g * (4 * NT), 4 * NT)], yT.rearrange("p a b -> p (a b)"))\
                   .then_inc(sem("yn_out"), 16)
            eng.wait_ge(sem("projT_kept"), 10 * (SG + 1) + 1)
            eng.dma_start(early_dram, early.rearrange("p a b -> p (a b)")).then_inc(sem("early_out"), 16)
            eng.wait_ge(sem("yn_out"), 16 * SG)
            eng.wait_ge(sem("tails_out"), 96 * SG)
            eng.wait_ge(sem("final_out"), 16 * SG)
            stage_end(eng, "E")

            eng.wait_ge(sem("early_out"), 16)
            eng.dma_start(yattF.rearrange("p a b -> p (a b)"), yatt_dram).then_inc(sem("yatt_in"), 16)
            eng.dma_start(yssdF.rearrange("p a b -> p (a b)"), yssd_dram).then_inc(sem("yssd_in"), 16)

            def load_gates(i):
                eng.wait_ge(sem("merged_out"), i * 32)
                if not isinstance(i, int):
                    apart(eng)
                eng.dma_start(gateA.rearrange("p a b -> p (a b)"), early_dram[:, bass.ds((i - LATE) * (FT * NT), FT * NT)])\
                   .then_inc(sem("gate_in"), 16)

            def merged_tiles(i):
                for j in range(FT):
                    eng.wait_ge(sem("merged_ready"), i * 2 + (j + 1))
                    apart(eng)
                    eng.dma_start(merged_dram[:, bass.ds(i * (2 * NT) + j * NT, NT)], gateA[:, j, :])\
                       .then_inc(sem("merged_out"), 16)
            with eng.Fori(0, LATE) as i:
                merged_tiles(i)
            with eng.Fori(LATE, NF - 1) as i:
                load_gates(i)
                merged_tiles(i)
            load_gates(NF - 1)
            eng.wait_ge(sem("merged_out"), 16 * (KC - FT))
            eng.wait_ge(sem("ya_ready"), KC)
            eng.dma_start(mergedT[:, 0:KC - FT, :].rearrange("p a b -> p (a b)"), merged_dram[:, 0:(KC - FT) * NT])\
               .then_inc(sem("merged_in"), 16)
            eng.wait_ge(sem("yb_ready"), KC)
            eng.dma_start(h_out[:, 0:4, :], a["x_prompt"][0].rearrange("(t p) n -> p t n", p=P)).then_inc(sem("resid_in"), 16)
            eng.dma_start(h_out[0:NS, 4, :], a["x_sample"].rearrange("b t d -> (b t) d")).then_inc(sem("resid_in"), 16)
            eng.dma_start(fg_bc, a["final_norm_g"].partition_broadcast(P)).then_inc(sem("fg_in"), 16)
            eng.wait_ge(sem("fg_in"), 16)


_NAMES = ["x_prompt", "x_sample", "cache_k", "cache_v", "cache_idx_k", "state_ssm", "state_conv", "page_table",
          "norm_g", "w_in", "conv_w", "conv_b", "dt_bias", "a_log", "d_skip", "ssd_norm_g", "idx_ln_w", "idx_ln_b",
          "w_branch", "w_out", "final_norm_g"]
_OUTS = [(1, SEQ, D_MODEL), (DB, DS, D_MODEL), (1, 1, SEQ, KVH, HD), (1, 1, SEQ, KVH, HD), (1, 1, SEQ, ID),
         (1, 1, SH, SP_, NST), (1, 1, CW - 1, CONV_DIM), (1, DB, DS, KVH, HD), (1, DB, DS, KVH, HD), (1, DB, DS, ID),
         (1, DB, SH, SP_, NST), (1, DB, CW - 1, CONV_DIM)]


def kernel(**inputs):
    import concourse.bacc as bacc
    from concourse.bass_utils import run_bass_kernel_spmd

    nc = bacc.Bacc("TRN2", target_bir_lowering=False, num_devices=1)
    arrays = {}

    def given(prefix, name, value):
        value = np.ascontiguousarray(value)
        arrays[prefix + name] = value
        return nc.dram_tensor(prefix + name, value.shape, mybir.dt.from_np(value.dtype), kind="ExternalInput").ap()
    a = {name: given("in_", name, inputs[name]) for name in _NAMES}
    c = {name: given("const_", name, value) for name, value in constant_arrays().items()}
    out = [nc.dram_tensor(f"out_{i}", shape, F32, kind="ExternalOutput").ap() for i, shape in enumerate(_OUTS)]
    build(nc, a, out, c)
    r = run_bass_kernel_spmd(nc, [arrays], core_ids=[0])
    return tuple(r.results[0][f"out_{i}"] for i in range(len(_OUTS)))
```
